# Optimizing a Trainium2 kernel written in Bass

```python
import math
import jax
import jax.numpy as jnp
from jax import lax
import numpy as np

D_MODEL = 1024
BATCH = 1
SEQ = 512
DEPTH = 2

GRID_W = 64
CTX_LEN = 256
N_MIXERS = 2
N_ATTN_LAYERS = (DEPTH + 1) // 2
N_GLA_LAYERS = DEPTH // 2

ALPHA = (2.0 * DEPTH) ** 0.25
BETA = (8.0 * DEPTH) ** -0.25
LN_EPS = 1e-5

DIFF_HEADS = 8
DIFF_HEAD_DIM = D_MODEL // DIFF_HEADS // 2
Q_BLOCK = 128
ROPE_BASE = 10000.0
ROT_FREQS = DIFF_HEAD_DIM // 4

GLA_HEADS = 4
GLA_DK = D_MODEL // 2 // GLA_HEADS
GLA_DV = D_MODEL // GLA_HEADS
GLA_GATE_RANK = 16
GLA_TAU = 16.0
GLA_CHUNK = 64

N_EXPERTS = 16
N_GROUPS = 4
EXPERTS_PER_GROUP = N_EXPERTS // N_GROUPS
TOP_K = 2
D_EXPERT = D_MODEL // 2
MOE_BLOCK = 128

kernel_name = 'hybrid_diffattn_gla_grouped_moe_prefix'

def layer_norm(x, g, b):
    xf = x.astype(jnp.float32)
    mu = jnp.mean(xf, axis=-1, keepdims=True)
    var = jnp.mean(jnp.square(xf - mu), axis=-1, keepdims=True)
    y = (xf - mu) * lax.rsqrt(var + LN_EPS) * g.astype(jnp.float32) + b.astype(jnp.float32)
    return y.astype(x.dtype)

def rms_norm(x, g):
    xf = x.astype(jnp.float32)
    y = xf * lax.rsqrt(jnp.mean(jnp.square(xf), axis=-1, keepdims=True) + LN_EPS) * g.astype(jnp.float32)
    return y.astype(x.dtype)

def modulate(h, shift, scale):
    return h * (1.0 + scale) + shift

def rope_2d_tables(rows, dtype):
    row = jnp.repeat(jnp.arange(rows, dtype=jnp.float32), GRID_W)
    col = jnp.tile(jnp.arange(GRID_W, dtype=jnp.float32), rows)
    inv_freq = ROPE_BASE ** (-jnp.arange(ROT_FREQS, dtype=jnp.float32) / ROT_FREQS)
    ang_r = row[:, None] * inv_freq
    ang_c = col[:, None] * inv_freq
    ang = jnp.concatenate([ang_r, ang_r, ang_c, ang_c], axis=-1)
    return jnp.cos(ang).astype(dtype), jnp.sin(ang).astype(dtype)

def apply_rope_2d(x, cos, sin):
    xr = x.reshape(x.shape[:-1] + (2, 2, ROT_FREQS))
    rot = jnp.concatenate([-xr[..., 1:, :], xr[..., :1, :]], axis=-2).reshape(x.shape)
    return x * cos[None, :, None, None, :] + rot * sin[None, :, None, None, :]

def diff_attention(h_lat, h_ctx, w_qkv, w_o, lam_vecs, subln_g, lambda_init, cos, sin, need_ctx):
    B, S, _ = h_lat.shape

    def project(h):
        T = h.shape[1]
        q, k, v = jnp.split(h @ w_qkv, 3, axis=-1)
        q = q.reshape(B, T, DIFF_HEADS, 2, DIFF_HEAD_DIM)
        k = k.reshape(B, T, DIFF_HEADS, 2, DIFF_HEAD_DIM)
        v = v.reshape(B, T, DIFF_HEADS, 2 * DIFF_HEAD_DIM)
        return q, k, v

    q_l, k_l, v_l = project(h_lat)
    q_l = apply_rope_2d(q_l, cos, sin)
    k_l = apply_rope_2d(k_l, cos, sin)
    q_c, k_c, v_c = project(h_ctx)

    lf = lam_vecs.astype(jnp.float32)
    lam = jnp.exp(jnp.sum(lf[0] * lf[1])) - jnp.exp(jnp.sum(lf[2] * lf[3])) + lambda_init
    scale = DIFF_HEAD_DIM ** -0.5

    def diff_softmax(q, k, v):
        s = jnp.einsum('bqhmd,bkhmd->bhmqk', q, k, preferred_element_type=jnp.float32) * scale
        p = jax.nn.softmax(s, axis=-1)
        a = p[:, :, 0] - lam * p[:, :, 1]
        return jnp.einsum('bhqk,bkhe->bqhe', a.astype(v.dtype), v)

    k_all = jnp.concatenate([k_c, k_l], axis=1)
    v_all = jnp.concatenate([v_c, v_l], axis=1)
    n_blocks = S // Q_BLOCK
    q_blocks = q_l.reshape(B, n_blocks, Q_BLOCK, DIFF_HEADS, 2, DIFF_HEAD_DIM).swapaxes(0, 1)
    o_l = lax.map(lambda qb: diff_softmax(qb, k_all, v_all), q_blocks)
    o_l = o_l.swapaxes(0, 1).reshape(B, S, DIFF_HEADS, 2 * DIFF_HEAD_DIM)

    def finish(o):
        o = rms_norm(o, subln_g) * (1.0 - lambda_init)
        return o.reshape(o.shape[0], o.shape[1], DIFF_HEADS * 2 * DIFF_HEAD_DIM) @ w_o

    y_lat = finish(o_l)
    y_ctx = finish(diff_softmax(q_c, k_c, v_c)) if need_ctx else None
    return y_lat, y_ctx

def gla_chunked(q, k, v, g, h0):
    B, H, T, DK = q.shape
    DV = v.shape[-1]
    n_chunks = T // GLA_CHUNK

    def to_chunks(a):
        return a.astype(jnp.float32).reshape(B, H, n_chunks, GLA_CHUNK, a.shape[-1]).transpose(2, 0, 1, 3, 4)

    lower_tri = jnp.tril(jnp.ones((GLA_CHUNK, GLA_CHUNK), dtype=bool))[None, None, :, :, None]

    def chunk_step(state, inp):
        qb, kb, vb, gb = inp
        b = jnp.cumsum(gb, axis=2)
        rel = jnp.where(lower_tri, b[:, :, :, None, :] - b[:, :, None, :, :], -jnp.inf)
        scores = jnp.einsum('bhtd,bhsd,bhtsd->bhts', qb, kb, jnp.exp(rel))
        o = jnp.einsum('bhts,bhsv->bhtv', scores, vb) + jnp.einsum('bhtd,bhdv->bhtv', qb * jnp.exp(b), state)
        b_last = b[:, :, -1:, :]
        state = jnp.exp(b_last[:, :, 0, :, None]) * state + jnp.einsum('bhsd,bhsv->bhdv', kb * jnp.exp(b_last - b), vb)
        return state, o

    state, o = lax.scan(chunk_step, h0, (to_chunks(q), to_chunks(k), to_chunks(v), to_chunks(g)))
    o = o.transpose(1, 2, 0, 3, 4).reshape(B, H, T, DV)
    return o.astype(v.dtype), state

def gla_mixer(h_lat, h_ctx, w_in, wg_down, wg_up, bg, norm_g, w_o, need_ctx):
    B = h_lat.shape[0]
    dk_tot = GLA_HEADS * GLA_DK
    dv_tot = GLA_HEADS * GLA_DV

    def heads(a, dh):
        return a.reshape(B, a.shape[1], GLA_HEADS, dh).transpose(0, 2, 1, 3)

    def project(h):
        q, k, v, r = jnp.split(h @ w_in, [dk_tot, 2 * dk_tot, 2 * dk_tot + dv_tot], axis=-1)
        gates = [heads(jax.nn.log_sigmoid(((h @ wg_down[d]) @ wg_up[d] + bg[d]).astype(jnp.float32)) / GLA_TAU, GLA_DK)
                 for d in range(2)]
        return heads(q, GLA_DK) * (GLA_DK ** -0.5), heads(k, GLA_DK), heads(v, GLA_DV), r, gates[0], gates[1]

    q_l, k_l, v_l, r_l, gf_l, gb_l = project(h_lat)
    q_c, k_c, v_c, r_c, gf_c, gb_c = project(h_ctx)
    h0 = jnp.zeros((B, GLA_HEADS, GLA_DK, GLA_DV), jnp.float32)

    def flip(a):
        return jnp.flip(a, axis=2)

    o_cf, s_f = gla_chunked(q_c, k_c, v_c, gf_c, h0)
    o_cb, s_b = gla_chunked(flip(q_c), flip(k_c), flip(v_c), flip(gb_c), h0)
    o_lf, _ = gla_chunked(q_l, k_l, v_l, gf_l, s_f)
    o_lb, _ = gla_chunked(flip(q_l), flip(k_l), flip(v_l), flip(gb_l), s_b)

    def finish(o, r):
        T = o.shape[2]
        o = rms_norm(o.transpose(0, 2, 1, 3), norm_g).reshape(B, T, dv_tot)
        return (o * jax.nn.silu(r)) @ w_o

    y_lat = finish(o_lf + flip(o_lb), r_l)
    y_ctx = finish(o_cf + flip(o_cb), r_c) if need_ctx else None
    return y_lat, y_ctx

def grouped_top2_moe(h, router_w, router_b, w_gate, w_up, w_down):
    T, D = h.shape
    logits = jnp.einsum('td,de->te', h, router_w, preferred_element_type=jnp.float32)
    affinity = jax.nn.sigmoid(logits)
    select = (affinity + router_b.astype(jnp.float32)).reshape(T, N_GROUPS, EXPERTS_PER_GROUP)
    group_score = jnp.sum(lax.top_k(select, TOP_K)[0], axis=-1)
    group = jnp.argmax(group_score, axis=-1)
    in_group = select[jnp.arange(T), group]
    _, local = lax.top_k(in_group, TOP_K)
    expert = group[:, None] * EXPERTS_PER_GROUP + local
    weight = jnp.take_along_axis(affinity, expert, axis=-1)
    weight = weight / jnp.sum(weight, axis=-1, keepdims=True)

    n_assign = T * TOP_K
    flat_e = expert.reshape(-1)
    flat_w = weight.reshape(-1)
    flat_t = jnp.repeat(jnp.arange(T, dtype=jnp.int32), TOP_K)
    order = jnp.argsort(flat_e)
    se, st, sw = flat_e[order], flat_t[order], flat_w[order]
    counts = jnp.bincount(flat_e, length=N_EXPERTS)
    padded = (counts + MOE_BLOCK - 1) // MOE_BLOCK * MOE_BLOCK
    seg_start = jnp.cumsum(counts) - counts
    pad_end = jnp.cumsum(padded)
    pad_start = pad_end - padded
    dest = pad_start[se] + jnp.arange(n_assign) - seg_start[se]
    n_pad = n_assign + N_EXPERTS * MOE_BLOCK
    n_blocks = n_pad // MOE_BLOCK
    x_pad = jnp.zeros((n_pad, D), h.dtype).at[dest].set(h[st])
    tok_pad = jnp.full((n_pad,), T, jnp.int32).at[dest].set(st)
    w_pad = jnp.zeros((n_pad,), jnp.float32).at[dest].set(sw)
    block_expert = jnp.minimum(jnp.searchsorted(pad_end, jnp.arange(n_blocks) * MOE_BLOCK, side='right'), N_EXPERTS - 1)

    def expert_block(args):
        xb, e = args
        return (jax.nn.silu(xb @ w_gate[e]) * (xb @ w_up[e])) @ w_down[e]

    y_pad = lax.map(expert_block, (x_pad.reshape(n_blocks, MOE_BLOCK, D), block_expert)).reshape(n_pad, D)
    out = jnp.zeros((T + 1, D), h.dtype).at[tok_pad].add(y_pad * w_pad[:, None].astype(h.dtype))
    return out[:T]

def setup_inputs(seed: int = 0) -> dict:
    key = jax.random.key(seed)
    ks = jax.random.split(key, 24)

    def nrm(k, shape, scale):
        return jax.random.normal(k, shape, jnp.float32) * scale

    dk_tot = GLA_HEADS * GLA_DK
    dv_tot = GLA_HEADS * GLA_DV
    return {
        'x': nrm(ks[0], (BATCH, SEQ, D_MODEL), 1.0),
        'c': nrm(ks[1], (BATCH, D_MODEL), 1.0),
        'ctx': nrm(ks[2], (BATCH, CTX_LEN, D_MODEL), 1.0),
        'c_ctx': nrm(ks[3], (D_MODEL,), 1.0),
        'ada_w': nrm(ks[4], (DEPTH, D_MODEL, 6 * D_MODEL), D_MODEL ** -0.5),
        'ada_b': nrm(ks[5], (DEPTH, 6 * D_MODEL), 0.02),
        'ln_g': 1.0 + nrm(ks[6], (DEPTH, 2, D_MODEL), 0.02),
        'ln_b': nrm(ks[7], (DEPTH, 2, D_MODEL), 0.02),
        'attn_w_qkv': nrm(ks[8], (N_ATTN_LAYERS, D_MODEL, 3 * D_MODEL), D_MODEL ** -0.5),
        'attn_w_o': nrm(ks[9], (N_ATTN_LAYERS, D_MODEL, D_MODEL), BETA * D_MODEL ** -0.5),
        'attn_lambda': nrm(ks[10], (N_ATTN_LAYERS, 4, DIFF_HEAD_DIM), 0.1),
        'attn_subln_g': 1.0 + nrm(ks[11], (N_ATTN_LAYERS, 2 * DIFF_HEAD_DIM), 0.02),
        'gla_w_in': nrm(ks[12], (N_GLA_LAYERS, D_MODEL, 2 * dk_tot + 2 * dv_tot), D_MODEL ** -0.5),
        'gla_wg_down': nrm(ks[13], (N_GLA_LAYERS, 2, D_MODEL, GLA_GATE_RANK), D_MODEL ** -0.5),
        'gla_wg_up': nrm(ks[14], (N_GLA_LAYERS, 2, GLA_GATE_RANK, dk_tot), GLA_GATE_RANK ** -0.5),
        'gla_bg': nrm(ks[15], (N_GLA_LAYERS, 2, dk_tot), 0.1),
        'gla_norm_g': 1.0 + nrm(ks[16], (N_GLA_LAYERS, GLA_DV), 0.02),
        'gla_w_o': nrm(ks[17], (N_GLA_LAYERS, dv_tot, D_MODEL), BETA * dv_tot ** -0.5),
        'router_w': nrm(ks[18], (D_MODEL, N_EXPERTS), D_MODEL ** -0.5),
        'router_b': nrm(ks[19], (N_EXPERTS,), 0.01),
        'moe_w_gate': nrm(ks[20], (DEPTH, N_EXPERTS, D_MODEL, D_EXPERT), D_MODEL ** -0.5),
        'moe_w_up': nrm(ks[21], (DEPTH, N_EXPERTS, D_MODEL, D_EXPERT), D_MODEL ** -0.5),
        'moe_w_down': nrm(ks[22], (DEPTH, N_EXPERTS, D_EXPERT, D_MODEL), BETA * D_EXPERT ** -0.5),
    }

def reference(x, c, ctx, c_ctx, ada_w, ada_b, ln_g, ln_b, attn_w_qkv, attn_w_o, attn_lambda, attn_subln_g,
              gla_w_in, gla_wg_down, gla_wg_up, gla_bg, gla_norm_g, gla_w_o, router_w, router_b,
              moe_w_gate, moe_w_up, moe_w_down):
    B, S, D = x.shape
    C = ctx.shape[1]
    ROWS = S // GRID_W
    cos, sin = rope_2d_tables(ROWS, x.dtype)
    silu_c = jax.nn.silu(c)
    silu_cc = jax.nn.silu(c_ctx)

    for i in range(DEPTH):
        need_ctx = i < DEPTH - 1
        mod = (silu_c @ ada_w[i] + ada_b[i])[:, None, :]
        mod_c = silu_cc @ ada_w[i] + ada_b[i]
        sh_m, sc_m, g_m, sh_f, sc_f, g_f = jnp.split(mod, 6, axis=-1)
        csh_m, csc_m, cg_m, csh_f, csc_f, cg_f = jnp.split(mod_c, 6, axis=-1)

        h_lat = modulate(x, sh_m, sc_m)
        h_ctx = modulate(ctx, csh_m, csc_m)
        j = i // N_MIXERS
        if i % N_MIXERS == 0:
            y_lat, y_ctx = diff_attention(h_lat, h_ctx, attn_w_qkv[j], attn_w_o[j], attn_lambda[j], attn_subln_g[j],
                                          0.8 - 0.6 * math.exp(-0.3 * i), cos, sin, need_ctx)
        else:
            y_lat, y_ctx = gla_mixer(h_lat, h_ctx, gla_w_in[j], gla_wg_down[j], gla_wg_up[j], gla_bg[j],
                                     gla_norm_g[j], gla_w_o[j], need_ctx)
        x = layer_norm(ALPHA * x + g_m * y_lat, ln_g[i, 0], ln_b[i, 0])
        if need_ctx:
            ctx = layer_norm(ALPHA * ctx + cg_m * y_ctx, ln_g[i, 0], ln_b[i, 0])

        tokens = modulate(x, sh_f, sc_f).reshape(B * S, D)
        if need_ctx:
            tokens = jnp.concatenate([tokens, modulate(ctx, csh_f, csc_f).reshape(B * C, D)], axis=0)
        y = grouped_top2_moe(tokens, router_w, router_b, moe_w_gate[i], moe_w_up[i], moe_w_down[i])
        x = layer_norm(ALPHA * x + g_f * y[:B * S].reshape(B, S, D), ln_g[i, 1], ln_b[i, 1])
        if need_ctx:
            ctx = layer_norm(ALPHA * ctx + cg_f * y[B * S:].reshape(B, C, D), ln_g[i, 1], ln_b[i, 1])
    return x


_drawn_inputs = setup_inputs


def setup_inputs(seed=0):
    import zlib

    import numpy as np

    out = dict(_drawn_inputs(seed))
    spreads = {}
    factors = {'attn_subln_g': 4.037, 'gla_bg': 2.956, 'gla_norm_g': 5.367}
    for name, (base, spread) in spreads.items():
        noise = np.random.default_rng([zlib.crc32(name.encode()), seed]).standard_normal(out[name].shape)
        drawn = base * np.exp(spread * noise) if base else spread * noise
        out[name] = jnp.asarray(drawn.astype(out[name].dtype))
    for name, factor in factors.items():
        out[name] = (out[name] * factor).astype(out[name].dtype)
    return out
```

```python
from contextlib import ExitStack
import math

import numpy as np
import concourse.bass as bass
from concourse import mybir

ALU = mybir.AluOpType
ACT = mybir.ActivationFunctionType
F32 = mybir.dt.float32
I32 = mybir.dt.int32
AX = mybir.AxisListType

P = 128
D = 1024
KC = D // P
SEQ, CTX = 512, 256
TOK = SEQ + CTX
LT, CT = SEQ // P, CTX // P
NT = LT + CT
ALPHA = 4.0 ** 0.25
EPS = 1e-5
HEADS, HD = 8, 64
GRID_W, ROT = 64, HD // 4
GH, DK, DV = 4, 128, 256
RANK = 16
TAU = 16.0
NE, NG, EPG = 16, 4, 4
FE = D // 2
LAMBDA0 = 0.8 - 0.6 * math.exp(0.0)
SLOT = 4096
RING = 6
MAXB = [(TOK * 2 + NE * (P - 1)) // P, (SEQ * 2 + NE * (P - 1)) // P]
NBMAX = TOK // P
TILES = [NT, LT]

STREAM = [("ada", 0, j) for j in range(4)]
STREAM += [("qkv", 0, 2 * part + hg) for hg in range(2) for part in range(3)]
STREAM += [("ada", 0, j) for j in range(4, 10)]
STREAM += [("wo", 0, 0), ("wo", 0, 1)]
STREAM += [("ada", 0, 10), ("ada", 0, 11)]
STREAM += [("ada", 1, j) for j in range(12)]
MOE0 = len(STREAM)
STREAM += [("moe", 0, i) for i in range(3 * NE)]
GLA0 = len(STREAM)
STREAM += [("gla", 1, j) for j in range(6)]
STREAM += [("wo", 1, 0), ("wo", 1, 1)]
MOE1 = len(STREAM)
STREAM += [("moe", 1, i) for i in range(3 * NE)]
MOEBASE = [MOE0, MOE1]
ADA_ITEMS = [p for p, it in enumerate(STREAM) if it[0] == "ada"]
PLAIN = [p for p, it in enumerate(STREAM) if it[0] != "moe"]


LAYER0_COUNTS = {
    "on_rdy": 6,
    "turn_mm": 12,
    "turn_ev": 12,
    "turn_use": 12,
    "y_mm": 6,
    "z_done": 6,
    "bn": 6,
    "ln_sqrt": 6,
    "ln_n": 6,
    "hf_rdy": 6,
    "aff": 1,
    "y_all": 1,
    "scat": 192,
    "slot_ld": 16,
    "mask": 1,
    "rank_mm": 1,
    "xfin": 6,
    "z2_done": 6,
    "bn2": 6,
    "ln2_sqrt": 6,
    "ln2_n": 6,
    "rows_ld": 16,
    "rows2_ld": 64,
    "rows3_ld": 64,
    "lgk": 64,
    "hf_st0": 48,
    "hf_st1": 48,
    "ya_ld0": 96,
    "ya_ld1": 96,
}


def after(l, name, v):
    return v + (LAYER0_COUNTS[name] if l else 0)


def constants():
    ident = np.eye(P, dtype=np.float32)
    rot = np.zeros((P, P), np.float32)
    for d in range(P):
        half = (d // ROT) % 2
        if half == 0:
            rot[d + ROT, d] = -1.0
        else:
            rot[d - ROT, d] = 1.0
    tri = np.triu(np.ones((P, P), np.float32), 1)
    ones = np.ones((P, P), np.float32)
    pos = np.arange(SEQ)
    inv = 10000.0 ** (-np.arange(ROT, dtype=np.float32) / ROT)
    inv = inv.astype(np.float32)
    ang_r = (pos // GRID_W).astype(np.float32)[:, None] * inv
    ang_c = (pos % GRID_W).astype(np.float32)[:, None] * inv
    ang = np.concatenate([ang_r, ang_r, ang_c, ang_c], -1)
    ang = np.concatenate([ang, ang], -1).T
    cs = np.stack([np.cos(ang), np.sin(ang)], 1).astype(np.float32).reshape(P, 2 * SEQ)
    i = np.arange(P)
    masks = [2.0 * ident]
    for lv in range(7):
        masks.append((((i[:, None] ^ i[None, :]) >> lv) == 1).astype(np.float32))
    masks = np.stack(masks, 1).reshape(P, 8 * P).astype(np.float32)
    row = np.zeros((P, 64), np.float32)
    row[:, 0:NBMAX] = np.arange(NBMAX) * P
    row[:, 8:8 + 28] = np.arange(28)
    row[:, 40:56] = np.where(np.arange(16) % 2 == 0, 1.0, -1.0)
    row[:, 56:56 + NT] = np.arange(NT)[None, :] * P + i[:, None]
    return np.concatenate([ident, rot, tri, ones, row, cs, masks], 1).astype(np.float32)


OFF = [(0, 1), (2, 3), (0, 2), (0, 3), (1, 2), (1, 3), (1, 0), (3, 2), (2, 0), (2, 1), (3, 0), (3, 1)]
NCONST = 4 * P + 64 + 2 * SEQ + 8 * P


def build(nc, a, out, consts, dumps=None):
    dumps = dumps or {}
    stack = ExitStack()
    with stack:
        def sb(name, cols, dt=F32, parts=P):
            return stack.enter_context(nc.sbuf_tensor(name, [parts, cols], dt))

        def sem(name):
            return stack.enter_context(nc.semaphore(name))

        def dram(name, shape, dt=F32):
            return nc.dram_tensor(name, shape, dt, kind="Internal").ap()

        ring = sb("ring", RING * SLOT)
        A0, A1, A2, A3 = (sb(f"arena{i}", NT * D) for i in range(4))
        cst = sb("cst", 4 * P + 64)
        cs = sb("cos_sin_or_masks", 8 * P)
        U = sb("union_small", 1792)
        sm = sb("small", 336)
        idx32 = sb("idx32", 192, I32)
        bank = [stack.enter_context(nc.psum_tensor(f"bank{i}", [P, 512], F32)) for i in range(8)]

        ident, rot, tri, ones = (cst[:, i * P:(i + 1) * P] for i in range(4))
        rowc = cst[:, 4 * P:4 * P + 64]
        kmul, jrow, sgn, tidf = rowc[:, 0:NBMAX], rowc[:, 8:36], rowc[:, 40:56], rowc[:, 56:56 + NT]

        modd = dram("mod_rows", [2, 2, 6 * D])
        hfd = [dram(f"ffn_in{l}", [TILES[l] * P, D]) for l in range(2)]
        ypad = [dram(f"expert_out{l}", [(MAXB[l] + 2) * P, D]) for l in range(2)]
        tokd = [dram(f"slot_token{l}", [P * 28, 1], I32) for l in range(2)]
        xsave = dram("x_between_layers", [SEQ, D])

        cur = [0]

        def take(n):
            cur[0] += n
            return sm[:, cur[0] - n:cur[0]]

        c_raw, c_act = take(16), take(16)
        modc = [take(32) for _ in range(2)]
        st_a = [take(16) for _ in range(2)]
        lam4, nlam = take(4), take(1)
        ss = take(48)
        rstd = take(48)
        bst, mv, sd = take(12), take(2), take(2)
        W2 = take(12)
        bgc = take(8)
        epst = take(1)
        rb = take(16)
        bstot, etot = take(24), take(12)
        routed = [idx32[:, 0:12], idx32[:, 12:24]]
        destI, addrI = routed
        tidI = idx32[:, 24:30]
        idxcur = idx32[:, 30:31]
        zeroI = idx32[:, 31:32]
        slotI = idx32[:, 32:60]
        inclI = idx32[:, 60:76]
        peI = idx32[:, 76:160]
        countI = idx32[:, 188:190]
        zfill = idx32[:, 160:188]

        def slot(p):
            s = p % RING
            return ring[:, s * SLOT:(s + 1) * SLOT]

        ring_ld = [sem(f"ring_loaded{i}") for i in range(RING)]
        ring_used = sem("ring_used")
        const_ld, x_ld, silu_c = sem("const_loaded"), sem("x_loaded"), sem("silu_c_done")
        ada_row = sem("ada_row_ready")
        adab_ld = [sem(f"ada_bias_loaded{i}") for i in range(2)]
        ada_st = [sem(f"ada_row_stored{i}") for i in range(2)]
        modc_ld = [sem(f"mod_cols_loaded{l}") for l in range(2)]
        xt_mm = [sem(f"x_transposed{l}") for l in range(2)]
        ht_l = [sem(f"h_latent_ready{l}") for l in range(2)]
        ht_c = [sem(f"h_context_ready{l}") for l in range(2)]
        S = {}
        for n in ("proj_mm", "qraw", "rot_mm", "rope_cos", "rope_done", "ctx_ev", "v_mm", "v_ev",
                  "sc_mm", "sc_half", "maxed", "exped", "pmix", "at_mm", "at_ev_lo", "at_ev_hi", "o_mm", "o_ev",
                  "lam_ld", "lam_a", "lam_b", "rms_sqrt", "dve", "act", "pool",
                  "cs_ld", "xres_ld", "routerw_ld",
                  "gq_mm", "gq_ev", "gk_mm", "gk_ev", "gv_mm", "gv_ev", "gd_mm", "gd_ev", "gr_ev",
                  "gw_ld", "gu_mm", "ls_exp", "ls_done", "lv_arg", "lv_exp", "lv_mul", "lv_mm", "lv_ev",
                  "tl_exp", "tl_done", "kc_exp", "kc_done", "kc_mm", "kc_ev", "st_mm", "st_ev", "off_mm", "off_ev", "go_mm", "go_ev",
                  "gss", "wz", "pool_ld", "passed", "bg_ld", "xsave_st", "mask_ld", "init", "outst"):
            S[n] = sem(n)
        L = [{n: sem(n) for n in LAYER0_COUNTS}]
        L.append(dict(L[0]))
        for l in range(2):
            L[l].update({n: sem(f"{n}{l}") for n in (
                "tbl", "tok_zero", "idx", "gath",
                "xt", "xt_a", "xt_v", "g_mm", "u_mm", "silu", "gmul", "gt_mm", "gt_ev", "yd_mm", "y_a", "y_v", "y_st", "yfill")})
        block = stack.enter_context(nc.Block())

        hT = A0[:, :].rearrange("p (c t) -> p c t", c=KC)
        xst = A1[:, :].rearrange("p (t n) -> p t n", t=NT)
        X = [A2[:, :].rearrange("p (t n) -> p t n", t=NT), A1[:, :].rearrange("p (t n) -> p t n", t=NT)]
        qT = A2[:, 0:4 * TOK].rearrange("p (h t) -> p h t", h=4)
        kT = A2[:, 4 * TOK:8 * TOK].rearrange("p (h t) -> p h t", h=4)
        vA = A3[:, 0:NT * 512].rearrange("p (t n) -> p t n", t=NT)
        PR = [A3[:, NT * 512 + i * 2 * TOK:NT * 512 + (i + 1) * 2 * TOK].rearrange("p (m k) -> p m k", m=2) for i in range(2)]
        qraw = [A3[:, NT * 512 + i * 512:NT * 512 + (i + 1) * 512] for i in range(2)]
        rtmp = A3[:, NT * 512 + 1024:NT * 512 + 1536]
        aT = [U[:, i * TOK:(i + 1) * TOK].rearrange("p (k q) -> p k q", k=NT) for i in range(2)]
        oall = A1[:, :].rearrange("p (t n) -> p t n", t=NT)
        adat = [A3[0:2, 4096 + i * 512:4096 + (i + 1) * 512] for i in range(2)]
        adab = [A3[0:2, 5120 + i * 512:5120 + (i + 1) * 512] for i in range(2)]
        oT = [A0[:, i * D:(i + 1) * D].rearrange("p (c t) -> p c t", c=KC) for i in range(2)]
        HF = [A0[:, (2 + i) * D:(3 + i) * D] for i in range(2)]
        scf, shf = A0[:, 4 * D:5 * D], A0[:, 5 * D:6 * D]
        gm, lng, lnb, Z = (A3[:, i * D:(i + 1) * D] for i in range(4))
        lamv = A3[:, 0:4 * HD]
        RT = A1[:, 4096:6144]
        xrow = A0[:, 0:D]
        xT = A0[:, D:2 * D].rearrange("p (c t) -> p c t", c=KC)
        gsil, gate = A0[:, 2 * D:2 * D + FE], A0[:, 2 * D + FE:3 * D]
        gT = A0[:, 3 * D:3 * D + FE].rearrange("p (c t) -> p c t", c=4)
        ysb = A0[:, 4 * D:5 * D]
        YB = [A1, A2]
        yab = [[YB[l][:, (2 * i + k) * D:(2 * i + k + 1) * D] for i in range(2) for k in range(2)] for l in range(2)]
        normg = [U[:, 256:256 + P], U[:, 256:256 + DV]]
        rwt = U[:, 0:128].rearrange("p (c n) -> p c n", c=KC)
        V1 = A1[:, :].rearrange("p (t n) -> p t n", t=NT)
        R1 = A2[:, 0:LT * D].rearrange("p (t n) -> p t n", t=LT)
        TL = A2[:, 4096:6144].rearrange("p (k t) -> p k t", k=4)
        QK = A3[:, 0:4096].rearrange("p (h k t) -> p h k t", h=GH, k=2)
        KX = A3[:, 4096:5120].rearrange("p (h t) -> p h t", h=GH)
        ST = A3[:, 5120:5632].rearrange("p (d e) -> p d e", d=2)
        KXT = A3[:, 5632:6144].rearrange("p (d t e) -> p d t e", d=2, t=2)
        GB = A0[:, 0:2 * TOK].rearrange("p (d t) -> p d t", d=2)
        LVB = [A0[:, 1536 + i * 1024:1536 + (i + 1) * 1024].rearrange("p (k t) -> p k t", k=2) for i in range(2)]
        LS = A0[:, 1536:3072].rearrange("p (d t) -> p d t", d=2)
        SO = A0[:, 1536:3072].rearrange("p (k t) -> p k t", k=12)
        VAR = A0[:, 3584:4864].rearrange("p (k t) -> p k t", k=10)
        SD = A0[:, 4864:5376].rearrange("p (b t) -> p b t", b=4)
        KXG = A0[:, 5376:5888].rearrange("p (d t) -> p d t", d=2)
        gdT = U[:, 0:TOK]
        wup = U[:, TOK:TOK + 512]
        wdn = U[:, TOK + 512:TOK + 1024].rearrange("p (c r) -> p c r", c=KC)
        cosT, sinT = cs[:, 0:SEQ], cs[:, SEQ:2 * SEQ]
        maskv = cs[:, :].rearrange("p (k t) -> p k t", k=8)

        def bcast_row(ap_1d, n):
            return ap_1d.unsqueeze(0).to_broadcast([P, n])

        def src_of(p):
            kind, l, j = STREAM[p]
            if kind == "ada":
                return a["ada_w"][l].rearrange("(p c) n -> p c n", c=KC)[:, :, j * 512:(j + 1) * 512]
            if kind == "qkv":
                return a["attn_w_qkv"][0].rearrange("(p c) n -> p c n", c=KC)[:, :, j * 512:(j + 1) * 512]
            if kind == "gla":
                return a["gla_w_in"][0].rearrange("(p c) n -> p c n", c=KC)[:, :, j * 512:(j + 1) * 512]
            w = a["attn_w_o"][0] if l == 0 else a["gla_w_o"][0]
            return w.rearrange("(p c) n -> p c n", c=KC)[:, :, j * 512:(j + 1) * 512]

        def used_value(p):
            return PLAIN.index(p) + 1

        def attn_units():
            return [(hb, t) for hb in range(4) for t in range(NT)]

        def turns(l):
            n, q = TILES[l], []
            for t in range(n):
                q.append(("o", t))
                if t >= 2:
                    q.append(("r", t - 2))
            return q + [("r", n - 2), ("r", n - 1)]

        @block.sync
        def _(sp):
            sp.dma_start(cst[:, :], consts[:, 0:4 * P + 64]).then_inc(const_ld, 16)
            sp.dma_start(c_raw[:, 0:8], a["c"][0].rearrange("(p c) -> p c", c=KC)).then_inc(const_ld, 16)
            sp.dma_start(c_raw[:, 8:16], a["c_ctx"].rearrange("(p c) -> p c", c=KC)).then_inc(const_ld, 16)

            def load_bias(n):
                _, l, j = STREAM[ADA_ITEMS[n]]
                if n >= 2:
                    sp.wait_ge(ada_row, n - 1)
                sp.dma_start(adab[n % 2], a["ada_b"][l][j * 512:(j + 1) * 512].unsqueeze(0).to_broadcast([2, 512])
                             ).then_inc(adab_ld[n % 2], 16)

            def store_row(n):
                _, l, j = STREAM[ADA_ITEMS[n]]
                sp.wait_ge(ada_row, n + 1)
                sp.dma_start(modd[l][:, j * 512:(j + 1) * 512], adat[n % 2]).then_inc(ada_st[n % 2], 16)

            def issue(p):
                if p >= RING:
                    q = p - RING
                    kind, l, j = STREAM[q]
                    if kind == "moe":
                        e = j // 3
                        if j % 3 == 0:
                            v = sp.value_load(inclI[0:1, e:e + 1], min_val=1, max_val=64)
                            sp.wait_ge(L[l]["yd_mm"], v)
                    else:
                        sp.wait_ge(ring_used, used_value(q))
                        if kind == "ada":
                            n = ADA_ITEMS.index(q)
                            store_row(n)
                            if n >= 4 or n < 2:
                                load_bias(n + 2)
                sp.dma_start(slot(p), src_of(p) if STREAM[p][0] != "moe" else None).then_inc(ring_ld[p % RING], 16)

            def issue_expert(l, e_static, e):
                p = MOEBASE[l] + 3 * e_static
                gw = a["moe_w_gate"][l].rearrange("e (p c) n -> p e (c n)", c=KC)
                uw = a["moe_w_up"][l].rearrange("e (p c) n -> p e (c n)", c=KC)
                dw = a["moe_w_down"][l].rearrange("e (p c) n -> p e (c n)", c=4)
                for i, w in enumerate((gw, uw, dw)):
                    src = w[:, bass.ds(e, 1), :].rearrange("p e n -> p (e n)")
                    sp.dma_start(slot(p + i), src).then_inc(ring_ld[(p + i) % RING], 16)

            load_bias(0)
            load_bias(1)
            for p in range(RING):
                issue(p)
                if p == 1:
                    for t in range(NT):
                        src = a["x"][0][t * P:(t + 1) * P, :] if t < LT else a["ctx"][0][(t - LT) * P:(t - LT + 1) * P, :]
                        sp.dma_start(xst[:, t, :], src).then_inc(x_ld, 16)
                    sp.dma_start(cs[:, :], consts[:, 4 * P + 64:4 * P + 64 + 2 * SEQ]).then_inc(S["cs_ld"], 16)
            for l in range(2):
                for p in range(RING if l == 0 else GLA0, MOEBASE[l]):
                    issue(p)
                    if p == ADA_ITEMS[4] + RING - 1:
                        sp.wait_ge(S["o_ev"], 48)
                        load_bias(4)
                        load_bias(5)
                    if p == GLA0:
                        sp.wait_ge(S["rope_done"], 16)
                        sp.dma_start(cs[:, :], consts[:, 4 * P + 64 + 2 * SEQ:NCONST]).then_inc(S["mask_ld"], 16)
                for e in range(2):
                    for i in range(3):
                        q = MOEBASE[l] + 3 * e + i - RING
                        sp.wait_ge(ring_used, used_value(q))
                        if STREAM[q][0] == "ada":
                            n = ADA_ITEMS.index(q)
                            store_row(n)
                            if n + 2 < len(ADA_ITEMS):
                                load_bias(n + 2)
                    issue_expert(l, e, e)
                sp.wait_ge(L[l]["tbl"], 1)
                with sp.Fori(1, NE // 2) as m:
                    for par in range(2):
                        v = sp.value_load(inclI[0:1, bass.ds(2 * m - 2 + par, 1)], min_val=1, max_val=64)
                        sp.wait_ge(L[l]["yd_mm"], v)
                        issue_expert(l, 2 + par, 2 * m + par)

        @block.tensor
        def _(pe):
            def ring_wait(p):
                pe.wait_ge(ring_ld[p % RING], 16 * (p // RING + 1))

            def ada(n):
                p = ADA_ITEMS[n]
                w = slot(p).rearrange("p (c n) -> p c n", c=KC)
                ring_wait(p)
                if n == 0:
                    pe.wait_ge(silu_c, 1)
                else:
                    pe.wait_ge(ada_row, n)
                cw = c_act.rearrange("p (s c) -> p c s", s=2)
                for c in range(KC):
                    mm = pe.matmul(bank[7][0:2, :], cw[:, c, :], w[:, c, :], start=(c == 0), stop=(c == KC - 1))
                mm.then_inc(ring_used, 1)

            def transpose_x(l):
                nl = X[0] if l else xst
                for c in range(KC):
                    if c >= 3:
                        pe.wait_ge(ht_l[l], c - 2)
                        pe.wait_ge(ht_c[l], c - 2)
                    for t in range(NT):
                        b = bank[c % 3] if t < LT else bank[3 + c % 3]
                        o = (t % LT) * P
                        mm = pe.transpose(b[:, o:o + P], nl[:, t, :].rearrange("p (q c) -> p c q", c=KC)[:, c, :], ident)
                    mm.then_inc(xt_mm[l], 1)

            pe.wait_ge(const_ld, 48)
            for n in range(4):
                ada(n)
            pe.wait_ge(x_ld, 16 * NT)
            transpose_x(0)
            pe.wait_ge(ht_l[0], KC)
            pe.wait_ge(ht_c[0], KC)

            k_blk = 0
            for hg in range(2):
                base = 4 + 3 * hg
                if hg:
                    pe.wait_ge(S["o_ev"], NT * 4 * hg)

                def rotate(i):
                    pe.wait_ge(S["qraw"], i + 1)
                    if i >= 2:
                        pe.wait_ge(S["rope_done"], i - 1)
                    pe.matmul(bank[4 + i % 2][:, :], rot, qraw[i % 2], start=True, stop=True).then_inc(S["rot_mm"], 1)

                for part in range(2):
                    p = base + part
                    ring_wait(p)
                    w = slot(p).rearrange("p (c n) -> p c n", c=KC)
                    for hb in range(4):
                        i = 8 * hg + 4 * part + hb
                        if i >= 2:
                            pe.wait_ge(S["qraw"], i - 1)
                            pe.wait_ge(S["ctx_ev"], i - 1)
                        for c in range(KC):
                            pe.matmul(bank[i % 2][:, :], w[:, c, hb * P:(hb + 1) * P], hT[:, c, 0:SEQ],
                                      start=(c == 0), stop=(c == KC - 1))
                        for c in range(KC):
                            mm = pe.matmul(bank[2 + i % 2][:, 0:CTX], w[:, c, hb * P:(hb + 1) * P], hT[:, c, SEQ:TOK],
                                           start=(c == 0), stop=(c == KC - 1))
                        mm.then_inc(S["proj_mm"], 1)
                        if i % 8:
                            rotate(i - 1)
                    pe.wait_ge(S["proj_mm"], 8 * hg + 4 * part + 4)
                    pe.sem_inc(ring_used, 1)
                rotate(8 * hg + 7)
                p = base + 2
                ring_wait(p)
                w = slot(p).rearrange("p (c n) -> p c n", c=KC)
                for t in range(NT):
                    n = NT * hg + t
                    if t >= 2:
                        pe.wait_ge(S["v_ev"], n - 1)
                    for c in range(KC):
                        mm = pe.matmul(bank[6 + t % 2][:, :], hT[:, c, t * P:(t + 1) * P], w[:, c, :],
                                       start=(c == 0), stop=(c == KC - 1))
                    mm.then_inc(S["v_mm"], 1)
                pe.wait_ge(S["v_mm"], NT * (hg + 1))
                pe.sem_inc(ring_used, 1)

                units = attn_units()
                u0 = len(units) * hg
                pe.wait_ge(S["rope_done"], 8 * (hg + 1))
                pe.wait_ge(S["ctx_ev"], 8 * (hg + 1))
                pe.wait_ge(S["v_ev"], NT * (hg + 1))

                def scores(k):
                    hb, t = units[k]
                    u = u0 + k
                    b0, b1, b2 = (bank[3 * (k % 2) + j] for j in range(3))
                    if k >= 2:
                        pe.wait_ge(S["exped"], u - 1)
                    q = [qT[64 * m:64 * m + 64, hb, t * P:(t + 1) * P] for m in range(2)]
                    kl = [kT[64 * m:64 * m + 64, hb, 0:SEQ] for m in range(2)]
                    kc = [kT[64 * m:64 * m + 64, hb, SEQ:TOK] for m in range(2)]
                    if t < LT:
                        pe.matmul(b2[:, 0:CTX], q[0], kc[0], start=True, stop=True).then_inc(S["sc_half"], 1)
                        pe.matmul(b0[:, :], q[0], kl[0], start=True, stop=True)
                        pe.matmul(b1[:, :], q[1], kl[1], start=True, stop=True)
                        pe.wait_ge(S["sc_half"], LT * (u // NT) + t + 1)
                        mm = pe.matmul(b2[:, CTX:2 * CTX], q[1], kc[1], start=True, stop=True)
                    else:
                        pe.matmul(b0[:, 0:CTX], q[0], kc[0], start=True, stop=True)
                        mm = pe.matmul(b1[:, 0:CTX], q[1], kc[1], start=True, stop=True)
                    mm.then_inc(S["sc_mm"], 1)

                def turn_probs(k):
                    hb, t = units[k]
                    u = u0 + k
                    pe.wait_ge(S["pmix"], u + 1)
                    if u >= 1:
                        pe.wait_ge(S["o_ev"], u)
                        pe.wait_ge(S["at_ev_lo"], u)
                    blocks = list(range(NT)) if t < LT else [4, 5]
                    for kb in blocks:
                        dst = bank[6][:, kb * P:(kb + 1) * P] if kb < 4 else bank[7][:, (kb - 4) * P:(kb - 3) * P]
                        mm = pe.transpose(dst, PR[k % 2][:, 0, kb * P:(kb + 1) * P], ident)
                    mm.then_inc(S["at_mm"], 1)

                def av(k):
                    hb, t = units[k]
                    u = u0 + k
                    pe.wait_ge(S["at_ev_lo"], u + 1)
                    pe.wait_ge(S["at_ev_hi"], u + 1)
                    blocks = list(range(NT)) if t < LT else [4, 5]
                    for kb in blocks:
                        mm = pe.matmul(bank[7][:, 256:384], aT[k % 2][:, kb, :], vA[:, kb, hb * P:(hb + 1) * P],
                                       start=(kb == blocks[0]), stop=(kb == blocks[-1]))
                    mm.then_inc(S["o_mm"], 1)

                scores(0)
                scores(1)
                for k in range(len(units)):
                    turn_probs(k)
                    if k + 2 < len(units):
                        scores(k + 2)
                    av(k)

            def mixer_out(l):
                q = turns(l)
                n = TILES[l]
                w0 = [p for p, it in enumerate(STREAM) if it[0] == "wo" and it[1] == l]
                wv = [slot(p).rearrange("p (c n) -> p c n", c=KC) for p in w0]
                src = [oall, R1][l]

                def turn(k):
                    kind, t = q[k]
                    if k >= 1:
                        pe.wait_ge(L[l]["turn_ev"], after(l, "turn_ev", k))
                    if kind == "o":
                        pe.wait_ge(L[l]["on_rdy"], after(l, "on_rdy", t + 1))
                        s = src[:, t, :]
                    else:
                        pe.wait_ge(L[l]["hf_rdy"], after(l, "hf_rdy", t + 1))
                        s = HF[t % 2]
                    for c in range(KC):
                        mm = pe.transpose(bank[2 + c // 4][:, (c % 4) * P:(c % 4 + 1) * P],
                                          s.rearrange("p (q c) -> p c q", c=KC)[:, c, :], ident)
                    mm.then_inc(L[l]["turn_mm"], 1)

                def use(k):
                    kind, t = q[k]
                    pe.wait_ge(L[l]["turn_ev"], after(l, "turn_ev", k + 1))
                    if kind == "o":
                        if t == 0:
                            ring_wait(w0[0])
                            ring_wait(w0[1])
                        if t >= 2:
                            pe.wait_ge(L[l]["z_done"], after(l, "z_done", t - 1))
                        for h in range(2):
                            for c in range(KC):
                                mm = pe.matmul(bank[4 * (t % 2) + h][:, :], oT[k % 2][:, c, :], wv[h][:, c, :],
                                               start=(c == 0), stop=(c == KC - 1))
                        mm.then_inc(L[l]["y_mm"], 1)
                        pe.wait_ge(L[l]["y_mm"], after(l, "y_mm", t + 1))
                        pe.sem_inc(L[l]["turn_use"], 1)
                        if t == n - 1:
                            pe.sem_inc(ring_used, 2)
                    else:
                        if t == 0:
                            pe.wait_ge(S["routerw_ld"], 16 * (l + 1))
                        for c in range(KC):
                            mm = pe.matmul(bank[6][:, t * 16:(t + 1) * 16], oT[k % 2][:, c, :], rwt[:, c, :],
                                           start=(c == 0), stop=(c == KC - 1), skip_group_check=True)
                        mm.then_inc(L[l]["turn_use"], 1)

                turn(0)
                for k in range(len(q)):
                    if k + 1 < len(q):
                        turn(k + 1)
                    use(k)

            def ranks(l):
                n = TILES[l]
                Mv, PM = RT[:, 0:n * 16], RT[:, 96:96 + n * 16]
                tot = RT[:, 96 + n * 16:112 + n * 16]
                pe.wait_ge(L[l]["mask"], after(l, "mask", 1))
                pe.matmul(bank[6][:, 0:n * 16], tri, Mv, start=True, stop=False, skip_group_check=True)
                pe.matmul(bank[6][:, 0:n * 16], ones, PM, start=False, stop=True, skip_group_check=True)
                pe.matmul(bank[5][:, 0:16], ones, tot, start=True, stop=True).then_inc(L[l]["rank_mm"], 1)

            def moe(l):
                E = L[l]
                base = MOEBASE[l]

                def turn(j, first=False):
                    pe.wait_ge(E["gath"], 16 * (j + 1))
                    if not first:
                        pe.wait_ge(E["xt_a"], j)
                        pe.wait_ge(E["xt_v"], j)
                    for c in range(KC):
                        mm = pe.transpose(bank[c // 4][:, (c % 4) * P:(c % 4 + 1) * P],
                                          xrow.rearrange("p (q c) -> p c q", c=KC)[:, c, :], ident)
                    mm.then_inc(E["xt"], 1)

                pe.wait_ge(E["tbl"], 1)
                pe.sem_inc(E["yd_mm"], 1)
                pe.sem_inc(E["gt_mm"], 1)
                nb = pe.value_load(inclI[0:1, NE - 1:NE], min_val=2, max_val=MAXB[l] + 1)
                turn(0, True)
                sl = [(base + i) % RING for i in range(3)]
                uses = [(base + i) // RING for i in range(3)]
                uses1 = [(base + 3 + i) // RING for i in range(3)]
                with pe.Fori(0, MAXB[l]) as j:
                    with pe.If(j + 1 < nb):
                        par = pe.value_load(peI[0:1, bass.ds(3 * j, 1)], min_val=0, max_val=1)
                        h0 = pe.value_load(peI[0:1, bass.ds(3 * j + 1, 1)], min_val=0, max_val=16 * 17)
                        h1 = pe.value_load(peI[0:1, bass.ds(3 * j + 2, 1)], min_val=0, max_val=16 * 17)

                        def weights(i, cols):
                            step = 3 * SLOT if sl[i] < 3 else -3 * SLOT
                            pe.wait_ge(ring_ld[sl[i]], h0 + 16 * uses[i])
                            pe.wait_ge(ring_ld[(sl[i] + 3) % RING], h1 + 16 * uses1[i])
                            return lambda c, o, n: ring[:, bass.ds(sl[i] * SLOT + par * step + c * cols + o, n)]

                        pe.wait_ge(E["xt_a"], j + 1)
                        pe.wait_ge(E["xt_v"], j + 1)
                        w = weights(0, FE)
                        pe.wait_ge(E["silu"], j + 1)
                        for c in range(KC):
                            mm = pe.matmul(bank[2][:, :], xT[:, c, :], w(c, 0, FE), start=(c == 0), stop=(c == KC - 1))
                        mm.then_inc(E["g_mm"], 1)
                        w = weights(1, FE)
                        pe.wait_ge(E["gmul"], j + 1)
                        for c in range(KC):
                            mm = pe.matmul(bank[3][:, :], xT[:, c, :], w(c, 0, FE), start=(c == 0), stop=(c == KC - 1))
                        mm.then_inc(E["u_mm"], 1)
                        turn(j + 1)
                        pe.wait_ge(E["gmul"], j + 2)
                        for c in range(4):
                            mm = pe.transpose(bank[4][:, c * P:(c + 1) * P],
                                              gate.rearrange("p (q c) -> p c q", c=4)[:, c, :], ident)
                        mm.then_inc(E["gt_mm"], 1)
                        w = weights(2, D)
                        pe.wait_ge(E["gt_ev"], j + 1)
                        pe.wait_ge(E["y_a"], j + 1)
                        pe.wait_ge(E["y_v"], j + 1)
                        for h in range(2):
                            for c in range(4):
                                mm = pe.matmul(bank[5 + h][:, :], gT[:, c, :], w(c, h * 512, 512), start=(c == 0), stop=(c == 3))
                        mm.then_inc(E["yd_mm"], 1)

            pe.wait_ge(S["o_ev"], 48)
            for n in range(4, 10):
                ada(n)
            mixer_out(0)
            for n in (10, 11):
                ada(n)
            ranks(0)
            for n in range(12, 24):
                ada(n)
            moe(0)

            pe.wait_ge(L[0]["xfin"], NT)
            transpose_x(1)
            pe.wait_ge(ht_l[1], KC)
            pe.wait_ge(ht_c[1], KC)
            for i in range(8):
                part, h = divmod(i, 4)
                p = GLA0 + part
                if h == 0:
                    ring_wait(p)
                w = slot(p).rearrange("p (c n) -> p c n", c=KC)
                if i >= 2:
                    pe.wait_ge(S["gq_ev"], i - 1)
                for c in range(KC):
                    mm = pe.matmul(bank[i % 2][:, :], w[:, c, h * P:(h + 1) * P], hT[:, c, 0:SEQ], start=(c == 0), stop=(c == KC - 1))
                mm.then_inc(S["gq_mm"], 1)
                if part:
                    if h >= 2:
                        pe.wait_ge(S["gk_ev"], h - 1)
                    for c in range(KC):
                        mm = pe.matmul(bank[2 + i % 2][:, 0:CTX], w[:, c, h * P:(h + 1) * P], hT[:, c, SEQ:TOK],
                                       start=(c == 0), stop=(c == KC - 1))
                    mm.then_inc(S["gk_mm"], 1)
                if h == 3:
                    pe.wait_ge(S["gq_mm"], i + 1)
                    if part:
                        pe.wait_ge(S["gk_mm"], 4)
                    pe.sem_inc(ring_used, 1)
            n = 0
            for j, tiles in ((2, NT), (3, NT), (4, LT), (5, LT)):
                p = GLA0 + j
                ring_wait(p)
                w = slot(p).rearrange("p (c n) -> p c n", c=KC)
                for t in range(tiles):
                    if n >= 4:
                        pe.wait_ge(S["gv_ev"], n - 3)
                    for c in range(KC):
                        mm = pe.matmul(bank[4 + n % 4][:, :], hT[:, c, t * P:(t + 1) * P], w[:, c, :], start=(c == 0), stop=(c == KC - 1))
                    mm.then_inc(S["gv_mm"], 1)
                    n += 1
                pe.wait_ge(S["gv_mm"], n)
                pe.sem_inc(ring_used, 1)
            pe.wait_ge(S["gw_ld"], 64)
            pe.wait_ge(S["wz"], 2)
            pe.wait_ge(S["gq_ev"], 8)
            for c in range(KC):
                pe.matmul(bank[0][0:64, :], wdn[:, c, :], hT[:, c, 0:SEQ], start=(c == 0), stop=(c == KC - 1))
            for c in range(KC):
                mm = pe.matmul(bank[1][0:64, 0:CTX], wdn[:, c, :], hT[:, c, SEQ:TOK], start=(c == 0), stop=(c == KC - 1))
            mm.then_inc(S["gd_mm"], 1)
            pe.wait_ge(S["gd_ev"], 1)
            pe.wait_ge(S["gk_ev"], 4)
            pe.wait_ge(S["gv_ev"], 20)
            lv = 0
            for h in range(GH):
                if h:
                    pe.wait_ge(S["off_ev"], 3 * h)
                    pe.wait_ge(S["kc_ev"], h)
                for d in range(2):
                    b0, b1 = bank[2 * d], bank[2 * d + 1]
                    w = wup[32 * d:32 * d + RANK, h * P:(h + 1) * P]
                    g = gdT[32 * d:32 * d + RANK, :]
                    pe.matmul(b0[:, :], w, g[:, 0:SEQ], start=True, stop=True)
                    pe.matmul(b1[:, 0:CTX], w, g[:, SEQ:TOK], start=True, stop=True).then_inc(S["gu_mm"], 1)
                for k in range(8):
                    if lv >= 2:
                        pe.wait_ge(S["lv_ev"], lv - 1)
                    if k == 0 and h:
                        pe.wait_ge(S["go_ev"], 4 * h)
                        pe.wait_ge(S["gss"], 4 * h)
                    if k:
                        pe.wait_ge(S["lv_mul"], 7 * h + k)
                    src = QK[:, h] if k == 0 else LVB[(k - 1) % 2]
                    for b in range(4):
                        mm = pe.matmul(bank[4 + lv % 2][:, b * P:(b + 1) * P], src[:, 1, b * P:(b + 1) * P],
                                       src[:, 0, b * P:(b + 1) * P], start=True, stop=True, skip_group_check=True)
                    mm.then_inc(S["lv_mm"], 1)
                    lv += 1
                pe.wait_ge(S["kc_done"], h + 1)
                pe.wait_ge(S["ls_done"], 2 * h + 2)
                for d in range(2):
                    for t in range(CT):
                        mm = pe.transpose(bank[3][:, (2 * d + t) * P:(2 * d + t + 1) * P], KXG[:, d, t * P:(t + 1) * P], ident)
                mm.then_inc(S["kc_mm"], 1)
                pe.wait_ge(S["kc_ev"], h + 1)
                for d in range(2):
                    for t in range(CT):
                        mm = pe.matmul(bank[6][:, d * DV:(d + 1) * DV], KXT[:, d, t, :], V1[:, LT + t, h * DV:(h + 1) * DV],
                                       start=(t == 0), stop=(t == CT - 1), skip_group_check=True)
                mm.then_inc(S["st_mm"], 1)
                pe.wait_ge(S["tl_done"], h + 1)
                for n, (s, t) in enumerate(OFF):
                    fwd = s < t
                    far = abs(s - t) > 1 or {s, t} == {1, 2}
                    if fwd:
                        kk = VAR[:, 0, :] if (s == 0 and far) else TL[:, 1, s * P:(s + 1) * P]
                        qq = VAR[:, 1, :] if (t == 3 and far) else TL[:, 0, t * P:(t + 1) * P]
                    else:
                        kk = VAR[:, 2, :] if (s == 3 and far) else TL[:, 3, s * P:(s + 1) * P]
                        qq = VAR[:, 3, :] if (t == 0 and far) else TL[:, 2, t * P:(t + 1) * P]
                    mm = pe.matmul(bank[n // 4][:, (n % 4) * P:(n % 4 + 1) * P], kk, qq, start=True, stop=True, skip_group_check=True)
                    if n % 4 == 3:
                        mm.then_inc(S["off_mm"], 1)
                pe.wait_ge(S["off_ev"], 3 * h + 3)
                pe.wait_ge(S["st_ev"], h + 1)
                pe.wait_ge(S["lv_ev"], 8 * h + 8)
                for t in range(LT):
                    b = bank[4 + t]
                    for s in range(LT):
                        lhs = SD[:, t, :] if s == t else SO[:, OFF.index((s, t)), :]
                        pe.matmul(b[:, 0:DV], lhs, V1[:, s, h * DV:(h + 1) * DV], start=(s == 0), stop=False)
                    qf = TL[:, 0, 0:P] if t == 0 else VAR[:, 3 + t, :]
                    qb = TL[:, 2, 3 * P:4 * P] if t == 3 else VAR[:, 7 + t, :]
                    pe.matmul(b[:, 0:DV], qf, ST[:, 0, :], start=False, stop=False)
                    pe.matmul(b[:, 0:DV], qb, ST[:, 1, :], start=False, stop=True).then_inc(S["go_mm"], 1)
            mixer_out(1)
            ranks(1)
            moe(1)

        @block.scalar
        def _(act):
            cnt = [0]

            def link(ins):
                cnt[0] += 1
                ins.then_inc(S["act"], 1)
                act.wait_ge(S["act"], cnt[0])

            act.wait_ge(const_ld, 48)
            act.activation(c_act, c_raw, ACT.Silu).then_inc(silu_c, 1)

            def context_h(l):
                act.wait_ge(modc_ld[l], 16 * 4)
                mvv = modc[l].rearrange("p (v s c) -> p v s c", v=2, s=2)
                for c in range(KC):
                    act.wait_ge(xt_mm[l], c + 1)
                    act.activation(hT[:, c, SEQ:TOK], bank[3 + c % 3][:, 0:CTX], ACT.Identity,
                                   bias=mvv[:, 0, 1, c:c + 1], scale=mvv[:, 1, 1, c:c + 1]).then_inc(ht_c[l], 1)

            act.wait_ge(S["lam_a"], 1)
            act.activation(lam4[:, 2:4], lam4[:, 0:2], ACT.Exp).then_inc(S["lam_b"], 1)
            context_h(0)
            for hg in range(2):
                if hg:
                    act.wait_ge(S["o_mm"], NT * 4 * hg)
                for i in range(8 * hg, 8 * hg + 8):
                    hb, dst = i % 4, (qT, kT)[(i % 8) // 4]
                    act.wait_ge(S["proj_mm"], i + 1)
                    if i >= 2:
                        act.wait_ge(S["rot_mm"], i - 1)
                        act.wait_ge(S["rope_cos"], i - 1)
                    act.activation(qraw[i % 2], bank[i % 2][:, :], ACT.Copy).then_inc(S["qraw"], 1)
                    act.activation(dst[:, hb, SEQ:TOK], bank[2 + i % 2][:, 0:CTX], ACT.Copy).then_inc(S["ctx_ev"], 1)
                for t in range(NT):
                    act.wait_ge(S["v_mm"], NT * hg + t + 1)
                    act.activation(vA[:, t, :], bank[6 + t % 2][:, :], ACT.Copy).then_inc(S["v_ev"], 1)
                units = attn_units()
                scale = float(HD) ** -0.5

                def probs(k):
                    hb, t = units[k]
                    u = len(units) * hg + k
                    b0, b1, b2 = (bank[3 * (k % 2) + j] for j in range(3))
                    st = st_a[k % 2]
                    if u >= 2:
                        act.wait_ge(S["at_mm"], u - 1)
                    if k == 0:
                        act.wait_ge(S["rope_done"], 8 * hg + 8)
                    act.wait_ge(S["maxed"], u + 1)
                    if t < LT:
                        for m in range(2):
                            act.activation(PR[k % 2][:, m, 0:SEQ], (b0, b1)[m][:, :], ACT.Exp, bias=st[:, 4 + m:5 + m],
                                           scale=scale, accum_out=st[:, 6 + 2 * m:7 + 2 * m])
                    for m in range(2):
                        src = b2[:, m * CTX:(m + 1) * CTX] if t < LT else (b0, b1)[m][:, 0:CTX]
                        ins = act.activation(PR[k % 2][:, m, SEQ:TOK], src, ACT.Exp,
                                             bias=st[:, 4 + m:5 + m], scale=scale, accum_out=st[:, 7 + 2 * m:8 + 2 * m])
                    ins.then_inc(S["exped"], 1)

                def out(k):
                    hb, t = units[k]
                    u = len(units) * hg + k
                    h = 4 * hg + hb
                    act.wait_ge(S["at_mm"], u + 1)
                    if u >= 2:
                        act.wait_ge(S["o_mm"], u - 1)
                    act.activation(aT[k % 2][:, 4:6, :], bank[7][:, 0:2 * P].rearrange("p (k q) -> p k q", k=2), ACT.Copy
                                   ).then_inc(S["at_ev_hi"], 1)

                def fin(k):
                    hb, t = units[k]
                    u = len(units) * hg + k
                    h = 4 * hg + hb
                    st = st_a[k % 2]
                    act.wait_ge(S["o_mm"], u + 1)
                    link(act.activation(oall[:, t, h * P:(h + 1) * P], bank[7][:, 256:384], ACT.Square, scale=st[:, 12:13],
                                        accum_out=ss[:, t * HEADS + h:t * HEADS + h + 1]))
                    act.activation(oall[:, t, h * P:(h + 1) * P], bank[7][:, 256:384], ACT.Copy, scale=st[:, 12:13]
                                   ).then_inc(S["o_ev"], 1)

                probs(0)
                for k in range(len(units)):
                    if k + 1 < len(units):
                        probs(k + 1)
                    out(k)
                    fin(k)
            act.wait_ge(S["o_ev"], 48)
            act.wait_ge(S["init"], 1)
            act.activation(rstd, ss, ACT.Sqrt, bias=epst, scale=1.0 / P).then_inc(S["rms_sqrt"], 1)

            def mixer_out(l):
                sq = 0
                for k, (kind, t) in enumerate(turns(l)):
                    if kind == "r":
                        act.wait_ge(L[l]["bn"], after(l, "bn", t + 1))
                        act.activation(sd[:, 0:1], mv[:, 1:2], ACT.Sqrt, bias=epst).then_inc(L[l]["ln_sqrt"], 1)
                        sq += 1
                    act.wait_ge(L[l]["turn_mm"], after(l, "turn_mm", k + 1))
                    if k >= 2:
                        act.wait_ge(L[l]["turn_use"], after(l, "turn_use", k - 1))
                    act.activation(oT[k % 2][:, 0:4, :], bank[2][:, :].rearrange("p (c t) -> p c t", c=4), ACT.Copy)
                    act.activation(oT[k % 2][:, 4:8, :], bank[3][:, :].rearrange("p (c t) -> p c t", c=4), ACT.Copy
                                   ).then_inc(L[l]["turn_ev"], 1)
                n = TILES[l]
                act.wait_ge(L[l]["turn_use"], after(l, "turn_use", len(turns(l))))
                act.activation(RT[:, 208:208 + n * 16], bank[6][:, 0:n * 16], ACT.Sigmoid).then_inc(L[l]["aff"], 1)

            def moe(l):
                E = L[l]
                act.wait_ge(E["tbl"], 1)
                nb = act.value_load(inclI[0:1, NE - 1:NE], min_val=2, max_val=MAXB[l] + 1)

                def turned(j):
                    act.wait_ge(E["xt"], j + 1)
                    act.activation(xT[:, 4:8, :], bank[1][:, :].rearrange("p (c t) -> p c t", c=4), ACT.Copy).then_inc(E["xt_a"], 1)

                act.sem_inc(E["silu"], 1)
                act.sem_inc(E["y_a"], 1)
                act.dma_start(ypad[l][(MAXB[l] + 1) * P:, :], X[l][:, 0, :]).then_inc(E["y_st"], 16)
                turned(0)
                with act.Fori(0, MAXB[l]) as j:
                    with act.If(j + 1 < nb):
                        act.wait_ge(E["g_mm"], j + 1)
                        act.wait_ge(E["gmul"], j + 1)
                        act.activation(gsil, bank[2][:, :], ACT.Silu).then_inc(E["silu"], 1)
                        act.wait_ge(E["u_mm"], j + 1)
                        turned(j + 1)
                        act.wait_ge(E["yd_mm"], j + 2)
                        act.wait_ge(E["y_st"], 16 * (j + 1))
                        act.activation(ysb[:, 0:512], bank[5][:, :], ACT.Copy).then_inc(E["y_a"], 1)
                        act.wait_ge(E["y_a"], j + 2)
                        act.wait_ge(E["y_v"], j + 2)
                        act.dma_start(ypad[l][bass.ds(j * P, P), :], ysb).then_inc(E["y_st"], 16)
                stores = act.value_load(countI[0:1, 0:1], min_val=16, max_val=16 * 28)
                act.wait_ge(E["y_st"], stores)
                act.sem_inc(E["y_all"], 1)
                for t in range(TILES[l]):
                    act.wait_ge(E["bn2"], after(l, "bn2", t + 1))
                    act.activation(sd[:, 1:2], mv[:, 1:2], ACT.Sqrt, bias=epst).then_inc(E["ln2_sqrt"], 1)

            mixer_out(0)
            moe(0)
            context_h(1)
            for i in range(8):
                part, h = divmod(i, 4)
                act.wait_ge(S["gq_mm"], i + 1)
                act.activation(QK[:, h, part, :], bank[i % 2][:, :], ACT.Copy, scale=(DK ** -0.5 if part == 0 else 1.0)
                               ).then_inc(S["gq_ev"], 1)
                if part:
                    act.wait_ge(S["gk_mm"], h + 1)
                    act.activation(KX[:, h, :], bank[2 + i % 2][:, 0:CTX], ACT.Copy).then_inc(S["gk_ev"], 1)
            n = 0
            for j, tiles in ((0, NT), (1, NT), (0, LT), (1, LT)):
                if n == 2 * NT:
                    act.wait_ge(S["xsave_st"], 16 * LT)
                for t in range(tiles):
                    act.wait_ge(S["gv_mm"], n + 1)
                    dst = (V1 if n < 2 * NT else R1)[:, t, j * 512:(j + 1) * 512]
                    act.activation(dst, bank[4 + n % 4][:, :], ACT.Copy if n < 2 * NT else ACT.Silu).then_inc(S["gv_ev"], 1)
                    n += 1
            act.wait_ge(S["gd_mm"], 1)
            act.activation(gdT[0:64, 0:SEQ], bank[0][0:64, :], ACT.Copy)
            act.activation(gdT[0:64, SEQ:TOK], bank[1][0:64, 0:CTX], ACT.Copy).then_inc(S["gd_ev"], 1)
            inv = 1.0 / TAU
            for h in range(GH):
                if h:
                    act.wait_ge(S["go_mm"], 4 * h)
                for d in range(2):
                    act.wait_ge(S["gu_mm"], 2 * h + d + 1)
                    bg = bgc[:, 4 * d + h:4 * d + h + 1]
                    act.activation(LS[:, d, 0:SEQ], bank[2 * d][:, :], ACT.Abs, bias=bg)
                    link(act.activation(LS[:, d, SEQ:TOK], bank[2 * d + 1][:, 0:CTX], ACT.Abs, bias=bg))
                link(act.activation(LS[:, :, :], LS[:, :, :], ACT.Exp, scale=-1.0))
                act.activation(LS[:, :, :], LS[:, :, :], ACT.Ln, bias=1.0).then_inc(S["ls_exp"], 1)
                for k in range(7):
                    i = 7 * h + k
                    act.wait_ge(S["lv_arg"], i + 1)
                    act.activation(LVB[k % 2], LVB[k % 2], ACT.Exp, scale=inv).then_inc(S["lv_exp"], 1)
                bf, bb = GB[:, 0, :], GB[:, 1, :]
                bias = lambda n: bstot[:, n:n + 1]
                act.activation(KXG[:, 0, :], bf[:, SEQ:TOK], ACT.Exp, scale=-inv, bias=bias(8))
                act.activation(KXG[:, 1, :], bb[:, SEQ:TOK], ACT.Exp, scale=-inv, bias=bias(9)).then_inc(S["kc_exp"], 1)
                act.activation(TL[:, 0, :], bf[:, 0:SEQ], ACT.Exp, scale=inv)
                act.activation(TL[:, 2, :], bb[:, 0:SEQ], ACT.Exp, scale=inv)
                for b in range(4):
                    act.activation(TL[:, 1, b * P:(b + 1) * P], bf[:, b * P:(b + 1) * P], ACT.Exp, scale=-inv, bias=bias(b))
                    act.activation(TL[:, 3, b * P:(b + 1) * P], bb[:, b * P:(b + 1) * P], ACT.Exp, scale=-inv, bias=bias(4 + b))
                act.activation(etot[:, 0:12], bstot[:, 12:24], ACT.Exp).then_inc(S["tl_exp"], 1)
                act.wait_ge(S["kc_mm"], h + 1)
                act.activation(KXT[:, :, :, :], bank[3][:, :].rearrange("p (d t e) -> p d t e", d=2, t=2), ACT.Copy
                               ).then_inc(S["kc_ev"], 1)
                act.wait_ge(S["st_mm"], h + 1)
                act.activation(ST[:, :, :], bank[6][:, :].rearrange("p (d e) -> p d e", d=2), ACT.Copy).then_inc(S["st_ev"], 1)
                for n in range(3):
                    act.wait_ge(S["off_mm"], 3 * h + n + 1)
                    if n == 0:
                        act.wait_ge(S["lv_mm"], 8 * h + 8)
                    act.activation(SO[:, 4 * n:4 * n + 4, :], bank[n][:, :].rearrange("p (k t) -> p k t", k=4), ACT.Copy
                                   ).then_inc(S["off_ev"], 1)
                for t in range(LT):
                    act.wait_ge(S["go_ev"], 4 * h + t + 1)
                    if h or t:
                        act.wait_ge(S["gss"], 4 * h + t)
                    act.activation(KXG[:, 0, :], bank[4 + t][:, 0:DV], ACT.Square,
                                   accum_out=ss[:, t * GH + h:t * GH + h + 1]).then_inc(S["gss"], 1)
            act.wait_ge(S["gss"], 16)
            act.activation(rstd[:, 0:16], ss[:, 0:16], ACT.Sqrt, bias=epst, scale=1.0 / DV).then_inc(S["rms_sqrt"], 1)
            mixer_out(1)
            moe(1)

        @block.vector
        def _(v):
            cnt = [0]

            def link(ins):
                cnt[0] += 1
                ins.then_inc(S["dve"], 1)
                v.wait_ge(S["dve"], cnt[0])

            def ada(n):
                j = STREAM[ADA_ITEMS[n]][2]
                v.wait_ge(ring_used, used_value(ADA_ITEMS[n]))
                if n == 4:
                    v.wait_ge(S["o_mm"], 48)
                v.wait_ge(adab_ld[n % 2], 16 * (n // 2 + 1))
                if n >= 2:
                    v.wait_ge(ada_st[n % 2], 16 * (n // 2))
                one = 1.0 if j in (2, 3, 8, 9) else 0.0
                v.scalar_tensor_tensor(adat[n % 2], bank[7][0:2, :], one, adab[n % 2], ALU.add, ALU.add).then_inc(ada_row, 1)

            def latent_h(l):
                v.wait_ge(modc_ld[l], 16 * 4)
                mvv = modc[l].rearrange("p (v s c) -> p v s c", v=2, s=2)
                for c in range(KC):
                    v.wait_ge(xt_mm[l], c + 1)
                    v.tensor_scalar(hT[:, c, 0:SEQ], bank[c % 3][:, :], mvv[:, 1, 0, c:c + 1], mvv[:, 0, 0, c:c + 1],
                                    ALU.mult, ALU.add).then_inc(ht_l[l], 1)

            v.memset(epst, EPS).then_inc(S["init"], 1)
            for n in range(4):
                ada(n)
            v.wait_ge(S["lam_ld"], 16)
            v.wait_ge(ada_row, 4)
            lv4 = lamv.rearrange("p (k d) -> p k d", k=4)
            for i in range(2):
                ins = v.tensor_tensor_reduce(out=Z[:, i * HD:(i + 1) * HD], in0=lv4[:, 2 * i, :], in1=lv4[:, 2 * i + 1, :], scale=1.0, scalar=0.0,
                                             op0=ALU.mult, op1=ALU.add, accum_out=lam4[:, i:i + 1])
            ins.then_inc(S["lam_a"], 1)
            v.wait_ge(S["lam_b"], 1)
            link(v.tensor_tensor(nlam, lam4[:, 3:4], lam4[:, 2:3], ALU.subtract))
            link(v.tensor_scalar(nlam, nlam, -LAMBDA0, None, ALU.add))
            latent_h(0)
            v.wait_ge(S["cs_ld"], 16)
            for hg in range(2):
                for i in range(8 * hg, 8 * hg + 8):
                    hb, dst = i % 4, (qT, kT)[(i % 8) // 4]
                    v.wait_ge(S["rot_mm"], i + 1)
                    v.wait_ge(S["rope_cos"], i + 1)
                    if i:
                        v.wait_ge(S["rope_done"], i)
                    link(v.tensor_tensor(rtmp, bank[4 + i % 2][:, :], sinT, ALU.mult))
                    v.tensor_tensor(dst[:, hb, 0:SEQ], dst[:, hb, 0:SEQ], rtmp, ALU.add).then_inc(S["rope_done"], 1)
                units = attn_units()
                scale = float(HD) ** -0.5

                def maxes(k):
                    hb, t = units[k]
                    b = bank[3 * (k % 2):3 * (k % 2) + 3]
                    st = st_a[k % 2]
                    u = len(units) * hg + k
                    if k >= 2:
                        v.wait_ge(S["o_ev"], u - 1)
                    v.wait_ge(S["sc_mm"], u + 1)
                    w = SEQ if t < LT else CTX
                    v.tensor_reduce(st[:, 0:1], b[0][:, 0:w], AX.X, ALU.max)
                    ins = v.tensor_reduce(st[:, 1:2], b[1][:, 0:w], AX.X, ALU.max)
                    if t < LT:
                        ins = v.tensor_reduce(st[:, 2:4], b[2][:, :].rearrange("p (m k) -> p m k", m=2), AX.X, ALU.max)
                    link(ins)
                    if t < LT:
                        link(v.tensor_tensor(st[:, 2:4], st[:, 0:2], st[:, 2:4], ALU.max))
                    peak = st[:, 2:4] if t < LT else st[:, 0:2]
                    v.tensor_scalar(st[:, 4:6], peak, -scale, None, ALU.mult).then_inc(S["maxed"], 1)

                def mix(k):
                    hb, t = units[k]
                    st = st_a[k % 2]
                    u = len(units) * hg + k
                    v.wait_ge(S["exped"], u + 1)
                    r4 = st[:, 6:10].rearrange("p (m k) -> p m k", m=2)
                    if t < LT:
                        link(v.tensor_tensor(st[:, 10:12], r4[:, :, 0], r4[:, :, 1], ALU.add))
                    else:
                        link(v.tensor_copy(st[:, 10:12], r4[:, :, 1]))
                    link(v.reciprocal(st[:, 12:14], st[:, 10:12]))
                    link(v.scalar_tensor_tensor(st[:, 14:15], st[:, 10:11], st[:, 13:14], nlam, ALU.mult, ALU.mult))
                    lo = 0 if t < LT else SEQ
                    v.scalar_tensor_tensor(PR[k % 2][:, 0, lo:TOK], PR[k % 2][:, 1, lo:TOK], st[:, 14:15],
                                           PR[k % 2][:, 0, lo:TOK], ALU.mult, ALU.add).then_inc(S["pmix"], 1)

                def turned(k):
                    hb, t = units[k]
                    u = len(units) * hg + k
                    v.wait_ge(S["at_mm"], u + 1)
                    if u >= 2:
                        v.wait_ge(S["o_mm"], u - 1)
                    if t < LT:
                        v.tensor_copy(aT[k % 2][:, 0:4, :], bank[6][:, :].rearrange("p (k q) -> p k q", k=4)).then_inc(S["at_ev_lo"], 1)
                    else:
                        v.sem_inc(S["at_ev_lo"], 1)

                maxes(0)
                mix(0)
                for k in range(len(units)):
                    if k + 1 < len(units):
                        maxes(k + 1)
                    turned(k)
                    if k + 1 < len(units):
                        mix(k + 1)

            def rms_rows(l):
                nh, w = (HEADS, P) if l == 0 else (GH, DV)
                n = TILES[l]
                src = [oall, R1][l]
                v.wait_ge(S["rms_sqrt"], l + 1)
                link(v.reciprocal(rstd[:, 0:n * nh], rstd[:, 0:n * nh]))
                if l == 0:
                    link(v.tensor_scalar(rstd, rstd, 1.0 - LAMBDA0, None, ALU.mult))
                for t in range(n):
                    o = src[:, t, :].rearrange("p (h w) -> p h w", h=nh)
                    r = rstd[:, t * nh:(t + 1) * nh].unsqueeze(2).to_broadcast([P, nh, w])
                    link(v.tensor_tensor(o, o, r, ALU.mult))
                    g = normg[l].unsqueeze(1).to_broadcast([P, nh, w])
                    if t == 0:
                        v.wait_ge(L[l]["rows_ld"], after(l, "rows_ld", 16))
                    v.tensor_tensor(o, o, g, ALU.mult).then_inc(L[l]["on_rdy"], 1)

            def stats(l, t, x, name_bn, name_sqrt, name_n, col):
                link(v.bn_stats(bst[:, 0:6], x[:, 0:512]))
                link(v.bn_stats(bst[:, 6:12], x[:, 512:1024]))
                v.bn_aggr(mv, bst.rearrange("p (k s) -> p k s", k=2)).then_inc(L[l][name_bn], 1)
                v.wait_ge(L[l][name_bn], after(l, name_bn, t + 1))
                v.wait_ge(L[l][name_sqrt], after(l, name_sqrt, t + 1))
                link(v.reciprocal(sd[:, col:col + 1], sd[:, col:col + 1]))
                v.tensor_scalar(x, x, mv[:, 0:1], sd[:, col:col + 1], ALU.subtract, ALU.mult).then_inc(L[l][name_n], 1)
                v.wait_ge(L[l][name_n], after(l, name_n, t + 1))

            def mixer_norm(l):
                for t in range(TILES[l]):
                    v.wait_ge(L[l]["y_mm"], after(l, "y_mm", t + 1))
                    if t == 0:
                        v.wait_ge(S["xres_ld"], 16 * (NT + (LT if l else 0)))
                    v.wait_ge(L[l]["rows2_ld"], after(l, "rows2_ld", 48 if t < LT else 64))
                    for h in range(2):
                        ins = v.tensor_tensor(Z[:, h * 512:(h + 1) * 512], bank[4 * (t % 2) + h][:, :], gm[:, h * 512:(h + 1) * 512], ALU.mult)
                    ins.then_inc(L[l]["z_done"], 1)
                    v.wait_ge(L[l]["z_done"], after(l, "z_done", t + 1))
                    x = X[l][:, t, :]
                    link(v.scalar_tensor_tensor(x, x, ALPHA, Z, ALU.mult, ALU.add))
                    stats(l, t, x, "bn", "ln_sqrt", "ln_n", 0)

            def route(l):
                n = TILES[l]
                E = L[l]
                m = n * 16
                Mv, PM, aff = RT[:, 0:m], RT[:, 96:112 + m], RT[:, 208:208 + m]
                sel, rk, tmp = RT[:, 304:304 + m], RT[:, 400:400 + m], RT[:, 496:496 + m]
                gs, gk, gt = RT[:, 592:592 + 4 * n], RT[:, 616:616 + 4 * n], RT[:, 640:640 + 4 * n]
                AB = RT[:, 664:664 + 2 * m]
                t2 = RT[:, 856:856 + 2 * m]
                big = RT[:, 1048:1496]
                f1, f2, f3, f4 = (RT[:, 1496 + 12 * i:1496 + 12 * i + 2 * n] for i in range(4))
                nbk, incl, excl = RT[:, 1560:1576], RT[:, 1576:1592], RT[:, 1592:1608]
                E28, P28, pet = RT[:, 1608:1636], RT[:, 1636:1664], RT[:, 1664:1748]

                def rank4(s, r, t, groups):
                    s, r, t = (x.rearrange("p (g i) -> p g i", i=4) for x in (s, r, t))
                    link(v.memset(r, 0.0))
                    for d in range(1, 4):
                        link(v.tensor_tensor(t[:, :, 0:4 - d], s[:, :, 0:4 - d], s[:, :, d:4], ALU.is_ge))
                        link(v.tensor_tensor(r[:, :, d:4], r[:, :, d:4], t[:, :, 0:4 - d], ALU.add))
                        link(v.scalar_tensor_tensor(r[:, :, 0:4 - d], r[:, :, 0:4 - d], 1.0, t[:, :, 0:4 - d], ALU.add, ALU.subtract))

                v.wait_ge(E["aff"], after(l, "aff", 1))
                a3 = aff.rearrange("p (t e) -> p t e", e=16)
                link(v.tensor_tensor(sel.rearrange("p (t e) -> p t e", e=16), a3, rb.unsqueeze(1).to_broadcast([P, n, 16]), ALU.add))
                rank4(sel, rk, tmp, 4 * n)
                link(v.scalar_tensor_tensor(tmp, rk, 2.0, sel, ALU.is_lt, ALU.mult))
                link(v.tensor_reduce(gs, tmp.rearrange("p (g i) -> p g i", i=4), AX.X, ALU.add))
                rank4(gs, gk, gt, n)
                link(v.tensor_scalar(gt, gk, 0.0, None, ALU.is_equal))
                g4 = gt.unsqueeze(2).to_broadcast([P, 4 * n, 4])
                r4 = rk.rearrange("p (g i) -> p g i", i=4)
                for k in range(2):
                    link(v.scalar_tensor_tensor(AB[:, k * m:(k + 1) * m].rearrange("p (g i) -> p g i", i=4), r4, float(k), g4,
                                                ALU.is_equal, ALU.mult))
                link(v.tensor_tensor(Mv, AB[:, 0:m], AB[:, m:2 * m], ALU.add))
                link(v.memset(PM[:, 0:16], 0.0))
                for t in range(n):
                    ins = v.tensor_tensor(PM[:, (t + 1) * 16:(t + 2) * 16], PM[:, t * 16:(t + 1) * 16], Mv[:, t * 16:(t + 1) * 16], ALU.add)
                    if t < n - 1:
                        link(ins)
                ins.then_inc(E["mask"], 1)
                ab3 = AB.rearrange("p (k e) -> p k e", k=2)
                t3 = t2.rearrange("p (k e) -> p k e", k=2)
                link(v.tensor_tensor(t3, ab3, aff.unsqueeze(1).to_broadcast([P, 2, m]), ALU.mult))
                w2 = W2[:, 0:2 * n]
                link(v.tensor_reduce(w2, t2.rearrange("p (k e) -> p k e", e=16), AX.X, ALU.add))
                link(v.tensor_tensor(f1[:, 0:n], w2[:, 0:n], w2[:, n:2 * n], ALU.add))
                link(v.reciprocal(f1[:, 0:n], f1[:, 0:n]))
                w3 = w2.rearrange("p (k t) -> p k t", k=2)
                link(v.tensor_tensor(w3, w3, f1[:, 0:n].unsqueeze(1).to_broadcast([P, 2, n]), ALU.mult))

            def route_2(l):
                n = TILES[l]
                E = L[l]
                m = n * 16
                AB, t2 = RT[:, 664:664 + 2 * m], RT[:, 856:856 + 2 * m]
                big = RT[:, 1048:1496]
                f1, f2, f3, f4 = (RT[:, 1496 + 12 * i:1496 + 12 * i + 2 * n] for i in range(4))
                nbk, incl, excl = RT[:, 1560:1576], RT[:, 1576:1592], RT[:, 1592:1608]
                E28, P28, pet = RT[:, 1608:1636], RT[:, 1636:1664], RT[:, 1664:1748]
                t3 = t2.rearrange("p (k t e) -> p k t e", k=2, e=16)
                ab4 = AB.rearrange("p (k t e) -> p k t e", k=2, e=16)
                v.wait_ge(E["rank_mm"], after(l, "rank_mm", 1))
                b6 = big[:, 0:96].rearrange("p (e k) -> p e k", k=6)
                link(v.tensor_tensor(b6, bank[5][:, 0:16].unsqueeze(2).to_broadcast([P, 16, 6]),
                                     kmul.unsqueeze(1).to_broadcast([P, 16, 6]), ALU.is_gt))
                link(v.tensor_reduce(nbk, b6, AX.X, ALU.add))
                link(v.tensor_tensor_scan(incl, ones[:, 0:16], nbk, 0.0, ALU.mult, ALU.add))
                link(v.tensor_tensor(excl, incl, nbk, ALU.subtract))
                rk3 = bank[6][:, 0:m].unsqueeze(1).to_broadcast([P, 2, m])
                link(v.tensor_tensor(t2.rearrange("p (k e) -> p k e", k=2), AB.rearrange("p (k e) -> p k e", k=2), rk3, ALU.mult))
                link(v.tensor_reduce(f1, t2.rearrange("p (k e) -> p k e", e=16), AX.X, ALU.add))
                link(v.tensor_tensor(t2.rearrange("p (k e) -> p k e", e=16), AB.rearrange("p (k e) -> p k e", e=16),
                                     excl.unsqueeze(1).to_broadcast([P, 2 * n, 16]), ALU.mult))
                link(v.tensor_reduce(f2, t2.rearrange("p (k e) -> p k e", e=16), AX.X, ALU.add))
                b5 = big[:, 0:10 * n].rearrange("p (t k) -> p t k", k=5)
                link(v.tensor_tensor(b5, f1.unsqueeze(2).to_broadcast([P, 2 * n, 5]),
                                     kmul[:, 1:6].unsqueeze(1).to_broadcast([P, 2 * n, 5]), ALU.is_ge))
                link(v.tensor_reduce(f3, b5, AX.X, ALU.add))
                link(v.tensor_tensor(f2, f2, f3, ALU.add))
                link(v.scalar_tensor_tensor(f1, f3, -float(P), f1, ALU.mult, ALU.add))
                link(v.scalar_tensor_tensor(f4, f2, float(P), f1, ALU.mult, ALU.add))
                link(v.scalar_tensor_tensor(f3, f1, 28.0, f2, ALU.mult, ALU.add))
                link(v.tensor_copy(destI[:, 0:2 * n], f4))
                link(v.tensor_copy(addrI[:, 0:2 * n], f3))
                link(v.tensor_copy(tidI, tidf))
                b28 = big.rearrange("p (j e) -> p j e", e=16)
                link(v.tensor_tensor(b28, incl.unsqueeze(1).to_broadcast([P, 28, 16]), jrow.unsqueeze(2).to_broadcast([P, 28, 16]), ALU.is_le))
                link(v.tensor_reduce(E28, b28, AX.X, ALU.add))
                link(v.tensor_tensor(b28, b28, sgn.unsqueeze(1).to_broadcast([P, 28, 16]), ALU.mult))
                link(v.tensor_reduce(P28, b28, AX.X, ALU.add))
                p3 = pet.rearrange("p (j k) -> p j k", k=3)
                link(v.tensor_scalar(E28, E28, 8.0, None, ALU.mult))
                link(v.tensor_copy(p3[:, :, 0], P28))
                link(v.scalar_tensor_tensor(p3[:, :, 1], P28, -8.0, E28, ALU.mult, ALU.add))
                link(v.tensor_scalar(p3[:, :, 1], p3[:, :, 1], 16.0, None, ALU.add))
                link(v.scalar_tensor_tensor(p3[:, :, 2], P28, 8.0, E28, ALU.mult, ALU.add))
                link(v.tensor_copy(peI, pet))
                link(v.tensor_scalar(f1[:, 0:1], incl[:, NE - 1:NE], 16.0, 16.0, ALU.mult, ALU.add))
                link(v.tensor_scalar(f1[:, 1:2], incl[:, NE - 1:NE], -16.0, 16.0 * (MAXB[l] + 1), ALU.mult, ALU.add))
                link(v.tensor_copy(countI, f1[:, 0:2]))
                link(v.tensor_scalar(incl, incl, 1.0, None, ALU.add))
                v.tensor_copy(inclI, incl).then_inc(E["tbl"], 1)

            def moe(l):
                E = L[l]
                v.wait_ge(E["tbl"], 1)
                nb = v.value_load(inclI[0:1, NE - 1:NE], min_val=2, max_val=MAXB[l] + 1)

                def turned(j):
                    v.wait_ge(E["xt"], j + 1)
                    v.tensor_copy(xT[:, 0:4, :], bank[0][:, :].rearrange("p (c t) -> p c t", c=4)).then_inc(E["xt_v"], 1)

                v.sem_inc(E["gmul"], 1)
                v.sem_inc(E["y_v"], 1)
                turned(0)
                with v.Fori(0, MAXB[l]) as j:
                    with v.If(j + 1 < nb):
                        v.wait_ge(E["silu"], j + 2)
                        v.wait_ge(E["u_mm"], j + 1)
                        v.wait_ge(E["gt_mm"], j + 1)
                        v.tensor_tensor(gate, bank[3][:, :], gsil, ALU.mult).then_inc(E["gmul"], 1)
                        turned(j + 1)
                        v.wait_ge(E["gt_mm"], j + 2)
                        v.wait_ge(E["yd_mm"], j + 1)
                        v.tensor_copy(gT, bank[4][:, :].rearrange("p (c t) -> p c t", c=4)).then_inc(E["gt_ev"], 1)
                        v.wait_ge(E["yd_mm"], j + 2)
                        v.wait_ge(E["y_st"], 16 * (j + 1))
                        v.tensor_copy(ysb[:, 512:1024], bank[6][:, :]).then_inc(E["y_v"], 1)
                n = TILES[l]
                for t in range(n):
                    x = X[l][:, t, :]
                    ya, yb = yab[l][2 * (t % 2)], yab[l][2 * (t % 2) + 1]
                    v.wait_ge(E[f"ya_ld{t % 2}"], after(l, f"ya_ld{t % 2}", 32 * (t // 2 + 1)))
                    if t == 0:
                        v.wait_ge(E["rows3_ld"], after(l, "rows3_ld", 48))
                    if t == LT:
                        v.wait_ge(E["rows3_ld"], after(l, "rows3_ld", 64))
                    link(v.tensor_scalar(ya, ya, W2[:, t:t + 1], None, ALU.mult))
                    link(v.scalar_tensor_tensor(ya, yb, W2[:, n + t:n + t + 1], ya, ALU.mult, ALU.add))
                    v.tensor_tensor(ya, ya, gm, ALU.mult).then_inc(E["z2_done"], 1)
                    v.wait_ge(E["z2_done"], after(l, "z2_done", t + 1))
                    link(v.scalar_tensor_tensor(x, x, ALPHA, ya, ALU.mult, ALU.add))
                    stats(l, t, x, "bn2", "ln2_sqrt", "ln2_n", 1)

            for n in range(4, 10):
                ada(n)
                if n == 5:
                    rms_rows(0)
            mixer_norm(0)
            route(0)
            for n in (10, 11):
                ada(n)
            route_2(0)
            for n in range(12, 24):
                ada(n)
            moe(0)
            latent_h(1)
            v.wait_ge(ht_l[1], KC)
            ind = [x.rearrange("p (b t) -> p b t", b=4) for x in (GB[:, 0, 0:SEQ], GB[:, 1, 0:SEQ])]
            v.wait_ge(S["mask_ld"], 16)
            for h in range(GH):
                v.wait_ge(S["ls_exp"], h + 1)
                for d in range(2):
                    bg = bgc[:, 4 * d + h:4 * d + h + 1]
                    v.tensor_scalar(GB[:, d, 0:SEQ], bank[2 * d][:, :], bg, 0.0, ALU.add, ALU.min)
                    link(v.tensor_scalar(GB[:, d, SEQ:TOK], bank[2 * d + 1][:, 0:CTX], bg, 0.0, ALU.add, ALU.min))
                    link(v.tensor_tensor(LS[:, d, :], GB[:, d, :], LS[:, d, :], ALU.subtract))
                    for o, w in [(b * P, P) for b in range(4)] + [(SEQ, CTX)]:
                        src, dst = LS[:, d, o:o + w], GB[:, d, o:o + w]
                        if d:
                            src, dst = src[:, ::-1], dst[:, ::-1]
                        one = ones[:, 0:1].to_broadcast([P, w])
                        ins = v.tensor_tensor_scan(dst, one, src, 0.0, ALU.mult, ALU.add)
                    link(ins)
                    v.sem_inc(S["ls_done"], 1)
                tf, tb = ind[0][:, :, P - 1], ind[1][:, :, 0]
                link(v.tensor_scalar(bstot[:, 0:4], tf, 1.0 / TAU, None, ALU.mult))
                link(v.tensor_scalar(bstot[:, 4:8], tb, 1.0 / TAU, None, ALU.mult))
                link(v.tensor_scalar(bstot[:, 8:9], GB[:, 0, TOK - 1:TOK], 1.0 / TAU, None, ALU.mult))
                link(v.tensor_scalar(bstot[:, 9:10], GB[:, 1, SEQ:SEQ + 1], 1.0 / TAU, None, ALU.mult))
                link(v.tensor_copy(bstot[:, 12:14], bstot[:, 1:3]))
                link(v.tensor_copy(bstot[:, 14:15], bstot[:, 6:7]))
                link(v.tensor_copy(bstot[:, 15:16], bstot[:, 5:6]))
                link(v.tensor_copy(bstot[:, 16:17], bstot[:, 0:1]))
                link(v.tensor_tensor(bstot[:, 17:18], bstot[:, 16:17], bstot[:, 1:2], ALU.add))
                link(v.tensor_tensor(bstot[:, 18:19], bstot[:, 17:18], bstot[:, 2:3], ALU.add))
                link(v.tensor_copy(bstot[:, 21:22], bstot[:, 7:8]))
                link(v.tensor_tensor(bstot[:, 20:21], bstot[:, 21:22], bstot[:, 6:7], ALU.add))
                link(v.tensor_tensor(bstot[:, 19:20], bstot[:, 20:21], bstot[:, 5:6], ALU.add))
                link(v.memset(bstot[:, 22:24], 0.0))

                def diag(k):
                    i = 8 * h + k
                    v.wait_ge(S["lv_mm"], i + 1)
                    ps = bank[4 + i % 2][:, :].rearrange("p (b t) -> p b t", b=4)
                    mk = maskv[:, k, :].unsqueeze(1).to_broadcast([P, 4, P])
                    if k == 0:
                        v.tensor_tensor(SD, ps, mk, ALU.mult).then_inc(S["lv_ev"], 1)
                    else:
                        if k == 1:
                            v.wait_ge(S["lv_ev"], i)
                        v.copy_predicated(SD, mk.bitcast(I32), ps).then_inc(S["lv_ev"], 1)

                def args(k):
                    l2 = 1 << k
                    lv = LVB[k % 2]
                    q, kk, f, b = (x.rearrange("p (n s l) -> p n s l", s=2, l=l2)
                                   for x in (lv[:, 0, :], lv[:, 1, :], GB[:, 0, 0:SEQ], GB[:, 1, 0:SEQ]))
                    npair = SEQ // (2 * l2)
                    rf = f[:, :, 0, l2 - 1:l2].to_broadcast([P, npair, l2])
                    rbk = b[:, :, 1, 0:1].to_broadcast([P, npair, l2])
                    if k >= 2:
                        v.wait_ge(S["lv_mm"], 8 * h + k)
                    v.tensor_tensor(q[:, :, 1, :], f[:, :, 1, :], rf, ALU.subtract)
                    v.tensor_tensor(q[:, :, 0, :], b[:, :, 0, :], rbk, ALU.subtract)
                    v.tensor_tensor(kk[:, :, 0, :], rf, f[:, :, 0, :], ALU.subtract)
                    v.tensor_tensor(kk[:, :, 1, :], rbk, b[:, :, 1, :], ALU.subtract).then_inc(S["lv_arg"], 1)

                args(0)
                args(1)
                diag(0)
                for k in range(7):
                    i = 7 * h + k
                    v.wait_ge(S["lv_exp"], i + 1)
                    v.tensor_tensor(LVB[k % 2], LVB[k % 2], QK[:, h], ALU.mult).then_inc(S["lv_mul"], 1)
                    diag(k + 1)
                    if k + 2 < 7:
                        args(k + 2)
                v.wait_ge(S["kc_exp"], h + 1)
                for d in range(2):
                    ins = v.tensor_tensor(KXG[:, d, :], KXG[:, d, :], KX[:, h, :], ALU.mult)
                ins.then_inc(S["kc_done"], 1)
                v.wait_ge(S["tl_exp"], h + 1)
                for k in range(4):
                    link(v.tensor_tensor(TL[:, k, :], TL[:, k, :], QK[:, h, k % 2, :], ALU.mult))
                qf, kf, qb, kb = (TL[:, k, :].rearrange("p (b t) -> p b t", b=4) for k in range(4))
                for dst, src, fac in ((0, kf[:, 0, :], 0), (1, qf[:, 3, :], 1), (2, kb[:, 3, :], 2), (3, qb[:, 0, :], 3),
                                      (4, qf[:, 1, :], 4), (5, qf[:, 2, :], 5), (6, qf[:, 3, :], 6),
                                      (7, qb[:, 0, :], 7), (8, qb[:, 1, :], 8), (9, qb[:, 2, :], 9)):
                    ins = v.tensor_scalar(VAR[:, dst, :], src, etot[:, fac:fac + 1], None, ALU.mult)
                ins.then_inc(S["tl_done"], 1)
                for t in range(LT):
                    v.wait_ge(S["go_mm"], 4 * h + t + 1)
                    r = R1[:, t, h * DV:(h + 1) * DV]
                    v.tensor_tensor(r, r, bank[4 + t][:, 0:DV], ALU.mult).then_inc(S["go_ev"], 1)
            v.wait_ge(S["go_ev"], 16)
            rms_rows(1)
            mixer_norm(1)
            route(1)
            route_2(1)
            moe(1)

        @block.gpsimd
        def _(g):
            cnt = [0]

            def link(ins):
                cnt[0] += 1
                ins.then_inc(S["pool"], 1)
                g.wait_ge(S["pool"], cnt[0])

            g.dma_start(lamv, a["attn_lambda"][0].rearrange("k d -> (k d)").unsqueeze(0).to_broadcast([P, 4 * HD])).then_inc(S["lam_ld"], 16)
            link(g.memset(idx32[:, :], 0))
            for l in range(2):
                g.dma_start(tokd[l].rearrange("(p j) o -> p (j o)", j=28), zfill).then_inc(L[l]["tok_zero"], 16)
            g.dma_start(rb, a["router_b"].unsqueeze(0).to_broadcast([P, 16])).then_inc(S["pool_ld"], 16)

            def mod_cols(l, n):
                for k in (n - 1, n):
                    g.wait_ge(ada_st[k % 2], 16 * (k // 2 + 1))
                mvv = modc[l].rearrange("p (v s c) -> p v s c", v=2, s=2)
                for vec in range(2):
                    for s in range(2):
                        g.dma_start(mvv[:, vec, s, :], modd[l][s, vec * D:(vec + 1) * D].rearrange("(p c) -> p c", c=KC)).then_inc(modc_ld[l], 16)

            mod_cols(0, 3)
            g.wait_ge(S["cs_ld"], 16)
            for i in range(16):
                hb, dst = i % 4, (qT, kT)[(i % 8) // 4]
                g.wait_ge(S["qraw"], i + 1)
                if i == 8:
                    g.wait_ge(S["o_mm"], 24)
                g.tensor_tensor(dst[:, hb, 0:SEQ], qraw[i % 2], cosT, ALU.mult).then_inc(S["rope_cos"], 1)

            def row(l, s, vec):
                return bcast_row(modd[l][s, vec * D:(vec + 1) * D], D)

            def mixer_rows(l):
                E = L[l]
                w = (P, DV)[l]
                gsrc = (a["attn_subln_g"][0], a["gla_norm_g"][0])[l]
                g.dma_start(normg[l], gsrc.unsqueeze(0).to_broadcast([P, w])).then_inc(E["rows_ld"], 16)
                g.dma_start(rwt, a["router_w"].rearrange("(p c) e -> p c e", c=KC)).then_inc(S["routerw_ld"], 16)
                for t in range(TILES[l]):
                    src = xsave[t * P:(t + 1) * P, :] if l else (
                        a["x"][0][t * P:(t + 1) * P, :] if t < LT else a["ctx"][0][(t - LT) * P:(t - LT + 1) * P, :])
                    g.dma_start(X[l][:, t, :], src).then_inc(S["xres_ld"], 16)
                if l == 0:
                    for k in (8, 9):
                        g.wait_ge(ada_st[k % 2], 16 * (k // 2 + 1))
                g.dma_start(gm, row(l, 0, 2)).then_inc(E["rows2_ld"], 16)
                g.dma_start(lng, bcast_row(a["ln_g"][l, 0], D)).then_inc(E["rows2_ld"], 16)
                g.dma_start(lnb, bcast_row(a["ln_b"][l, 0], D)).then_inc(E["rows2_ld"], 16)
                g.dma_start(scf, row(l, 0, 4)).then_inc(E["lgk"], 16)
                g.dma_start(shf, row(l, 0, 3)).then_inc(E["lgk"], 16)
                for t in range(TILES[l]):
                    x = X[l][:, t, :]
                    hf = HF[t % 2]
                    g.wait_ge(E["ln_n"], after(l, "ln_n", t + 1))
                    if t == 0:
                        g.wait_ge(E["rows2_ld"], after(l, "rows2_ld", 48))
                        g.wait_ge(E["lgk"], after(l, "lgk", 32))
                    if t == LT:
                        g.wait_ge(E["lgk"], after(l, "lgk", 64))
                    link(g.tensor_tensor(x, x, lng, ALU.mult))
                    link(g.tensor_tensor(x, x, lnb, ALU.add))
                    if t >= 2:
                        g.wait_ge(E[f"hf_st{t % 2}"], after(l, f"hf_st{t % 2}", 16 * (t // 2)))
                        g.wait_ge(E["turn_mm"], after(l, "turn_mm", turns(l).index(("r", t - 2)) + 1))
                    link(g.tensor_tensor(hf, x, scf, ALU.mult))
                    g.tensor_tensor(hf, hf, shf, ALU.add).then_inc(E["hf_rdy"], 1)
                    g.wait_ge(E["hf_rdy"], after(l, "hf_rdy", t + 1))
                    g.dma_start(hfd[l][t * P:(t + 1) * P, :], hf).then_inc(E[f"hf_st{t % 2}"], 16)
                    if l == 0 and t == LT - 1:
                        g.wait_ge(E["z_done"], after(l, "z_done", LT))
                        g.dma_start(gm, row(l, 1, 2)).then_inc(E["rows2_ld"], 16)
                        g.dma_start(scf, row(l, 1, 4)).then_inc(E["lgk"], 16)
                        g.dma_start(shf, row(l, 1, 3)).then_inc(E["lgk"], 16)

            def dispatch(l):
                E = L[l]
                n = TILES[l]
                g.wait_ge(E["tbl"], 1)
                g.wait_ge(E["tok_zero"], 16)
                for k in range(2 * n):
                    g.indirect_dma_start(out=tokd[l], out_offset=bass.IndirectOffsetOnAxis(ap=addrI[:, k:k + 1], axis=0),
                                         in_=tidI[:, k % n:k % n + 1], in_offset=None).then_inc(E["scat"], 16)
                g.wait_ge(E["scat"], after(l, "scat", 32 * n))
                g.dma_start(slotI, tokd[l].rearrange("(p j) o -> p (j o)", j=28)).then_inc(E["slot_ld"], 16)
                for b in range(2):
                    g.wait_ge(E[f"hf_st{b}"], after(l, f"hf_st{b}", 16 * (n // 2)))
                g.wait_ge(E["slot_ld"], after(l, "slot_ld", 16))

            def moe(l):
                E = L[l]
                n = TILES[l]
                nb = g.value_load(inclI[0:1, NE - 1:NE], min_val=2, max_val=MAXB[l] + 1)

                def passed():
                    g.sem_inc(S["passed"], 1)

                def gather(j):
                    g.tensor_copy(idxcur, slotI[:, bass.ds(j, 1)]).then_inc(E["idx"], 1)
                    g.wait_ge(E["idx"], j + 1)
                    passed()
                    g.indirect_dma_start(out=xrow, out_offset=None, in_=hfd[l],
                                         in_offset=bass.IndirectOffsetOnAxis(ap=idxcur, axis=0)).then_inc(E["gath"], 16)

                g.tensor_copy(idxcur, slotI[:, 0:1]).then_inc(E["idx"], 1)
                g.wait_ge(E["idx"], 1)
                g.indirect_dma_start(out=xrow, out_offset=None, in_=hfd[l],
                                     in_offset=bass.IndirectOffsetOnAxis(ap=idxcur, axis=0)).then_inc(E["gath"], 16)
                with g.Fori(0, MAXB[l] + 1) as j:
                    with g.If(j + 1 >= nb):
                        g.dma_start(ypad[l][bass.ds(j * P, P), :], X[l][:, 0, :]).then_inc(E["yfill"], 16)
                with g.Fori(0, MAXB[l]) as j:
                    with g.If(j + 1 < nb):
                        g.wait_ge(E["xt"], j + 1)
                        g.wait_ge(E["gath"], 16 * (j + 1))
                        gather(j + 1)
                g.wait_ge(E["gath"], 16 * nb)
                passed()
                if l == 0:
                    for k in (10, 11):
                        g.wait_ge(ada_st[k % 2], 16 * (k // 2 + 1))
                g.dma_start(gm, row(l, 0, 5)).then_inc(E["rows3_ld"], 16)
                g.dma_start(lng, bcast_row(a["ln_g"][l, 1], D)).then_inc(E["rows3_ld"], 16)
                g.dma_start(lnb, bcast_row(a["ln_b"][l, 1], D)).then_inc(E["rows3_ld"], 16)
                g.wait_ge(E["y_all"], after(l, "y_all", 1))
                fills = g.value_load(countI[0:1, 1:2], min_val=16, max_val=16 * 28)
                g.wait_ge(E["yfill"], fills)
                passed()

                def fetch(t):
                    for k in range(2):
                        g.indirect_dma_start(out=yab[l][2 * (t % 2) + k], out_offset=None, in_=ypad[l],
                                             in_offset=bass.IndirectOffsetOnAxis(ap=destI[:, k * n + t:k * n + t + 1], axis=0)
                                             ).then_inc(E[f"ya_ld{t % 2}"], 16)

                fetch(0)
                fetch(1)
                for t in range(n):
                    x = X[l][:, t, :]
                    if l == 0 and t == LT - 1:
                        g.wait_ge(E["z2_done"], after(l, "z2_done", LT))
                        g.dma_start(gm, row(l, 1, 5)).then_inc(E["rows3_ld"], 16)
                    g.wait_ge(E["ln2_n"], after(l, "ln2_n", t + 1))
                    if t == 0:
                        g.wait_ge(E["rows3_ld"], after(l, "rows3_ld", 48))
                    if t + 2 < n:
                        fetch(t + 2)
                    link(g.tensor_tensor(x, x, lng, ALU.mult))
                    g.tensor_tensor(x, x, lnb, ALU.add).then_inc(E["xfin"], 1)
                    g.wait_ge(E["xfin"], after(l, "xfin", t + 1))
                    if l:
                        g.dma_start(out[0][t * P:(t + 1) * P, :], x).then_inc(S["outst"], 16)
                    elif t < LT:
                        g.dma_start(xsave[t * P:(t + 1) * P, :], x).then_inc(S["xsave_st"], 16)

            g.wait_ge(S["o_mm"], 48)
            g.wait_ge(S["o_ev"], 48)
            mixer_rows(0)
            dispatch(0)
            moe(0)
            mod_cols(1, 23)
            link(g.memset(wdn, 0.0))
            g.sem_inc(S["wz"], 1)
            for d in range(2):
                g.dma_start(wdn[:, :, 32 * d:32 * d + RANK], a["gla_wg_down"][0, d].rearrange("(p c) r -> p c r", c=KC)).then_inc(S["gw_ld"], 16)
                g.dma_start(wup[32 * d:32 * d + RANK, :], a["gla_wg_up"][0, d]).then_inc(S["gw_ld"], 16)
            for d in range(2):
                g.dma_start(bgc[:, 4 * d:4 * d + 4], a["gla_bg"][0, d].rearrange("(h p) -> p h", p=P), allow_slow_non_contiguous=True).then_inc(S["bg_ld"], 16)
            g.wait_ge(S["bg_ld"], 32)
            g.sem_inc(S["wz"], 1)
            g.wait_ge(S["go_mm"], 16)
            g.wait_ge(S["go_ev"], 16)
            g.wait_ge(S["gss"], 16)
            mixer_rows(1)
            dispatch(1)
            moe(1)
            g.wait_ge(S["outst"], 16 * LT)


_INS = ["x", "c", "ctx", "c_ctx", "ada_w", "ada_b", "ln_g", "ln_b", "attn_w_qkv", "attn_w_o", "attn_lambda", "attn_subln_g",
        "gla_w_in", "gla_wg_down", "gla_wg_up", "gla_bg", "gla_norm_g", "gla_w_o", "router_w", "router_b",
        "moe_w_gate", "moe_w_up", "moe_w_down"]


def kernel(**inputs):
    from concourse import bacc
    from concourse.bass_utils import run_bass_kernel_spmd

    nc = bacc.Bacc("TRN2", target_bir_lowering=False, num_devices=1)
    arrays, aps = {}, {}
    for name in _INS:
        arr = np.ascontiguousarray(inputs[name])
        arrays[f"in_{name}"] = arr
        aps[name] = nc.dram_tensor(f"in_{name}", arr.shape, mybir.dt.from_np(arr.dtype), kind="ExternalInput").ap()
    table = constants()
    arrays["constants"] = table
    const_ap = nc.dram_tensor("constants", table.shape, F32, kind="ExternalInput").ap()
    out = nc.dram_tensor("out", (1, SEQ, D), F32, kind="ExternalOutput").ap()
    build(nc, aps, out, const_ap)
    r = run_bass_kernel_spmd(nc, [arrays], core_ids=[0])
    return r.results[0]["out"]
```

```python
from contextlib import ExitStack
import math

import numpy as np
import concourse.bass as bass
from concourse import mybir

ALU = mybir.AluOpType
ACT = mybir.ActivationFunctionType
F32 = mybir.dt.float32
I32 = mybir.dt.int32
AX = mybir.AxisListType

P = 128
D = 1024
KC = D // P
SEQ, CTX = 512, 256
TOK = SEQ + CTX
LT, CT = SEQ // P, CTX // P
NT = LT + CT
ALPHA = 4.0 ** 0.25
EPS = 1e-5
HEADS, HD = 8, 64
GRID_W, ROT = 64, HD // 4
GH, DK, DV = 4, 128, 256
RANK = 16
TAU = 16.0
NE, NG, EPG = 16, 4, 4
FE = D // 2
LAMBDA0 = 0.8 - 0.6 * math.exp(0.0)
SLOT = 4096
RING = 6
MAXB = [(TOK * 2 + NE * (P - 1)) // P, (SEQ * 2 + NE * (P - 1)) // P]
NBMAX = TOK // P
TILES = [NT, LT]

STREAM = [("ada", 0, j) for j in range(4)]
STREAM += [("qkv", 0, 2 * part + hg) for hg in range(2) for part in range(3)]
STREAM += [("ada", 0, j) for j in range(4, 10)]
STREAM += [("wo", 0, 0), ("wo", 0, 1)]
STREAM += [("ada", 0, 10), ("ada", 0, 11)]
STREAM += [("ada", 1, j) for j in range(12)]
MOE0 = len(STREAM)
STREAM += [("moe", 0, i) for i in range(3 * NE)]
GLA0 = len(STREAM)
STREAM += [("gla", 1, j) for j in range(6)]
STREAM += [("gap", 1, 0), ("gap", 1, 1)]
STREAM += [("wo", 1, 0), ("wo", 1, 1)]
MOE1 = len(STREAM)
STREAM += [("moe", 1, i) for i in range(3 * NE)]
MOEBASE = [MOE0, MOE1]
ADA_ITEMS = [p for p, it in enumerate(STREAM) if it[0] == "ada"]
PLAIN = [p for p, it in enumerate(STREAM) if it[0] not in ("moe", "gap")]


def loads(p):
    return sum(STREAM[q][0] != "gap" for q in range(p % RING, p + 1, RING))


LAYER0_COUNTS = {
    "on_rdy": 6,
    "turn_mm": 12,
    "turn_ev": 12,
    "turn_use": 12,
    "y_mm": 6,
    "z_done": 6,
    "bn": 6,
    "ln_sqrt": 6,
    "ln_n": 6,
    "hf_rdy": 6,
    "aff": 1,
    "y_all": 1,
    "scat": 192,
    "slot_ld": 16,
    "mask": 1,
    "rank_mm": 1,
    "xfin": 6,
    "z2_done": 6,
    "bn2": 6,
    "ln2_sqrt": 6,
    "ln2_n": 6,
    "rows_ld": 16,
    "rows2_ld": 64,
    "rows3_ld": 64,
    "lgk": 64,
    "hf_st0": 48,
    "hf_st1": 48,
    "ya_ld0": 96,
    "ya_ld1": 96,
}


def after(l, name, v):
    return v + (LAYER0_COUNTS[name] if l else 0)


def constants():
    ident = np.eye(P, dtype=np.float32)
    rot = np.zeros((P, P), np.float32)
    for d in range(P):
        half = (d // ROT) % 2
        if half == 0:
            rot[d + ROT, d] = -1.0
        else:
            rot[d - ROT, d] = 1.0
    tri = np.triu(np.ones((P, P), np.float32), 1)
    ones = np.ones((P, P), np.float32)
    pos = np.arange(SEQ)
    inv = 10000.0 ** (-np.arange(ROT, dtype=np.float32) / ROT)
    inv = inv.astype(np.float32)
    ang_r = (pos // GRID_W).astype(np.float32)[:, None] * inv
    ang_c = (pos % GRID_W).astype(np.float32)[:, None] * inv
    ang = np.concatenate([ang_r, ang_r, ang_c, ang_c], -1)
    ang = np.concatenate([ang, ang], -1).T
    cs = np.stack([np.cos(ang), np.sin(ang)], 1).astype(np.float32).reshape(P, 2 * SEQ)
    i = np.arange(P)
    masks = [2.0 * ident]
    for lv in range(7):
        masks.append((((i[:, None] ^ i[None, :]) >> lv) == 1).astype(np.float32))
    masks = np.stack(masks, 1).reshape(P, 8 * P).astype(np.float32)
    row = np.zeros((P, 64), np.float32)
    row[:, 0:NBMAX] = np.arange(NBMAX) * P
    row[:, 8:8 + 28] = np.arange(28)
    row[:, 40:56] = np.where(np.arange(16) % 2 == 0, 1.0, -1.0)
    row[:, 56:56 + NT] = np.arange(NT)[None, :] * P + i[:, None]
    return np.concatenate([ident, rot, tri, ones, row, cs, masks], 1).astype(np.float32)


OFF = [(0, 1), (2, 3), (0, 2), (0, 3), (1, 2), (1, 3), (1, 0), (3, 2), (2, 0), (2, 1), (3, 0), (3, 1)]
NCONST = 4 * P + 64 + 2 * SEQ + 8 * P


def build(nc, a, out, consts, dumps=None):
    dumps = dumps or {}
    stack = ExitStack()
    with stack:
        def sb(name, cols, dt=F32, parts=P):
            return stack.enter_context(nc.sbuf_tensor(name, [parts, cols], dt))

        def sem(name):
            return stack.enter_context(nc.semaphore(name))

        def dram(name, shape, dt=F32):
            return nc.dram_tensor(name, shape, dt, kind="Internal").ap()

        ring = sb("ring", RING * SLOT)
        A0, A1, A2, A3 = (sb(f"arena{i}", NT * D) for i in range(4))
        cst = sb("cst", 4 * P + 64)
        cs = sb("cos_sin_or_masks", 8 * P)
        U = sb("union_small", 1792)
        sm = sb("small", 368)
        idx32 = sb("idx32", 192, I32)
        bank = [stack.enter_context(nc.psum_tensor(f"bank{i}", [P, 512], F32)) for i in range(8)]

        ident, rot, tri, ones = (cst[:, i * P:(i + 1) * P] for i in range(4))
        rowc = cst[:, 4 * P:4 * P + 64]
        kmul, jrow, sgn, tidf = rowc[:, 0:NBMAX], rowc[:, 8:36], rowc[:, 40:56], rowc[:, 56:56 + NT]

        modd = dram("mod_rows", [2, 2, 6 * D])
        hfd = [dram(f"ffn_in{l}", [TILES[l] * P, D]) for l in range(2)]
        ypad = [dram(f"expert_out{l}", [(MAXB[l] + 2) * P, D]) for l in range(2)]
        tokd = [dram(f"slot_token{l}", [P * 28, 1], I32) for l in range(2)]
        xsave = dram("x_between_layers", [SEQ, D])

        cur = [0]

        def take(n):
            cur[0] += n
            return sm[:, cur[0] - n:cur[0]]

        c_raw, c_act = take(16), take(16)
        modc = [take(32) for _ in range(2)]
        st_a = [take(16) for _ in range(4)]
        lam4, nlam = take(4), take(1)
        ss = take(48)
        rstd = take(48)
        bst, mv, sd = take(12), take(2), take(2)
        W2 = take(12)
        bgc = take(8)
        epst = take(1)
        rb = take(16)
        bstot, etot = take(24), take(12)
        ctot = [8, 22]
        routed = [idx32[:, 0:12], idx32[:, 12:24]]
        destI, addrI = routed
        tidI = idx32[:, 24:30]
        idxcur = idx32[:, 30:31]
        zeroI = idx32[:, 31:32]
        slotI = idx32[:, 32:60]
        inclI = idx32[:, 60:76]
        peI = idx32[:, 76:160]
        countI = idx32[:, 188:190]
        zfill = idx32[:, 160:188]

        def slot(p):
            s = p % RING
            return ring[:, s * SLOT:(s + 1) * SLOT]

        ring_ld = [sem(f"ring_loaded{i}") for i in range(RING)]
        ring_used = sem("ring_used")
        const_ld, x_ld, silu_c = sem("const_loaded"), sem("x_loaded"), sem("silu_c_done")
        ada_row = sem("ada_row_ready")
        adab_ld = [sem(f"ada_bias_loaded{i}") for i in range(2)]
        ada_st = [sem(f"ada_row_stored{i}") for i in range(2)]
        modc_ld = [sem(f"mod_cols_loaded{l}") for l in range(2)]
        xt_mm = [sem(f"x_transposed{l}") for l in range(2)]
        ht_l = [sem(f"h_latent_ready{l}") for l in range(2)]
        ht_c = [sem(f"h_context_ready{l}") for l in range(2)]
        S = {}
        for n in ("proj_mm", "qraw", "rot_mm", "rope_cos", "rope_done", "ctx_ev", "v_mm", "v_ev",
                  "sc_mm", "sc_half", "maxed", "exped", "pmix", "at_mm", "at_ev_lo", "at_ev_hi", "o_mm", "o_ev",
                  "lam_ld", "lam_a", "lam_b", "rms_sqrt", "dve", "act", "pool",
                  "cs_ld", "xres_ld", "routerw_ld",
                  "gq_mm", "gq_ev", "gk_mm", "gk_ev", "gv_mm", "gv_ev", "gd_mm", "gd_ev", "gr_ev",
                  "gw_ld", "gu_mm", "ls_exp", "ls_done", "lv_arg", "lv_exp", "lv_mul", "lv_mm", "lv_ev",
                  "tl_exp", "tl_done", "kc_exp", "kc_done", "kc_mm", "kc_ev", "st_mm", "st_ev", "off_mm", "off_ev", "go_mm", "go_ev",
                  "gss", "wz", "pool_ld", "passed", "bg_ld", "xsave_st", "mask_ld", "init", "outst"):
            S[n] = sem(n)
        L = [{n: sem(n) for n in LAYER0_COUNTS}]
        L.append(dict(L[0]))
        for l in range(2):
            L[l].update({n: sem(f"{n}{l}") for n in (
                "tbl", "tok_zero", "idx", "gath",
                "xt", "xt_a", "xt_v", "g_mm", "u_mm", "silu", "gmul", "gt_mm", "gt_ev", "yd_mm", "y_a", "y_v", "y_st", "yfill")})
        block = stack.enter_context(nc.Block())

        hT = A0[:, :].rearrange("p (c t) -> p c t", c=KC)
        xst = A1[:, :].rearrange("p (t n) -> p t n", t=NT)
        X = [A2[:, :].rearrange("p (t n) -> p t n", t=NT), A1[:, :].rearrange("p (t n) -> p t n", t=NT)]
        qT = A2[:, 0:4 * TOK].rearrange("p (h t) -> p h t", h=4)
        kT = A2[:, 4 * TOK:8 * TOK].rearrange("p (h t) -> p h t", h=4)
        vA = A3[:, 0:NT * 512].rearrange("p (t n) -> p t n", t=NT)
        PR = [A3[:, NT * 512 + i * 2 * TOK:NT * 512 + (i + 1) * 2 * TOK].rearrange("p (m k) -> p m k", m=2) for i in range(2)]
        qraw = [A3[:, NT * 512 + i * 512:NT * 512 + (i + 1) * 512] for i in range(2)]
        rtmp = A3[:, NT * 512 + 1024:NT * 512 + 1536]
        aT = [U[:, i * TOK:(i + 1) * TOK].rearrange("p (k q) -> p k q", k=NT) for i in range(2)]
        squares = U[:, 2 * TOK:2 * TOK + P]
        oall = A1[:, :].rearrange("p (t n) -> p t n", t=NT)
        adat = [A3[0:2, 4096 + i * 512:4096 + (i + 1) * 512] for i in range(2)]
        adab = [A3[0:2, 5120 + i * 512:5120 + (i + 1) * 512] for i in range(2)]
        oT = [A0[:, i * D:(i + 1) * D].rearrange("p (c t) -> p c t", c=KC) for i in range(2)]
        HF = [A0[:, (2 + i) * D:(3 + i) * D] for i in range(2)]
        scf, shf = A0[:, 4 * D:5 * D], A0[:, 5 * D:6 * D]
        gm, lng, lnb, Z = (A3[:, i * D:(i + 1) * D] for i in range(4))
        lamv = A3[:, 0:4 * HD]
        RT = A1[:, 4096:6144]
        xrow = A0[:, 0:D]
        xT = A0[:, D:2 * D].rearrange("p (c t) -> p c t", c=KC)
        gsil, gate = A0[:, 2 * D:2 * D + FE], A0[:, 2 * D + FE:3 * D]
        gT = A0[:, 3 * D:3 * D + FE].rearrange("p (c t) -> p c t", c=4)
        ysb = A0[:, 4 * D:5 * D]
        gbank = [bank[2][:, 0:256], bank[7][:, 0:256]]
        gtbank = [bank[4][:, 0:256], bank[2][:, 256:512]]
        YB = [A1, A2]
        yab = [[YB[l][:, (2 * i + k) * D:(2 * i + k + 1) * D] for i in range(2) for k in range(2)] for l in range(2)]
        normg = [U[:, 256:256 + P], U[:, 256:256 + DV]]
        rwt = U[:, 0:128].rearrange("p (c n) -> p c n", c=KC)
        V1 = A1[:, :].rearrange("p (t n) -> p t n", t=NT)
        R1 = A2[:, 0:LT * D].rearrange("p (t n) -> p t n", t=LT)
        QK = A3[:, 0:4096].rearrange("p (h k t) -> p h k t", h=GH, k=2)
        KX = A3[:, 4096:5120].rearrange("p (h t) -> p h t", h=GH)
        ST = A3[:, 5120:5632].rearrange("p (d e) -> p d e", d=2)
        KXT = A3[:, 5632:6144].rearrange("p (d t e) -> p d t e", d=2, t=2)
        W0, W1 = slot(GLA0 + 6), slot(GLA0 + 7)
        GB = [W[:, 0:2 * TOK].rearrange("p (d t) -> p d t", d=2) for W in (W0, W1)]
        LS = W0[:, 1536:3072].rearrange("p (d t) -> p d t", d=2)
        LVB = [x.rearrange("p (k t) -> p k t", k=2) for x in (W0[:, 3072:4096], W1[:, 1536:2560], W1[:, 2560:3584])]
        SD = [x.rearrange("p (b t) -> p b t", b=4) for x in (W1[:, 3584:4096], U[:, TOK + 512:TOK + 1024])]
        SO = A0[:, 0:1536].rearrange("p (k t) -> p k t", k=12)
        VARO = A0[:, 1536:2048].rearrange("p (k t) -> p k t", k=4)
        VARD = [A0[:, 2048 + 768 * i:2816 + 768 * i].rearrange("p (k t) -> p k t", k=6) for i in range(2)]
        KXG = A0[:, 3584:4096].rearrange("p (d t) -> p d t", d=2)
        TL = [A2[:, 4096:6144].rearrange("p (k t) -> p k t", k=4), A0[:, 4096:6144].rearrange("p (k t) -> p k t", k=4)]
        gdT = U[:, 0:TOK]
        wup = U[:, TOK:TOK + 512]
        wdn = U[:, TOK + 512:TOK + 1024].rearrange("p (c r) -> p c r", c=KC)
        cosT, sinT = cs[:, 0:SEQ], cs[:, SEQ:2 * SEQ]
        maskv = cs[:, :].rearrange("p (k t) -> p k t", k=8)

        def bcast_row(ap_1d, n):
            return ap_1d.unsqueeze(0).to_broadcast([P, n])

        def src_of(p):
            kind, l, j = STREAM[p]
            if kind == "ada":
                return a["ada_w"][l].rearrange("(p c) n -> p c n", c=KC)[:, :, j * 512:(j + 1) * 512]
            if kind == "qkv":
                return a["attn_w_qkv"][0].rearrange("(p c) n -> p c n", c=KC)[:, :, j * 512:(j + 1) * 512]
            if kind == "gla":
                return a["gla_w_in"][0].rearrange("(p c) n -> p c n", c=KC)[:, :, j * 512:(j + 1) * 512]
            w = a["attn_w_o"][0] if l == 0 else a["gla_w_o"][0]
            return w.rearrange("(p c) n -> p c n", c=KC)[:, :, j * 512:(j + 1) * 512]

        def used_value(p):
            return PLAIN.index(p) + 1

        vr_tiles = [(j, t) for j, tiles in ((2, NT), (3, NT), (4, LT), (5, LT)) for t in range(tiles)]
        VR_CUT = [len(vr_tiles) * k // 8 for k in range(9)]

        def attn_units():
            return [(hb, t) for hb in range(4) for t in range(NT)]

        def turns(l):
            n, q = TILES[l], []
            for t in range(n):
                q.append(("o", t))
                if t >= 2:
                    q.append(("r", t - 2))
            return q + [("r", n - 2), ("r", n - 1)]

        @block.sync
        def _(sp):
            sp.dma_start(cst[:, :], consts[:, 0:4 * P + 64]).then_inc(const_ld, 16)
            sp.dma_start(c_raw[:, 0:8], a["c"][0].rearrange("(p c) -> p c", c=KC)).then_inc(const_ld, 16)
            sp.dma_start(c_raw[:, 8:16], a["c_ctx"].rearrange("(p c) -> p c", c=KC)).then_inc(const_ld, 16)

            def load_bias(n):
                _, l, j = STREAM[ADA_ITEMS[n]]
                if n >= 2:
                    sp.wait_ge(ada_row, n - 1)
                sp.dma_start(adab[n % 2], a["ada_b"][l][j * 512:(j + 1) * 512].unsqueeze(0).to_broadcast([2, 512])
                             ).then_inc(adab_ld[n % 2], 16)

            def store_row(n):
                _, l, j = STREAM[ADA_ITEMS[n]]
                sp.wait_ge(ada_row, n + 1)
                sp.dma_start(modd[l][:, j * 512:(j + 1) * 512], adat[n % 2]).then_inc(ada_st[n % 2], 16)

            def issue(p):
                if p >= RING:
                    q = p - RING
                    kind, l, j = STREAM[q]
                    if kind == "moe":
                        e = j // 3
                        if j % 3 == 0:
                            v = sp.value_load(inclI[0:1, e:e + 1], min_val=1, max_val=64)
                            sp.wait_ge(L[l]["yd_mm"], v)
                    else:
                        sp.wait_ge(ring_used, used_value(q))
                        if kind == "ada":
                            n = ADA_ITEMS.index(q)
                            store_row(n)
                            if n >= 4 or n < 2:
                                load_bias(n + 2)
                sp.dma_start(slot(p), src_of(p) if STREAM[p][0] != "moe" else None).then_inc(ring_ld[p % RING], 16)

            def issue_expert(l, e_static, e):
                p = MOEBASE[l] + 3 * e_static
                gw = a["moe_w_gate"][l].rearrange("e (p c) n -> p e (c n)", c=KC)
                uw = a["moe_w_up"][l].rearrange("e (p c) n -> p e (c n)", c=KC)
                dw = a["moe_w_down"][l].rearrange("e (c p) n -> p e c n", c=4)
                for i, w in enumerate((uw, gw)):
                    src = w[:, bass.ds(e, 1), :].rearrange("p e n -> p (e n)")
                    sp.dma_start(slot(p + i), src).then_inc(ring_ld[(p + i) % RING], 16)
                src = dw[:, bass.ds(e, 1), :, :].rearrange("p e c n -> p (e c) n")
                sp.dma_start(slot(p + 2).rearrange("p (c n) -> p c n", c=4), src).then_inc(ring_ld[(p + 2) % RING], 16)

            load_bias(0)
            load_bias(1)
            for p in range(RING):
                issue(p)
                if p == 1:
                    for t in range(NT):
                        src = a["x"][0][t * P:(t + 1) * P, :] if t < LT else a["ctx"][0][(t - LT) * P:(t - LT + 1) * P, :]
                        sp.dma_start(xst[:, t, :], src).then_inc(x_ld, 16)
                    sp.dma_start(cs[:, :], consts[:, 4 * P + 64:4 * P + 64 + 2 * SEQ]).then_inc(S["cs_ld"], 16)
            for l in range(2):
                for p in range(RING if l == 0 else GLA0, MOEBASE[l]):
                    if STREAM[p][0] != "gap":
                        issue(p)
                    if p == ADA_ITEMS[4] + RING - 1:
                        sp.wait_ge(S["o_ev"], 48)
                        load_bias(4)
                        load_bias(5)
                    if p == GLA0:
                        sp.wait_ge(S["rope_done"], 16)
                        sp.dma_start(cs[:, :], consts[:, 4 * P + 64 + 2 * SEQ:NCONST]).then_inc(S["mask_ld"], 16)
                for e in range(2):
                    for i in range(3):
                        q = MOEBASE[l] + 3 * e + i - RING
                        if STREAM[q][0] == "gap":
                            sp.wait_ge(S["go_mm"], 16)
                            continue
                        sp.wait_ge(ring_used, used_value(q))
                        if STREAM[q][0] == "ada":
                            n = ADA_ITEMS.index(q)
                            store_row(n)
                            if n + 2 < len(ADA_ITEMS):
                                load_bias(n + 2)
                    issue_expert(l, e, e)
                sp.wait_ge(L[l]["tbl"], 1)
                with sp.Fori(1, NE // 2) as m:
                    for par in range(2):
                        v = sp.value_load(inclI[0:1, bass.ds(2 * m - 2 + par, 1)], min_val=1, max_val=64)
                        sp.wait_ge(L[l]["yd_mm"], v)
                        issue_expert(l, 2 + par, 2 * m + par)

        @block.tensor
        def _(pe):
            def ring_wait(p):
                pe.wait_ge(ring_ld[p % RING], 16 * loads(p))

            def ada(n):
                p = ADA_ITEMS[n]
                w = slot(p).rearrange("p (c n) -> p c n", c=KC)
                ring_wait(p)
                if n == 0:
                    pe.wait_ge(silu_c, 1)
                else:
                    pe.wait_ge(ada_row, n)
                cw = c_act.rearrange("p (s c) -> p c s", s=2)
                for c in range(KC):
                    mm = pe.matmul(bank[7][0:2, :], cw[:, c, :], w[:, c, :], start=(c == 0), stop=(c == KC - 1))
                mm.then_inc(ring_used, 1)

            def transpose_x(l):
                nl = X[0] if l else xst
                for c in range(KC):
                    if c >= 3:
                        pe.wait_ge(ht_l[l], c - 2)
                        pe.wait_ge(ht_c[l], c - 2)
                    for t in range(NT):
                        b = bank[c % 3] if t < LT else bank[3 + c % 3]
                        o = (t % LT) * P
                        mm = pe.transpose(b[:, o:o + P], nl[:, t, :].rearrange("p (q c) -> p c q", c=KC)[:, c, :], ident)
                    mm.then_inc(xt_mm[l], 1)

            pe.wait_ge(const_ld, 48)
            for n in range(4):
                ada(n)
            pe.wait_ge(x_ld, 16 * NT)
            transpose_x(0)
            pe.wait_ge(ht_l[0], KC)
            pe.wait_ge(ht_c[0], KC)

            k_blk = 0
            for hg in range(2):
                base = 4 + 3 * hg
                if hg:
                    pe.wait_ge(S["o_ev"], NT * 4 * hg)

                def rotate(i):
                    pe.wait_ge(S["qraw"], i + 1)
                    if i >= 2:
                        pe.wait_ge(S["rope_done"], i - 1)
                    pe.matmul(bank[4 + i % 2][:, :], rot, qraw[i % 2], start=True, stop=True).then_inc(S["rot_mm"], 1)

                for part in range(2):
                    p = base + part
                    ring_wait(p)
                    w = slot(p).rearrange("p (c n) -> p c n", c=KC)
                    for hb in range(4):
                        i = 8 * hg + 4 * part + hb
                        if i >= 2:
                            pe.wait_ge(S["qraw"], i - 1)
                            pe.wait_ge(S["ctx_ev"], i - 1)
                        for c in range(KC):
                            pe.matmul(bank[i % 2][:, :], w[:, c, hb * P:(hb + 1) * P], hT[:, c, 0:SEQ],
                                      start=(c == 0), stop=(c == KC - 1))
                        for c in range(KC):
                            mm = pe.matmul(bank[2 + i % 2][:, 0:CTX], w[:, c, hb * P:(hb + 1) * P], hT[:, c, SEQ:TOK],
                                           start=(c == 0), stop=(c == KC - 1))
                        mm.then_inc(S["proj_mm"], 1)
                        if i % 8:
                            rotate(i - 1)
                    pe.wait_ge(S["proj_mm"], 8 * hg + 4 * part + 4)
                    pe.sem_inc(ring_used, 1)
                rotate(8 * hg + 7)
                p = base + 2
                ring_wait(p)
                w = slot(p).rearrange("p (c n) -> p c n", c=KC)
                for t in range(NT):
                    n = NT * hg + t
                    if t >= 2:
                        pe.wait_ge(S["v_ev"], n - 1)
                    for c in range(KC):
                        mm = pe.matmul(bank[6 + t % 2][:, :], hT[:, c, t * P:(t + 1) * P], w[:, c, :],
                                       start=(c == 0), stop=(c == KC - 1))
                    mm.then_inc(S["v_mm"], 1)
                pe.wait_ge(S["v_mm"], NT * (hg + 1))
                pe.sem_inc(ring_used, 1)

                units = attn_units()
                u0 = len(units) * hg
                pe.wait_ge(S["rope_done"], 8 * (hg + 1))
                pe.wait_ge(S["ctx_ev"], 8 * (hg + 1))
                pe.wait_ge(S["v_ev"], NT * (hg + 1))

                def scores(k):
                    hb, t = units[k]
                    u = u0 + k
                    b0, b1, b2 = (bank[3 * (k % 2) + j] for j in range(3))
                    if k >= 2:
                        pe.wait_ge(S["exped"], u - 1)
                    q = [qT[64 * m:64 * m + 64, hb, t * P:(t + 1) * P] for m in range(2)]
                    kl = [kT[64 * m:64 * m + 64, hb, 0:SEQ] for m in range(2)]
                    kc = [kT[64 * m:64 * m + 64, hb, SEQ:TOK] for m in range(2)]
                    if t < LT:
                        pe.matmul(b2[:, 0:CTX], q[0], kc[0], start=True, stop=True).then_inc(S["sc_half"], 1)
                        pe.matmul(b0[:, :], q[0], kl[0], start=True, stop=True)
                        pe.matmul(b1[:, :], q[1], kl[1], start=True, stop=True)
                        pe.wait_ge(S["sc_half"], LT * (u // NT) + t + 1)
                        mm = pe.matmul(b2[:, CTX:2 * CTX], q[1], kc[1], start=True, stop=True)
                    else:
                        pe.matmul(b0[:, 0:CTX], q[0], kc[0], start=True, stop=True)
                        mm = pe.matmul(b1[:, 0:CTX], q[1], kc[1], start=True, stop=True)
                    mm.then_inc(S["sc_mm"], 1)

                def turn_probs(k):
                    hb, t = units[k]
                    u = u0 + k
                    pe.wait_ge(S["pmix"], u + 1)
                    if t < LT:
                        if u >= 1:
                            pe.wait_ge(S["at_ev_lo"], u)
                        for kb in range(4):
                            mm = pe.transpose(bank[6][:, kb * P:(kb + 1) * P], PR[k % 2][:, 0, kb * P:(kb + 1) * P], ident)
                        mm.then_inc(S["at_mm"], 1)
                    else:
                        pe.sem_inc(S["at_mm"], 1)
                    if u >= 1:
                        pe.wait_ge(S["o_ev"], u)
                    for kb in (4, 5):
                        mm = pe.transpose(bank[7][:, (kb - 4) * P:(kb - 3) * P], PR[k % 2][:, 0, kb * P:(kb + 1) * P], ident)
                    mm.then_inc(S["at_mm"], 1)

                def av(k):
                    hb, t = units[k]
                    u = u0 + k
                    pe.wait_ge(S["at_ev_lo"], u + 1)
                    pe.wait_ge(S["at_ev_hi"], u + 1)
                    blocks = list(range(NT)) if t < LT else [4, 5]
                    for kb in blocks:
                        mm = pe.matmul(bank[7][:, 256:384], aT[k % 2][:, kb, :], vA[:, kb, hb * P:(hb + 1) * P],
                                       start=(kb == blocks[0]), stop=(kb == blocks[-1]))
                    mm.then_inc(S["o_mm"], 1)

                scores(0)
                scores(1)
                for k in range(len(units)):
                    turn_probs(k)
                    if k + 2 < len(units):
                        scores(k + 2)
                    av(k)

            def mixer_out(l):
                q = turns(l)
                n = TILES[l]
                w0 = [p for p, it in enumerate(STREAM) if it[0] == "wo" and it[1] == l]
                wv = [slot(p).rearrange("p (c n) -> p c n", c=KC) for p in w0]
                src = [oall, R1][l]

                def turn(k):
                    kind, t = q[k]
                    if k >= 1:
                        pe.wait_ge(L[l]["turn_ev"], after(l, "turn_ev", k))
                    if kind == "o":
                        pe.wait_ge(L[l]["on_rdy"], after(l, "on_rdy", t + 1))
                        s = src[:, t, :]
                    else:
                        pe.wait_ge(L[l]["hf_rdy"], after(l, "hf_rdy", t + 1))
                        s = HF[t % 2]
                    for c in range(KC):
                        mm = pe.transpose(bank[2 + c // 4][:, (c % 4) * P:(c % 4 + 1) * P],
                                          s.rearrange("p (q c) -> p c q", c=KC)[:, c, :], ident)
                    mm.then_inc(L[l]["turn_mm"], 1)

                def use(k):
                    kind, t = q[k]
                    pe.wait_ge(L[l]["turn_ev"], after(l, "turn_ev", k + 1))
                    if kind == "o":
                        if t == 0:
                            ring_wait(w0[0])
                            ring_wait(w0[1])
                        if t >= 2:
                            pe.wait_ge(L[l]["z_done"], after(l, "z_done", t - 1))
                        for h in range(2):
                            for c in range(KC):
                                mm = pe.matmul(bank[4 * (t % 2) + h][:, :], oT[k % 2][:, c, :], wv[h][:, c, :],
                                               start=(c == 0), stop=(c == KC - 1))
                        mm.then_inc(L[l]["y_mm"], 1)
                        pe.wait_ge(L[l]["y_mm"], after(l, "y_mm", t + 1))
                        pe.sem_inc(L[l]["turn_use"], 1)
                        if t == n - 1:
                            pe.sem_inc(ring_used, 2)
                    else:
                        if t == 0:
                            pe.wait_ge(S["routerw_ld"], 16 * (l + 1))
                        for c in range(KC):
                            mm = pe.matmul(bank[6][:, t * 16:(t + 1) * 16], oT[k % 2][:, c, :], rwt[:, c, :],
                                           start=(c == 0), stop=(c == KC - 1), skip_group_check=True)
                        mm.then_inc(L[l]["turn_use"], 1)

                turn(0)
                for k in range(len(q)):
                    if k + 1 < len(q):
                        turn(k + 1)
                    use(k)

            def ranks(l):
                n = TILES[l]
                Mv, PM = RT[:, 0:n * 16], RT[:, 96:96 + n * 16]
                tot = RT[:, 96 + n * 16:112 + n * 16]
                pe.wait_ge(L[l]["mask"], after(l, "mask", 1))
                pe.matmul(bank[6][:, 0:n * 16], tri, Mv, start=True, stop=False, skip_group_check=True)
                pe.matmul(bank[6][:, 0:n * 16], ones, PM, start=False, stop=True, skip_group_check=True)
                pe.matmul(bank[5][:, 0:16], ones, tot, start=True, stop=True).then_inc(L[l]["rank_mm"], 1)

            def moe(l):
                E = L[l]
                base = MOEBASE[l]

                def turn(j, first=False):
                    pe.wait_ge(E["gath"], 16 * (j + 1))
                    if not first:
                        pe.wait_ge(E["xt_a"], j)
                        pe.wait_ge(E["xt_v"], j)
                    for c in range(KC):
                        mm = pe.transpose(bank[c // 4][:, (c % 4) * P:(c % 4 + 1) * P],
                                          xrow.rearrange("p (q c) -> p c q", c=KC)[:, c, :], ident)
                    mm.then_inc(E["xt"], 1)

                pe.wait_ge(E["tbl"], 1)
                pe.sem_inc(E["yd_mm"], 1)
                nb = pe.value_load(inclI[0:1, NE - 1:NE], min_val=2, max_val=MAXB[l] + 1)
                turn(0, True)
                sl = [(base + i) % RING for i in range(3)]
                uses = [loads(base + i) - 1 for i in range(3)]
                uses1 = [loads(base + 3 + i) - 1 for i in range(3)]
                with pe.Fori(0, MAXB[l]) as j:
                    with pe.If(j + 1 < nb):
                        par = pe.value_load(peI[0:1, bass.ds(3 * j, 1)], min_val=0, max_val=1)
                        h0 = pe.value_load(peI[0:1, bass.ds(3 * j + 1, 1)], min_val=0, max_val=16 * 17)
                        h1 = pe.value_load(peI[0:1, bass.ds(3 * j + 2, 1)], min_val=0, max_val=16 * 17)

                        def weights(i, cols):
                            step = 3 * SLOT if sl[i] < 3 else -3 * SLOT
                            pe.wait_ge(ring_ld[sl[i]], h0 + 16 * uses[i])
                            pe.wait_ge(ring_ld[(sl[i] + 3) % RING], h1 + 16 * uses1[i])
                            return lambda c, o, n: ring[:, bass.ds(sl[i] * SLOT + par * step + c * cols + o, n)]

                        pe.wait_ge(E["xt_a"], j + 1)
                        pe.wait_ge(E["xt_v"], j + 1)
                        w = weights(0, FE)
                        for c in range(KC):
                            mm = pe.matmul(bank[3][:, :], xT[:, c, :], w(c, 0, FE), start=(c == 0), stop=(c == KC - 1))
                        mm.then_inc(E["u_mm"], 1)
                        w = weights(1, FE)
                        for h in range(2):
                            for c in range(KC):
                                mm = pe.matmul(gbank[h], xT[:, c, :], w(c, h * 256, 256), start=(c == 0), stop=(c == KC - 1))
                            mm.then_inc(E["g_mm"], 1)

                        def turn_gate(h):
                            pe.wait_ge(E["gmul"], 2 * j + h + 1)
                            for c in (2 * h, 2 * h + 1):
                                mm = pe.transpose(gtbank[h][:, (c % 2) * P:(c % 2 + 1) * P], gate[:, c * P:(c + 1) * P], ident)
                            mm.then_inc(E["gt_mm"], 1)

                        turn_gate(0)
                        turn(j + 1)
                        turn_gate(1)
                        w = weights(2, D)
                        pe.wait_ge(E["y_a"], j + 1)
                        pe.wait_ge(E["y_v"], j + 1)
                        for h in range(2):
                            pe.wait_ge(E["gt_ev"], 2 * j + h + 1)
                            for o in range(2):
                                for c in (2 * h, 2 * h + 1):
                                    mm = pe.matmul(bank[5 + o][:, :], gT[:, c, :], w(c, o * 512, 512), start=(c == 0), stop=(c == 3),
                                                   skip_group_check=True)
                        mm.then_inc(E["yd_mm"], 1)

            pe.wait_ge(S["o_ev"], 48)
            for n in range(4, 10):
                ada(n)
            mixer_out(0)
            for n in (10, 11):
                ada(n)
            ranks(0)
            for n in range(12, 24):
                ada(n)
            moe(0)

            pe.wait_ge(L[0]["xfin"], NT)
            transpose_x(1)
            pe.wait_ge(ht_l[1], KC)
            pe.wait_ge(ht_c[1], KC)
            for i in range(8):
                part, h = divmod(i, 4)
                p = GLA0 + part
                if h == 0:
                    ring_wait(p)
                w = slot(p).rearrange("p (c n) -> p c n", c=KC)
                if i >= 2:
                    pe.wait_ge(S["gq_ev"], i - 1)
                for c in range(KC):
                    mm = pe.matmul(bank[i % 2][:, :], w[:, c, h * P:(h + 1) * P], hT[:, c, 0:SEQ], start=(c == 0), stop=(c == KC - 1))
                mm.then_inc(S["gq_mm"], 1)
                if part:
                    if h >= 2:
                        pe.wait_ge(S["gk_ev"], h - 1)
                    for c in range(KC):
                        mm = pe.matmul(bank[2 + i % 2][:, 0:CTX], w[:, c, h * P:(h + 1) * P], hT[:, c, SEQ:TOK],
                                       start=(c == 0), stop=(c == KC - 1))
                    mm.then_inc(S["gk_mm"], 1)
                if h == 3:
                    pe.wait_ge(S["gq_mm"], i + 1)
                    if part:
                        pe.wait_ge(S["gk_mm"], 4)
                    pe.sem_inc(ring_used, 1)
            pe.wait_ge(S["gw_ld"], 64)
            pe.wait_ge(S["wz"], 2)
            pe.wait_ge(S["gq_ev"], 8)
            for c in range(KC):
                pe.matmul(bank[0][0:64, :], wdn[:, c, :], hT[:, c, 0:SEQ], start=(c == 0), stop=(c == KC - 1))
            for c in range(KC):
                mm = pe.matmul(bank[1][0:64, 0:CTX], wdn[:, c, :], hT[:, c, SEQ:TOK], start=(c == 0), stop=(c == KC - 1))
            mm.then_inc(S["gd_mm"], 1)
            pe.wait_ge(S["gd_ev"], 1)
            pe.wait_ge(S["gk_ev"], 4)

            def project(n):
                j, t = vr_tiles[n]
                p = GLA0 + j
                if t == 0:
                    ring_wait(p)
                w = slot(p).rearrange("p (c n) -> p c n", c=KC)
                if n >= 2:
                    pe.wait_ge(S["gv_ev"], n - 1)
                for c in range(KC):
                    mm = pe.matmul(bank[6 + n % 2][:, :], hT[:, c, t * P:(t + 1) * P], w[:, c, :], start=(c == 0), stop=(c == KC - 1))
                mm.then_inc(S["gv_mm"], 1)
                if n + 1 == len(vr_tiles) or vr_tiles[n + 1][0] != j:
                    pe.wait_ge(S["gv_mm"], n + 1)
                    pe.sem_inc(ring_used, 1)

            def gates(h):
                if h:
                    pe.wait_ge(S["ls_done"], 3 * h)
                for d in range(2):
                    b0, b1 = bank[2 * d], bank[2 * d + 1]
                    w = wup[32 * d:32 * d + RANK, h * P:(h + 1) * P]
                    g = gdT[32 * d:32 * d + RANK, :]
                    pe.matmul(b0[:, :], w, g[:, 0:SEQ], start=True, stop=True)
                    pe.matmul(b1[:, 0:CTX], w, g[:, SEQ:TOK], start=True, stop=True).then_inc(S["gu_mm"], 1)

            def level(h, k):
                lv = 8 * h + k
                if lv >= 2:
                    pe.wait_ge(S["lv_ev"], lv - 1)
                if k:
                    pe.wait_ge(S["lv_mul"], 7 * h + k)
                src = QK[:, h] if k == 0 else LVB[(7 * h + k - 1) % 3]
                for b in range(4):
                    mm = pe.matmul(bank[4 + lv % 2][:, b * P:(b + 1) * P], src[:, 1, b * P:(b + 1) * P],
                                   src[:, 0, b * P:(b + 1) * P], start=True, stop=True, skip_group_check=True)
                mm.then_inc(S["lv_mm"], 1)

            def off_diagonal(h, g):
                if g == 0:
                    pe.wait_ge(S["tl_done"], h + 1)
                    if h:
                        pe.wait_ge(S["go_ev"], 4 * h)
                        pe.wait_ge(S["gss"], 4 * h)
                if g == 2:
                    pe.wait_ge(S["off_ev"], 3 * h + 1)
                tl = TL[h % 2]
                for n in range(4 * g, 4 * g + 4):
                    s, t = OFF[n]
                    far = abs(s - t) > 1 or {s, t} == {1, 2}
                    if s < t:
                        kk = VARO[:, 0, :] if (s == 0 and far) else tl[:, 1, s * P:(s + 1) * P]
                        qq = VARO[:, 1, :] if (t == 3 and far) else tl[:, 0, t * P:(t + 1) * P]
                    else:
                        kk = VARO[:, 2, :] if (s == 3 and far) else tl[:, 3, s * P:(s + 1) * P]
                        qq = VARO[:, 3, :] if (t == 0 and far) else tl[:, 2, t * P:(t + 1) * P]
                    mm = pe.matmul(bank[6 + g % 2][:, (n % 4) * P:(n % 4 + 1) * P], kk, qq, start=True, stop=True, skip_group_check=True)
                mm.then_inc(S["off_mm"], 1)

            def context_keys(h):
                pe.wait_ge(S["kc_done"], h + 1)
                pe.wait_ge(S["off_ev"], 3 * h + 2)
                for d in range(2):
                    for t in range(CT):
                        mm = pe.transpose(bank[7][:, (2 * d + t) * P:(2 * d + t + 1) * P], KXG[:, d, t * P:(t + 1) * P], ident)
                mm.then_inc(S["kc_mm"], 1)

            def context_states(h):
                pe.wait_ge(S["kc_ev"], h + 1)
                pe.wait_ge(S["off_ev"], 3 * h + 3)
                for d in range(2):
                    for t in range(CT):
                        mm = pe.matmul(bank[6][:, d * DV:(d + 1) * DV], KXT[:, d, t, :], V1[:, LT + t, h * DV:(h + 1) * DV],
                                       start=(t == 0), stop=(t == CT - 1), skip_group_check=True)
                mm.then_inc(S["st_mm"], 1)

            def outputs(h, t):
                if t == 0:
                    pe.wait_ge(S["lv_ev"], 8 * h + 8)
                    pe.wait_ge(S["st_ev"], h + 1)
                if t >= 2:
                    pe.wait_ge(S["go_ev"], 4 * h + t - 1)
                    pe.wait_ge(S["gss"], 4 * h + t - 1)
                b = bank[6 + t % 2]
                for s in range(LT):
                    lhs = SD[h % 2][:, t, :] if s == t else SO[:, OFF.index((s, t)), :]
                    pe.matmul(b[:, 0:DV], lhs, V1[:, s, h * DV:(h + 1) * DV], start=(s == 0), stop=False)
                qf = TL[h % 2][:, 0, 0:P] if t == 0 else VARD[h % 2][:, t - 1, :]
                qb = TL[h % 2][:, 2, 3 * P:4 * P] if t == 3 else VARD[h % 2][:, 3 + t, :]
                pe.matmul(b[:, 0:DV], qf, ST[:, 0, :], start=False, stop=False)
                pe.matmul(b[:, 0:DV], qb, ST[:, 1, :], start=False, stop=True).then_inc(S["go_mm"], 1)

            gates(0)
            for h in range(GH):
                for k in range(8):
                    level(h, k)
                    if k == 0 and h + 1 < GH:
                        gates(h + 1)
                    if h == 0:
                        for n in range(VR_CUT[k], VR_CUT[k + 1]):
                            project(n)
                    elif k < 4:
                        outputs(h - 1, k)
                    elif k == 4:
                        off_diagonal(h, 0)
                        off_diagonal(h, 1)
                    elif k == 5:
                        off_diagonal(h, 2)
                        context_keys(h)
                    elif k == 6:
                        context_states(h)
                if h == 0:
                    pe.wait_ge(S["gv_ev"], len(vr_tiles))
                    for g in range(3):
                        off_diagonal(h, g)
                    context_keys(h)
                    context_states(h)
            for t in range(LT):
                outputs(GH - 1, t)
            mixer_out(1)
            ranks(1)
            moe(1)

        @block.scalar
        def _(act):
            cnt = [0]

            def link(ins):
                cnt[0] += 1
                ins.then_inc(S["act"], 1)
                act.wait_ge(S["act"], cnt[0])

            act.wait_ge(const_ld, 48)
            act.activation(c_act, c_raw, ACT.Silu).then_inc(silu_c, 1)

            def context_h(l):
                act.wait_ge(modc_ld[l], 16 * 4)
                mvv = modc[l].rearrange("p (v s c) -> p v s c", v=2, s=2)
                for c in range(KC):
                    act.wait_ge(xt_mm[l], c + 1)
                    act.activation(hT[:, c, SEQ:TOK], bank[3 + c % 3][:, 0:CTX], ACT.Identity,
                                   bias=mvv[:, 0, 1, c:c + 1], scale=mvv[:, 1, 1, c:c + 1]).then_inc(ht_c[l], 1)

            act.wait_ge(S["lam_a"], 1)
            act.activation(lam4[:, 2:4], lam4[:, 0:2], ACT.Exp).then_inc(S["lam_b"], 1)
            context_h(0)
            for hg in range(2):
                if hg:
                    act.wait_ge(S["o_mm"], NT * 4 * hg)
                for i in range(8 * hg, 8 * hg + 8):
                    hb, dst = i % 4, (qT, kT)[(i % 8) // 4]
                    act.wait_ge(S["proj_mm"], i + 1)
                    if i >= 2:
                        act.wait_ge(S["rot_mm"], i - 1)
                        act.wait_ge(S["rope_cos"], i - 1)
                    act.activation(qraw[i % 2], bank[i % 2][:, :], ACT.Copy).then_inc(S["qraw"], 1)
                    act.activation(dst[:, hb, SEQ:TOK], bank[2 + i % 2][:, 0:CTX], ACT.Copy).then_inc(S["ctx_ev"], 1)
                for t in range(NT):
                    act.wait_ge(S["v_mm"], NT * hg + t + 1)
                    act.activation(vA[:, t, :], bank[6 + t % 2][:, :], ACT.Copy).then_inc(S["v_ev"], 1)
                units = attn_units()
                scale = float(HD) ** -0.5

                def probs(k):
                    hb, t = units[k]
                    u = len(units) * hg + k
                    b0, b1, b2 = (bank[3 * (k % 2) + j] for j in range(3))
                    st = st_a[k % 4]
                    if u >= 2:
                        act.wait_ge(S["at_mm"], 2 * u - 2)
                    if k == 0:
                        act.wait_ge(S["rope_done"], 8 * hg + 8)
                    act.wait_ge(S["maxed"], u + 1)
                    if t < LT:
                        for m in range(2):
                            act.activation(PR[k % 2][:, m, 0:SEQ], (b0, b1)[m][:, :], ACT.Exp, bias=st[:, 4 + m:5 + m],
                                           scale=scale, accum_out=st[:, 6 + 2 * m:7 + 2 * m])
                    for m in range(2):
                        src = b2[:, m * CTX:(m + 1) * CTX] if t < LT else (b0, b1)[m][:, 0:CTX]
                        ins = act.activation(PR[k % 2][:, m, SEQ:TOK], src, ACT.Exp,
                                             bias=st[:, 4 + m:5 + m], scale=scale, accum_out=st[:, 7 + 2 * m:8 + 2 * m])
                    ins.then_inc(S["exped"], 1)

                def out(k):
                    hb, t = units[k]
                    u = len(units) * hg + k
                    h = 4 * hg + hb
                    act.wait_ge(S["at_mm"], 2 * u + 2)
                    if u >= 2:
                        act.wait_ge(S["o_mm"], u - 1)
                    act.activation(aT[k % 2][:, 4:6, :], bank[7][:, 0:2 * P].rearrange("p (k q) -> p k q", k=2), ACT.Copy
                                   ).then_inc(S["at_ev_hi"], 1)

                def fin(k):
                    hb, t = units[k]
                    u = len(units) * hg + k
                    h = 4 * hg + hb
                    st = st_a[k % 4]
                    act.wait_ge(S["o_mm"], u + 1)
                    act.activation(oall[:, t, h * P:(h + 1) * P], bank[7][:, 256:384], ACT.Copy, scale=st[:, 12:13]
                                   ).then_inc(S["o_ev"], 1)

                def square(k):
                    hb, t = units[k]
                    u = len(units) * hg + k
                    h = 4 * hg + hb
                    act.wait_ge(S["o_ev"], u + 1)
                    if cnt[0]:
                        act.wait_ge(S["act"], cnt[0])
                    act.activation(squares, oall[:, t, h * P:(h + 1) * P], ACT.Square,
                                   accum_out=ss[:, t * HEADS + h:t * HEADS + h + 1]).then_inc(S["act"], 1)
                    cnt[0] += 1

                probs(0)
                for k in range(len(units)):
                    out(k)
                    if k:
                        square(k - 1)
                    if k + 1 < len(units):
                        probs(k + 1)
                    fin(k)
                square(len(units) - 1)
            act.wait_ge(S["act"], cnt[0])
            act.wait_ge(S["init"], 1)
            act.activation(rstd, ss, ACT.Sqrt, bias=epst, scale=1.0 / P).then_inc(S["rms_sqrt"], 1)

            def mixer_out(l):
                sq = 0
                for k, (kind, t) in enumerate(turns(l)):
                    if kind == "r":
                        act.wait_ge(L[l]["bn"], after(l, "bn", t + 1))
                        act.activation(sd[:, 0:1], mv[:, 1:2], ACT.Sqrt, bias=epst).then_inc(L[l]["ln_sqrt"], 1)
                        sq += 1
                    act.wait_ge(L[l]["turn_mm"], after(l, "turn_mm", k + 1))
                    if k >= 2:
                        act.wait_ge(L[l]["turn_use"], after(l, "turn_use", k - 1))
                    act.activation(oT[k % 2][:, 0:4, :], bank[2][:, :].rearrange("p (c t) -> p c t", c=4), ACT.Copy)
                    act.activation(oT[k % 2][:, 4:8, :], bank[3][:, :].rearrange("p (c t) -> p c t", c=4), ACT.Copy
                                   ).then_inc(L[l]["turn_ev"], 1)
                n = TILES[l]
                act.wait_ge(L[l]["turn_use"], after(l, "turn_use", len(turns(l))))
                act.activation(RT[:, 208:208 + n * 16], bank[6][:, 0:n * 16], ACT.Sigmoid).then_inc(L[l]["aff"], 1)

            def moe(l):
                E = L[l]
                act.wait_ge(E["tbl"], 1)
                nb = act.value_load(inclI[0:1, NE - 1:NE], min_val=2, max_val=MAXB[l] + 1)

                def turned(j):
                    act.wait_ge(E["xt"], j + 1)
                    act.activation(xT[:, 4:8, :], bank[1][:, :].rearrange("p (c t) -> p c t", c=4), ACT.Copy).then_inc(E["xt_a"], 1)

                act.sem_inc(E["y_a"], 1)
                act.dma_start(ypad[l][(MAXB[l] + 1) * P:, :], X[l][:, 0, :]).then_inc(E["y_st"], 16)
                turned(0)
                with act.Fori(0, MAXB[l]) as j:
                    with act.If(j + 1 < nb):
                        for h in range(2):
                            act.wait_ge(E["g_mm"], 2 * j + h + 1)
                            act.activation(gsil[:, h * 256:(h + 1) * 256], gbank[h], ACT.Silu).then_inc(E["silu"], 1)
                        turned(j + 1)
                        act.wait_ge(E["yd_mm"], j + 2)
                        act.wait_ge(E["y_st"], 16 * (j + 1))
                        act.activation(ysb[:, 0:512], bank[5][:, :], ACT.Copy).then_inc(E["y_a"], 1)
                        act.wait_ge(E["y_a"], j + 2)
                        act.wait_ge(E["y_v"], j + 2)
                        act.dma_start(ypad[l][bass.ds(j * P, P), :], ysb).then_inc(E["y_st"], 16)
                stores = act.value_load(countI[0:1, 0:1], min_val=16, max_val=16 * 28)
                act.wait_ge(E["y_st"], stores)
                act.sem_inc(E["y_all"], 1)
                for t in range(TILES[l]):
                    act.wait_ge(E["bn2"], after(l, "bn2", t + 1))
                    act.activation(sd[:, 1:2], mv[:, 1:2], ACT.Sqrt, bias=epst).then_inc(E["ln2_sqrt"], 1)

            mixer_out(0)
            moe(0)
            context_h(1)
            for i in range(8):
                part, h = divmod(i, 4)
                act.wait_ge(S["gq_mm"], i + 1)
                act.activation(QK[:, h, part, :], bank[i % 2][:, :], ACT.Copy, scale=(DK ** -0.5 if part == 0 else 1.0)
                               ).then_inc(S["gq_ev"], 1)
                if part:
                    act.wait_ge(S["gk_mm"], h + 1)
                    act.activation(KX[:, h, :], bank[2 + i % 2][:, 0:CTX], ACT.Copy).then_inc(S["gk_ev"], 1)
            act.wait_ge(S["gd_mm"], 1)
            act.activation(gdT[0:64, 0:SEQ], bank[0][0:64, :], ACT.Copy)
            act.activation(gdT[0:64, SEQ:TOK], bank[1][0:64, 0:CTX], ACT.Copy).then_inc(S["gd_ev"], 1)
            inv = 1.0 / TAU

            def project(n):
                j, t = vr_tiles[n]
                if j == 4 and t == 0:
                    act.wait_ge(S["xsave_st"], 16 * LT)
                act.wait_ge(S["gv_mm"], n + 1)
                dst = (V1 if j < 4 else R1)[:, t, (j % 2) * 512:(j % 2 + 1) * 512]
                act.activation(dst, bank[6 + n % 2][:, :], ACT.Copy if j < 4 else ACT.Silu).then_inc(S["gv_ev"], 1)

            def log_sigmoid(h, part):
                if part == 0:
                    if h:
                        act.wait_ge(S["ls_done"], 3 * h)
                    for d in range(2):
                        act.wait_ge(S["gu_mm"], 2 * h + d + 1)
                        bg = bgc[:, 4 * d + h:4 * d + h + 1]
                        act.activation(LS[:, d, 0:SEQ], bank[2 * d][:, :], ACT.Abs, bias=bg)
                        link(act.activation(LS[:, d, SEQ:TOK], bank[2 * d + 1][:, 0:CTX], ACT.Abs, bias=bg))
                else:
                    link(act.activation(LS[:, :, :], LS[:, :, :], ACT.Exp, scale=-1.0))
                    act.activation(LS[:, :, :], LS[:, :, :], ACT.Ln, bias=1.0).then_inc(S["ls_exp"], 1)

            def level(h, k):
                n = 7 * h + k
                act.wait_ge(S["lv_arg"], n + 1)
                act.activation(LVB[n % 3], LVB[n % 3], ACT.Exp, scale=inv).then_inc(S["lv_exp"], 1)

            bias = lambda n: bstot[:, n:n + 1]

            def decay_context(h):
                bf, bb = GB[h % 2][:, 0, :], GB[h % 2][:, 1, :]
                act.wait_ge(S["ls_done"], 3 * h + 3)
                if h:
                    act.wait_ge(S["kc_mm"], h)
                act.activation(KXG[:, 0, :], bf[:, SEQ:TOK], ACT.Exp, scale=-inv, bias=bias(ctot[h % 2]))
                act.activation(KXG[:, 1, :], bb[:, SEQ:TOK], ACT.Exp, scale=-inv, bias=bias(ctot[h % 2] + 1)).then_inc(S["kc_exp"], 1)

            def decay_blocks(h):
                bf, bb = GB[h % 2][:, 0, :], GB[h % 2][:, 1, :]
                tl = TL[h % 2]
                act.wait_ge(S["ls_done"], 3 * h + 3)
                if h >= 2:
                    act.wait_ge(S["go_mm"], 4 * (h - 1))
                act.activation(tl[:, 0, :], bf[:, 0:SEQ], ACT.Exp, scale=inv)
                act.activation(tl[:, 2, :], bb[:, 0:SEQ], ACT.Exp, scale=inv)
                for b in range(4):
                    act.activation(tl[:, 1, b * P:(b + 1) * P], bf[:, b * P:(b + 1) * P], ACT.Exp, scale=-inv, bias=bias(b))
                    act.activation(tl[:, 3, b * P:(b + 1) * P], bb[:, b * P:(b + 1) * P], ACT.Exp, scale=-inv, bias=bias(4 + b))
                if h:
                    act.wait_ge(S["tl_done"], h)
                act.activation(etot[:, 0:10], bstot[:, 12:22], ACT.Exp).then_inc(S["tl_exp"], 1)

            def off_diagonal(h, g):
                act.wait_ge(S["off_mm"], 3 * h + g + 1)
                if g == 0 and h:
                    act.wait_ge(S["go_mm"], 4 * h)
                act.activation(SO[:, 4 * g:4 * g + 4, :], bank[6 + g % 2][:, :].rearrange("p (k t) -> p k t", k=4), ACT.Copy
                               ).then_inc(S["off_ev"], 1)

            def context_keys(h):
                act.wait_ge(S["kc_mm"], h + 1)
                act.activation(KXT[:, :, :, :], bank[7][:, :].rearrange("p (d t e) -> p d t e", d=2, t=2), ACT.Copy
                               ).then_inc(S["kc_ev"], 1)

            def context_states(h):
                act.wait_ge(S["st_mm"], h + 1)
                act.activation(ST[:, :, :], bank[6][:, :].rearrange("p (d e) -> p d e", d=2), ACT.Copy).then_inc(S["st_ev"], 1)

            def square(h, t):
                act.wait_ge(S["go_ev"], 4 * h + t + 1)
                act.activation(bank[6 + t % 2][:, DV:2 * DV], bank[6 + t % 2][:, 0:DV], ACT.Square,
                               accum_out=ss[:, t * GH + h:t * GH + h + 1]).then_inc(S["gss"], 1)

            log_sigmoid(0, 0)
            log_sigmoid(0, 1)
            for h in range(GH):
                for k in range(8):
                    if k < 7:
                        level(h, k)
                    if h == 0 and k == 1:
                        decay_blocks(0)
                    if h + 1 < GH:
                        if k == 1:
                            log_sigmoid(h + 1, 0)
                        if k == 2:
                            log_sigmoid(h + 1, 1)
                    if h == 0:
                        for n in range(VR_CUT[k], VR_CUT[k + 1]):
                            project(n)
                        if k == 7:
                            act.wait_ge(S["gv_mm"], len(vr_tiles))
                            decay_context(0)
                            for g in range(3):
                                off_diagonal(0, g)
                            context_keys(0)
                            context_states(0)
                    else:
                        if 1 <= k < 5:
                            square(h - 1, k - 1)
                        if k == 4:
                            off_diagonal(h, 0)
                            off_diagonal(h, 1)
                        if k == 5:
                            off_diagonal(h, 2)
                            context_keys(h)
                        if k == 6:
                            context_states(h)
                    if h + 1 < GH:
                        if k == (6 if h else 7):
                            decay_context(h + 1)
                        if k == 7:
                            decay_blocks(h + 1)
            for t in range(LT):
                square(GH - 1, t)
            act.wait_ge(S["gss"], 16)
            act.activation(rstd[:, 0:16], ss[:, 0:16], ACT.Sqrt, bias=epst, scale=1.0 / DV).then_inc(S["rms_sqrt"], 1)
            mixer_out(1)
            moe(1)

        @block.vector
        def _(v):
            cnt = [0]

            def link(ins):
                cnt[0] += 1
                ins.then_inc(S["dve"], 1)
                v.wait_ge(S["dve"], cnt[0])

            def ada(n):
                j = STREAM[ADA_ITEMS[n]][2]
                v.wait_ge(ring_used, used_value(ADA_ITEMS[n]))
                if n == 4:
                    v.wait_ge(S["o_mm"], 48)
                v.wait_ge(adab_ld[n % 2], 16 * (n // 2 + 1))
                if n >= 2:
                    v.wait_ge(ada_st[n % 2], 16 * (n // 2))
                one = 1.0 if j in (2, 3, 8, 9) else 0.0
                v.scalar_tensor_tensor(adat[n % 2], bank[7][0:2, :], one, adab[n % 2], ALU.add, ALU.add).then_inc(ada_row, 1)

            def latent_h(l):
                v.wait_ge(modc_ld[l], 16 * 4)
                mvv = modc[l].rearrange("p (v s c) -> p v s c", v=2, s=2)
                for c in range(KC):
                    v.wait_ge(xt_mm[l], c + 1)
                    v.tensor_scalar(hT[:, c, 0:SEQ], bank[c % 3][:, :], mvv[:, 1, 0, c:c + 1], mvv[:, 0, 0, c:c + 1],
                                    ALU.mult, ALU.add).then_inc(ht_l[l], 1)

            v.memset(epst, EPS).then_inc(S["init"], 1)
            for n in range(4):
                ada(n)
            v.wait_ge(S["lam_ld"], 16)
            v.wait_ge(ada_row, 4)
            lv4 = lamv.rearrange("p (k d) -> p k d", k=4)
            for i in range(2):
                ins = v.tensor_tensor_reduce(out=Z[:, i * HD:(i + 1) * HD], in0=lv4[:, 2 * i, :], in1=lv4[:, 2 * i + 1, :], scale=1.0, scalar=0.0,
                                             op0=ALU.mult, op1=ALU.add, accum_out=lam4[:, i:i + 1])
            ins.then_inc(S["lam_a"], 1)
            v.wait_ge(S["lam_b"], 1)
            link(v.tensor_tensor(nlam, lam4[:, 3:4], lam4[:, 2:3], ALU.subtract))
            link(v.tensor_scalar(nlam, nlam, -LAMBDA0, None, ALU.add))
            latent_h(0)
            v.wait_ge(S["cs_ld"], 16)
            for hg in range(2):
                for i in range(8 * hg, 8 * hg + 8):
                    hb, dst = i % 4, (qT, kT)[(i % 8) // 4]
                    v.wait_ge(S["rot_mm"], i + 1)
                    v.wait_ge(S["rope_cos"], i + 1)
                    if i:
                        v.wait_ge(S["rope_done"], i)
                    link(v.tensor_tensor(rtmp, bank[4 + i % 2][:, :], sinT, ALU.mult))
                    v.tensor_tensor(dst[:, hb, 0:SEQ], dst[:, hb, 0:SEQ], rtmp, ALU.add).then_inc(S["rope_done"], 1)
                units = attn_units()
                scale = float(HD) ** -0.5

                def maxes(k):
                    hb, t = units[k]
                    b = bank[3 * (k % 2):3 * (k % 2) + 3]
                    st = st_a[k % 4]
                    u = len(units) * hg + k
                    if k >= 4:
                        v.wait_ge(S["o_ev"], u - 3)
                    v.wait_ge(S["sc_mm"], u + 1)
                    w = SEQ if t < LT else CTX
                    v.tensor_reduce(st[:, 0:1], b[0][:, 0:w], AX.X, ALU.max)
                    ins = v.tensor_reduce(st[:, 1:2], b[1][:, 0:w], AX.X, ALU.max)
                    if t < LT:
                        ins = v.tensor_reduce(st[:, 2:4], b[2][:, :].rearrange("p (m k) -> p m k", m=2), AX.X, ALU.max)
                    link(ins)
                    if t < LT:
                        link(v.tensor_tensor(st[:, 2:4], st[:, 0:2], st[:, 2:4], ALU.max))
                    peak = st[:, 2:4] if t < LT else st[:, 0:2]
                    v.tensor_scalar(st[:, 4:6], peak, -scale, None, ALU.mult).then_inc(S["maxed"], 1)

                def mix(k):
                    hb, t = units[k]
                    st = st_a[k % 4]
                    u = len(units) * hg + k
                    v.wait_ge(S["exped"], u + 1)
                    r4 = st[:, 6:10].rearrange("p (m k) -> p m k", m=2)
                    if t < LT:
                        link(v.tensor_tensor(st[:, 10:12], r4[:, :, 0], r4[:, :, 1], ALU.add))
                    else:
                        link(v.tensor_copy(st[:, 10:12], r4[:, :, 1]))
                    link(v.reciprocal(st[:, 12:14], st[:, 10:12]))
                    link(v.scalar_tensor_tensor(st[:, 14:15], st[:, 10:11], st[:, 13:14], nlam, ALU.mult, ALU.mult))
                    lo = 0 if t < LT else SEQ
                    v.scalar_tensor_tensor(PR[k % 2][:, 0, lo:TOK], PR[k % 2][:, 1, lo:TOK], st[:, 14:15],
                                           PR[k % 2][:, 0, lo:TOK], ALU.mult, ALU.add).then_inc(S["pmix"], 1)

                def turned(k):
                    hb, t = units[k]
                    u = len(units) * hg + k
                    v.wait_ge(S["at_mm"], 2 * u + 1)
                    if u >= 2:
                        v.wait_ge(S["o_mm"], u - 1)
                    if t < LT:
                        v.tensor_copy(aT[k % 2][:, 0:4, :], bank[6][:, :].rearrange("p (k q) -> p k q", k=4)).then_inc(S["at_ev_lo"], 1)
                    else:
                        v.sem_inc(S["at_ev_lo"], 1)

                maxes(0)
                mix(0)
                maxes(1)
                for k in range(len(units)):
                    turned(k)
                    if k + 1 < len(units):
                        mix(k + 1)
                    if k + 2 < len(units):
                        maxes(k + 2)

            def rms_rows(l):
                nh, w = (HEADS, P) if l == 0 else (GH, DV)
                n = TILES[l]
                src = [oall, R1][l]
                v.wait_ge(S["rms_sqrt"], l + 1)
                link(v.reciprocal(rstd[:, 0:n * nh], rstd[:, 0:n * nh]))
                if l == 0:
                    link(v.tensor_scalar(rstd, rstd, 1.0 - LAMBDA0, None, ALU.mult))
                for t in range(n):
                    o = src[:, t, :].rearrange("p (h w) -> p h w", h=nh)
                    r = rstd[:, t * nh:(t + 1) * nh].unsqueeze(2).to_broadcast([P, nh, w])
                    link(v.tensor_tensor(o, o, r, ALU.mult))
                    g = normg[l].unsqueeze(1).to_broadcast([P, nh, w])
                    if t == 0:
                        v.wait_ge(L[l]["rows_ld"], after(l, "rows_ld", 16))
                    v.tensor_tensor(o, o, g, ALU.mult).then_inc(L[l]["on_rdy"], 1)

            def stats(l, t, x, name_bn, name_sqrt, name_n, col):
                link(v.bn_stats(bst[:, 0:6], x[:, 0:512]))
                link(v.bn_stats(bst[:, 6:12], x[:, 512:1024]))
                v.bn_aggr(mv, bst.rearrange("p (k s) -> p k s", k=2)).then_inc(L[l][name_bn], 1)
                v.wait_ge(L[l][name_bn], after(l, name_bn, t + 1))
                v.wait_ge(L[l][name_sqrt], after(l, name_sqrt, t + 1))
                link(v.reciprocal(sd[:, col:col + 1], sd[:, col:col + 1]))
                v.tensor_scalar(x, x, mv[:, 0:1], sd[:, col:col + 1], ALU.subtract, ALU.mult).then_inc(L[l][name_n], 1)
                v.wait_ge(L[l][name_n], after(l, name_n, t + 1))

            def mixer_norm(l):
                for t in range(TILES[l]):
                    v.wait_ge(L[l]["y_mm"], after(l, "y_mm", t + 1))
                    if t == 0:
                        v.wait_ge(S["xres_ld"], 16 * (NT + (LT if l else 0)))
                    v.wait_ge(L[l]["rows2_ld"], after(l, "rows2_ld", 48 if t < LT else 64))
                    for h in range(2):
                        ins = v.tensor_tensor(Z[:, h * 512:(h + 1) * 512], bank[4 * (t % 2) + h][:, :], gm[:, h * 512:(h + 1) * 512], ALU.mult)
                    ins.then_inc(L[l]["z_done"], 1)
                    v.wait_ge(L[l]["z_done"], after(l, "z_done", t + 1))
                    x = X[l][:, t, :]
                    link(v.scalar_tensor_tensor(x, x, ALPHA, Z, ALU.mult, ALU.add))
                    stats(l, t, x, "bn", "ln_sqrt", "ln_n", 0)

            def route(l):
                n = TILES[l]
                E = L[l]
                m = n * 16
                Mv, PM, aff = RT[:, 0:m], RT[:, 96:112 + m], RT[:, 208:208 + m]
                sel, rk, tmp = RT[:, 304:304 + m], RT[:, 400:400 + m], RT[:, 496:496 + m]
                gs, gk, gt = RT[:, 592:592 + 4 * n], RT[:, 616:616 + 4 * n], RT[:, 640:640 + 4 * n]
                AB = RT[:, 664:664 + 2 * m]
                t2 = RT[:, 856:856 + 2 * m]
                big = RT[:, 1048:1496]
                f1, f2, f3, f4 = (RT[:, 1496 + 12 * i:1496 + 12 * i + 2 * n] for i in range(4))
                nbk, incl, excl = RT[:, 1560:1576], RT[:, 1576:1592], RT[:, 1592:1608]
                E28, P28, pet = RT[:, 1608:1636], RT[:, 1636:1664], RT[:, 1664:1748]

                def rank4(s, r, t, groups):
                    s, r, t = (x.rearrange("p (g i) -> p g i", i=4) for x in (s, r, t))
                    link(v.memset(r, 0.0))
                    for d in range(1, 4):
                        link(v.tensor_tensor(t[:, :, 0:4 - d], s[:, :, 0:4 - d], s[:, :, d:4], ALU.is_ge))
                        link(v.tensor_tensor(r[:, :, d:4], r[:, :, d:4], t[:, :, 0:4 - d], ALU.add))
                        link(v.scalar_tensor_tensor(r[:, :, 0:4 - d], r[:, :, 0:4 - d], 1.0, t[:, :, 0:4 - d], ALU.add, ALU.subtract))

                v.wait_ge(E["aff"], after(l, "aff", 1))
                a3 = aff.rearrange("p (t e) -> p t e", e=16)
                link(v.tensor_tensor(sel.rearrange("p (t e) -> p t e", e=16), a3, rb.unsqueeze(1).to_broadcast([P, n, 16]), ALU.add))
                rank4(sel, rk, tmp, 4 * n)
                link(v.scalar_tensor_tensor(tmp, rk, 2.0, sel, ALU.is_lt, ALU.mult))
                link(v.tensor_reduce(gs, tmp.rearrange("p (g i) -> p g i", i=4), AX.X, ALU.add))
                rank4(gs, gk, gt, n)
                link(v.tensor_scalar(gt, gk, 0.0, None, ALU.is_equal))
                g4 = gt.unsqueeze(2).to_broadcast([P, 4 * n, 4])
                r4 = rk.rearrange("p (g i) -> p g i", i=4)
                for k in range(2):
                    link(v.scalar_tensor_tensor(AB[:, k * m:(k + 1) * m].rearrange("p (g i) -> p g i", i=4), r4, float(k), g4,
                                                ALU.is_equal, ALU.mult))
                link(v.tensor_tensor(Mv, AB[:, 0:m], AB[:, m:2 * m], ALU.add))
                link(v.memset(PM[:, 0:16], 0.0))
                for t in range(n):
                    ins = v.tensor_tensor(PM[:, (t + 1) * 16:(t + 2) * 16], PM[:, t * 16:(t + 1) * 16], Mv[:, t * 16:(t + 1) * 16], ALU.add)
                    if t < n - 1:
                        link(ins)
                ins.then_inc(E["mask"], 1)
                ab3 = AB.rearrange("p (k e) -> p k e", k=2)
                t3 = t2.rearrange("p (k e) -> p k e", k=2)
                link(v.tensor_tensor(t3, ab3, aff.unsqueeze(1).to_broadcast([P, 2, m]), ALU.mult))
                w2 = W2[:, 0:2 * n]
                link(v.tensor_reduce(w2, t2.rearrange("p (k e) -> p k e", e=16), AX.X, ALU.add))
                link(v.tensor_tensor(f1[:, 0:n], w2[:, 0:n], w2[:, n:2 * n], ALU.add))
                link(v.reciprocal(f1[:, 0:n], f1[:, 0:n]))
                w3 = w2.rearrange("p (k t) -> p k t", k=2)
                link(v.tensor_tensor(w3, w3, f1[:, 0:n].unsqueeze(1).to_broadcast([P, 2, n]), ALU.mult))

            def route_2(l):
                n = TILES[l]
                E = L[l]
                m = n * 16
                AB, t2 = RT[:, 664:664 + 2 * m], RT[:, 856:856 + 2 * m]
                big = RT[:, 1048:1496]
                f1, f2, f3, f4 = (RT[:, 1496 + 12 * i:1496 + 12 * i + 2 * n] for i in range(4))
                nbk, incl, excl = RT[:, 1560:1576], RT[:, 1576:1592], RT[:, 1592:1608]
                E28, P28, pet = RT[:, 1608:1636], RT[:, 1636:1664], RT[:, 1664:1748]
                t3 = t2.rearrange("p (k t e) -> p k t e", k=2, e=16)
                ab4 = AB.rearrange("p (k t e) -> p k t e", k=2, e=16)
                v.wait_ge(E["rank_mm"], after(l, "rank_mm", 1))
                b6 = big[:, 0:96].rearrange("p (e k) -> p e k", k=6)
                link(v.tensor_tensor(b6, bank[5][:, 0:16].unsqueeze(2).to_broadcast([P, 16, 6]),
                                     kmul.unsqueeze(1).to_broadcast([P, 16, 6]), ALU.is_gt))
                link(v.tensor_reduce(nbk, b6, AX.X, ALU.add))
                link(v.tensor_tensor_scan(incl, ones[:, 0:16], nbk, 0.0, ALU.mult, ALU.add))
                link(v.tensor_tensor(excl, incl, nbk, ALU.subtract))
                rk3 = bank[6][:, 0:m].unsqueeze(1).to_broadcast([P, 2, m])
                link(v.tensor_tensor(t2.rearrange("p (k e) -> p k e", k=2), AB.rearrange("p (k e) -> p k e", k=2), rk3, ALU.mult))
                link(v.tensor_reduce(f1, t2.rearrange("p (k e) -> p k e", e=16), AX.X, ALU.add))
                link(v.tensor_tensor(t2.rearrange("p (k e) -> p k e", e=16), AB.rearrange("p (k e) -> p k e", e=16),
                                     excl.unsqueeze(1).to_broadcast([P, 2 * n, 16]), ALU.mult))
                link(v.tensor_reduce(f2, t2.rearrange("p (k e) -> p k e", e=16), AX.X, ALU.add))
                b5 = big[:, 0:10 * n].rearrange("p (t k) -> p t k", k=5)
                link(v.tensor_tensor(b5, f1.unsqueeze(2).to_broadcast([P, 2 * n, 5]),
                                     kmul[:, 1:6].unsqueeze(1).to_broadcast([P, 2 * n, 5]), ALU.is_ge))
                link(v.tensor_reduce(f3, b5, AX.X, ALU.add))
                link(v.tensor_tensor(f2, f2, f3, ALU.add))
                link(v.scalar_tensor_tensor(f1, f3, -float(P), f1, ALU.mult, ALU.add))
                link(v.scalar_tensor_tensor(f4, f2, float(P), f1, ALU.mult, ALU.add))
                link(v.scalar_tensor_tensor(f3, f1, 28.0, f2, ALU.mult, ALU.add))
                link(v.tensor_copy(destI[:, 0:2 * n], f4))
                link(v.tensor_copy(addrI[:, 0:2 * n], f3))
                link(v.tensor_copy(tidI, tidf))
                b28 = big.rearrange("p (j e) -> p j e", e=16)
                link(v.tensor_tensor(b28, incl.unsqueeze(1).to_broadcast([P, 28, 16]), jrow.unsqueeze(2).to_broadcast([P, 28, 16]), ALU.is_le))
                link(v.tensor_reduce(E28, b28, AX.X, ALU.add))
                link(v.tensor_tensor(b28, b28, sgn.unsqueeze(1).to_broadcast([P, 28, 16]), ALU.mult))
                link(v.tensor_reduce(P28, b28, AX.X, ALU.add))
                p3 = pet.rearrange("p (j k) -> p j k", k=3)
                link(v.tensor_scalar(E28, E28, 8.0, None, ALU.mult))
                link(v.tensor_copy(p3[:, :, 0], P28))
                link(v.scalar_tensor_tensor(p3[:, :, 1], P28, -8.0, E28, ALU.mult, ALU.add))
                link(v.tensor_scalar(p3[:, :, 1], p3[:, :, 1], 16.0, None, ALU.add))
                link(v.scalar_tensor_tensor(p3[:, :, 2], P28, 8.0, E28, ALU.mult, ALU.add))
                link(v.tensor_copy(peI, pet))
                link(v.tensor_scalar(f1[:, 0:1], incl[:, NE - 1:NE], 16.0, 16.0, ALU.mult, ALU.add))
                link(v.tensor_scalar(f1[:, 1:2], incl[:, NE - 1:NE], -16.0, 16.0 * (MAXB[l] + 1), ALU.mult, ALU.add))
                link(v.tensor_copy(countI, f1[:, 0:2]))
                link(v.tensor_scalar(incl, incl, 1.0, None, ALU.add))
                v.tensor_copy(inclI, incl).then_inc(E["tbl"], 1)

            def moe(l):
                E = L[l]
                v.wait_ge(E["tbl"], 1)
                nb = v.value_load(inclI[0:1, NE - 1:NE], min_val=2, max_val=MAXB[l] + 1)

                def turned(j):
                    v.wait_ge(E["xt"], j + 1)
                    v.tensor_copy(xT[:, 0:4, :], bank[0][:, :].rearrange("p (c t) -> p c t", c=4)).then_inc(E["xt_v"], 1)

                v.sem_inc(E["y_v"], 1)
                turned(0)
                with v.Fori(0, MAXB[l]) as j:
                    with v.If(j + 1 < nb):
                        v.wait_ge(E["u_mm"], j + 1)
                        for h in range(2):
                            v.wait_ge(E["silu"], 2 * j + h + 1)
                            cols = slice(h * 256, (h + 1) * 256)
                            v.tensor_tensor(gate[:, cols], bank[3][:, cols], gsil[:, cols], ALU.mult).then_inc(E["gmul"], 1)
                        for h in range(2):
                            v.wait_ge(E["gt_mm"], 2 * j + h + 1)
                            v.tensor_copy(gT[:, 2 * h:2 * h + 2, :], gtbank[h].rearrange("p (c t) -> p c t", c=2)).then_inc(E["gt_ev"], 1)
                        turned(j + 1)
                        v.wait_ge(E["yd_mm"], j + 2)
                        v.wait_ge(E["y_st"], 16 * (j + 1))
                        v.tensor_copy(ysb[:, 512:1024], bank[6][:, :]).then_inc(E["y_v"], 1)
                n = TILES[l]
                for t in range(n):
                    x = X[l][:, t, :]
                    ya, yb = yab[l][2 * (t % 2)], yab[l][2 * (t % 2) + 1]
                    v.wait_ge(E[f"ya_ld{t % 2}"], after(l, f"ya_ld{t % 2}", 32 * (t // 2 + 1)))
                    if t == 0:
                        v.wait_ge(E["rows3_ld"], after(l, "rows3_ld", 48))
                    if t == LT:
                        v.wait_ge(E["rows3_ld"], after(l, "rows3_ld", 64))
                    link(v.tensor_scalar(ya, ya, W2[:, t:t + 1], None, ALU.mult))
                    link(v.scalar_tensor_tensor(ya, yb, W2[:, n + t:n + t + 1], ya, ALU.mult, ALU.add))
                    v.tensor_tensor(ya, ya, gm, ALU.mult).then_inc(E["z2_done"], 1)
                    v.wait_ge(E["z2_done"], after(l, "z2_done", t + 1))
                    link(v.scalar_tensor_tensor(x, x, ALPHA, ya, ALU.mult, ALU.add))
                    stats(l, t, x, "bn2", "ln2_sqrt", "ln2_n", 1)

            for n in range(4, 10):
                ada(n)
                if n == 5:
                    rms_rows(0)
            mixer_norm(0)
            route(0)
            for n in (10, 11):
                ada(n)
            route_2(0)
            for n in range(12, 24):
                ada(n)
            moe(0)
            latent_h(1)
            v.wait_ge(ht_l[1], KC)
            v.wait_ge(S["mask_ld"], 16)

            def log_sigmoid(h, d):
                gb = GB[h % 2]
                v.wait_ge(S["ls_exp"], h + 1)
                bg = bgc[:, 4 * d + h:4 * d + h + 1]
                v.tensor_scalar(gb[:, d, 0:SEQ], bank[2 * d][:, :], bg, 0.0, ALU.add, ALU.min)
                link(v.tensor_scalar(gb[:, d, SEQ:TOK], bank[2 * d + 1][:, 0:CTX], bg, 0.0, ALU.add, ALU.min))
                link(v.tensor_tensor(LS[:, d, :], gb[:, d, :], LS[:, d, :], ALU.subtract))
                for o, w in [(b * P, P) for b in range(4)] + [(SEQ, CTX)]:
                    src, dst = LS[:, d, o:o + w], gb[:, d, o:o + w]
                    if d:
                        src, dst = src[:, ::-1], dst[:, ::-1]
                    one = ones[:, 0:1].to_broadcast([P, w])
                    ins = v.tensor_tensor_scan(dst, one, src, 0.0, ALU.mult, ALU.add)
                ins.then_inc(S["ls_done"], 1)

            def totals(h):
                gb = GB[h % 2]
                v.wait_ge(S["ls_done"], 3 * h + 2)
                tf = gb[:, 0, 0:SEQ].rearrange("p (b t) -> p b t", b=4)[:, :, P - 1]
                tb = gb[:, 1, 0:SEQ].rearrange("p (b t) -> p b t", b=4)[:, :, 0]
                v.tensor_scalar(bstot[:, 0:4], tf, 1.0 / TAU, None, ALU.mult)
                v.tensor_scalar(bstot[:, 4:8], tb, 1.0 / TAU, None, ALU.mult)
                v.tensor_scalar(bstot[:, ctot[h % 2]:ctot[h % 2] + 1], gb[:, 0, TOK - 1:TOK], 1.0 / TAU, None, ALU.mult)
                link(v.tensor_scalar(bstot[:, ctot[h % 2] + 1:ctot[h % 2] + 2], gb[:, 1, SEQ:SEQ + 1], 1.0 / TAU, None, ALU.mult))
                v.tensor_copy(bstot[:, 12:14], bstot[:, 1:3])
                v.tensor_copy(bstot[:, 14:15], bstot[:, 6:7])
                v.tensor_copy(bstot[:, 15:16], bstot[:, 5:6])
                v.tensor_copy(bstot[:, 16:17], bstot[:, 0:1])
                v.tensor_tensor(bstot[:, 17:18], bstot[:, 0:1], bstot[:, 1:2], ALU.add)
                v.tensor_copy(bstot[:, 21:22], bstot[:, 7:8])
                link(v.tensor_tensor(bstot[:, 20:21], bstot[:, 7:8], bstot[:, 6:7], ALU.add))
                v.tensor_tensor(bstot[:, 18:19], bstot[:, 17:18], bstot[:, 2:3], ALU.add)
                v.tensor_tensor(bstot[:, 19:20], bstot[:, 20:21], bstot[:, 5:6], ALU.add).then_inc(S["ls_done"], 1)

            def level(h, k):
                n = 7 * h + k
                v.wait_ge(S["lv_exp"], n + 1)
                v.tensor_tensor(LVB[n % 3], LVB[n % 3], QK[:, h], ALU.mult).then_inc(S["lv_mul"], 1)

            def diag(h, k):
                i = 8 * h + k
                v.wait_ge(S["lv_mm"], i + 1)
                ps = bank[4 + i % 2][:, :].rearrange("p (b t) -> p b t", b=4)
                mk = maskv[:, k, :].unsqueeze(1).to_broadcast([P, 4, P])
                if k == 0:
                    if h >= 2:
                        v.wait_ge(S["go_mm"], 4 * (h - 1))
                    v.tensor_tensor(SD[h % 2], ps, mk, ALU.mult).then_inc(S["lv_ev"], 1)
                else:
                    v.wait_ge(S["lv_ev"], i)
                    v.copy_predicated(SD[h % 2], mk.bitcast(I32), ps).then_inc(S["lv_ev"], 1)

            def decay_context(h):
                v.wait_ge(S["kc_exp"], h + 1)
                for d in range(2):
                    ins = v.tensor_tensor(KXG[:, d, :], KXG[:, d, :], KX[:, h, :], ALU.mult)
                ins.then_inc(S["kc_done"], 1)

            def decay_blocks(h):
                tl = TL[h % 2]
                v.wait_ge(S["tl_exp"], h + 1)
                for k in range(4):
                    ins = v.tensor_tensor(tl[:, k, :], tl[:, k, :], QK[:, h, k % 2, :], ALU.mult)
                link(ins)
                if h:
                    v.wait_ge(S["off_mm"], 3 * h)
                qf, kf, qb, kb = (tl[:, k, :].rearrange("p (b t) -> p b t", b=4) for k in range(4))
                for n, src in enumerate((kf[:, 0, :], qf[:, 3, :], kb[:, 3, :], qb[:, 0, :],
                                         qf[:, 1, :], qf[:, 2, :], qf[:, 3, :], qb[:, 0, :], qb[:, 1, :], qb[:, 2, :])):
                    dst = VARO[:, n, :] if n < 4 else VARD[h % 2][:, n - 4, :]
                    ins = v.tensor_scalar(dst, src, etot[:, n:n + 1], None, ALU.mult)
                ins.then_inc(S["tl_done"], 1)

            def outputs(h, t):
                v.wait_ge(S["go_mm"], 4 * h + t + 1)
                r = R1[:, t, h * DV:(h + 1) * DV]
                v.tensor_tensor(r, r, bank[6 + t % 2][:, 0:DV], ALU.mult).then_inc(S["go_ev"], 1)

            for d in range(2):
                log_sigmoid(0, d)
            totals(0)
            for h in range(GH):
                for k in range(8):
                    if k < 7:
                        level(h, k)
                    diag(h, k)
                    if h and k < 4:
                        outputs(h - 1, k)
                    if h + 1 < GH:
                        if k in (3, 4):
                            log_sigmoid(h + 1, k - 3)
                        if k == 5:
                            totals(h + 1)
                if h == 0:
                    v.wait_ge(S["gv_mm"], len(vr_tiles))
                    decay_context(0)
                    decay_blocks(0)
                if h + 1 < GH:
                    decay_context(h + 1)
                    decay_blocks(h + 1)
            for t in range(LT):
                outputs(GH - 1, t)
            v.wait_ge(S["go_ev"], 16)
            rms_rows(1)
            mixer_norm(1)
            route(1)
            route_2(1)
            moe(1)

        @block.gpsimd
        def _(g):
            cnt = [0]

            def link(ins):
                cnt[0] += 1
                ins.then_inc(S["pool"], 1)
                g.wait_ge(S["pool"], cnt[0])

            g.dma_start(lamv, a["attn_lambda"][0].rearrange("k d -> (k d)").unsqueeze(0).to_broadcast([P, 4 * HD])).then_inc(S["lam_ld"], 16)
            link(g.memset(idx32[:, :], 0))
            for l in range(2):
                g.dma_start(tokd[l].rearrange("(p j) o -> p (j o)", j=28), zfill).then_inc(L[l]["tok_zero"], 16)
            g.dma_start(rb, a["router_b"].unsqueeze(0).to_broadcast([P, 16])).then_inc(S["pool_ld"], 16)

            def mod_cols(l, n):
                for k in (n - 1, n):
                    g.wait_ge(ada_st[k % 2], 16 * (k // 2 + 1))
                mvv = modc[l].rearrange("p (v s c) -> p v s c", v=2, s=2)
                for vec in range(2):
                    for s in range(2):
                        g.dma_start(mvv[:, vec, s, :], modd[l][s, vec * D:(vec + 1) * D].rearrange("(p c) -> p c", c=KC)).then_inc(modc_ld[l], 16)

            mod_cols(0, 3)
            g.wait_ge(S["cs_ld"], 16)
            for i in range(16):
                hb, dst = i % 4, (qT, kT)[(i % 8) // 4]
                g.wait_ge(S["qraw"], i + 1)
                if i == 8:
                    g.wait_ge(S["o_mm"], 24)
                g.tensor_tensor(dst[:, hb, 0:SEQ], qraw[i % 2], cosT, ALU.mult).then_inc(S["rope_cos"], 1)

            def row(l, s, vec):
                return bcast_row(modd[l][s, vec * D:(vec + 1) * D], D)

            def mixer_rows(l):
                E = L[l]
                w = (P, DV)[l]
                gsrc = (a["attn_subln_g"][0], a["gla_norm_g"][0])[l]
                g.dma_start(normg[l], gsrc.unsqueeze(0).to_broadcast([P, w])).then_inc(E["rows_ld"], 16)
                g.dma_start(rwt, a["router_w"].rearrange("(p c) e -> p c e", c=KC)).then_inc(S["routerw_ld"], 16)
                for t in range(TILES[l]):
                    src = xsave[t * P:(t + 1) * P, :] if l else (
                        a["x"][0][t * P:(t + 1) * P, :] if t < LT else a["ctx"][0][(t - LT) * P:(t - LT + 1) * P, :])
                    g.dma_start(X[l][:, t, :], src).then_inc(S["xres_ld"], 16)
                if l == 0:
                    for k in (8, 9):
                        g.wait_ge(ada_st[k % 2], 16 * (k // 2 + 1))
                g.dma_start(gm, row(l, 0, 2)).then_inc(E["rows2_ld"], 16)
                g.dma_start(lng, bcast_row(a["ln_g"][l, 0], D)).then_inc(E["rows2_ld"], 16)
                g.dma_start(lnb, bcast_row(a["ln_b"][l, 0], D)).then_inc(E["rows2_ld"], 16)
                g.dma_start(scf, row(l, 0, 4)).then_inc(E["lgk"], 16)
                g.dma_start(shf, row(l, 0, 3)).then_inc(E["lgk"], 16)
                for t in range(TILES[l]):
                    x = X[l][:, t, :]
                    hf = HF[t % 2]
                    g.wait_ge(E["ln_n"], after(l, "ln_n", t + 1))
                    if t == 0:
                        g.wait_ge(E["rows2_ld"], after(l, "rows2_ld", 48))
                        g.wait_ge(E["lgk"], after(l, "lgk", 32))
                    if t == LT:
                        g.wait_ge(E["lgk"], after(l, "lgk", 64))
                    link(g.tensor_tensor(x, x, lng, ALU.mult))
                    link(g.tensor_tensor(x, x, lnb, ALU.add))
                    if t >= 2:
                        g.wait_ge(E[f"hf_st{t % 2}"], after(l, f"hf_st{t % 2}", 16 * (t // 2)))
                        g.wait_ge(E["turn_mm"], after(l, "turn_mm", turns(l).index(("r", t - 2)) + 1))
                    link(g.tensor_tensor(hf, x, scf, ALU.mult))
                    g.tensor_tensor(hf, hf, shf, ALU.add).then_inc(E["hf_rdy"], 1)
                    g.wait_ge(E["hf_rdy"], after(l, "hf_rdy", t + 1))
                    g.dma_start(hfd[l][t * P:(t + 1) * P, :], hf).then_inc(E[f"hf_st{t % 2}"], 16)
                    if l == 0 and t == LT - 1:
                        g.wait_ge(E["z_done"], after(l, "z_done", LT))
                        g.dma_start(gm, row(l, 1, 2)).then_inc(E["rows2_ld"], 16)
                        g.dma_start(scf, row(l, 1, 4)).then_inc(E["lgk"], 16)
                        g.dma_start(shf, row(l, 1, 3)).then_inc(E["lgk"], 16)

            def dispatch(l):
                E = L[l]
                n = TILES[l]
                g.wait_ge(E["tbl"], 1)
                g.wait_ge(E["tok_zero"], 16)
                for k in range(2 * n):
                    g.indirect_dma_start(out=tokd[l], out_offset=bass.IndirectOffsetOnAxis(ap=addrI[:, k:k + 1], axis=0),
                                         in_=tidI[:, k % n:k % n + 1], in_offset=None).then_inc(E["scat"], 16)
                g.wait_ge(E["scat"], after(l, "scat", 32 * n))
                g.dma_start(slotI, tokd[l].rearrange("(p j) o -> p (j o)", j=28)).then_inc(E["slot_ld"], 16)
                for b in range(2):
                    g.wait_ge(E[f"hf_st{b}"], after(l, f"hf_st{b}", 16 * (n // 2)))
                g.wait_ge(E["slot_ld"], after(l, "slot_ld", 16))

            def moe(l):
                E = L[l]
                n = TILES[l]
                nb = g.value_load(inclI[0:1, NE - 1:NE], min_val=2, max_val=MAXB[l] + 1)

                def passed():
                    g.sem_inc(S["passed"], 1)

                def gather(j):
                    g.tensor_copy(idxcur, slotI[:, bass.ds(j, 1)]).then_inc(E["idx"], 1)
                    g.wait_ge(E["idx"], j + 1)
                    passed()
                    g.indirect_dma_start(out=xrow, out_offset=None, in_=hfd[l],
                                         in_offset=bass.IndirectOffsetOnAxis(ap=idxcur, axis=0)).then_inc(E["gath"], 16)

                g.tensor_copy(idxcur, slotI[:, 0:1]).then_inc(E["idx"], 1)
                g.wait_ge(E["idx"], 1)
                g.indirect_dma_start(out=xrow, out_offset=None, in_=hfd[l],
                                     in_offset=bass.IndirectOffsetOnAxis(ap=idxcur, axis=0)).then_inc(E["gath"], 16)
                with g.Fori(0, MAXB[l] + 1) as j:
                    with g.If(j + 1 >= nb):
                        g.dma_start(ypad[l][bass.ds(j * P, P), :], X[l][:, 0, :]).then_inc(E["yfill"], 16)
                with g.Fori(0, MAXB[l]) as j:
                    with g.If(j + 1 < nb):
                        g.wait_ge(E["xt"], j + 1)
                        g.wait_ge(E["gath"], 16 * (j + 1))
                        gather(j + 1)
                g.wait_ge(E["gath"], 16 * nb)
                passed()
                if l == 0:
                    for k in (10, 11):
                        g.wait_ge(ada_st[k % 2], 16 * (k // 2 + 1))
                g.dma_start(gm, row(l, 0, 5)).then_inc(E["rows3_ld"], 16)
                g.dma_start(lng, bcast_row(a["ln_g"][l, 1], D)).then_inc(E["rows3_ld"], 16)
                g.dma_start(lnb, bcast_row(a["ln_b"][l, 1], D)).then_inc(E["rows3_ld"], 16)
                g.wait_ge(E["y_all"], after(l, "y_all", 1))
                fills = g.value_load(countI[0:1, 1:2], min_val=16, max_val=16 * 28)
                g.wait_ge(E["yfill"], fills)
                passed()

                def fetch(t):
                    for k in range(2):
                        g.indirect_dma_start(out=yab[l][2 * (t % 2) + k], out_offset=None, in_=ypad[l],
                                             in_offset=bass.IndirectOffsetOnAxis(ap=destI[:, k * n + t:k * n + t + 1], axis=0)
                                             ).then_inc(E[f"ya_ld{t % 2}"], 16)

                fetch(0)
                fetch(1)
                for t in range(n):
                    x = X[l][:, t, :]
                    if l == 0 and t == LT - 1:
                        g.wait_ge(E["z2_done"], after(l, "z2_done", LT))
                        g.dma_start(gm, row(l, 1, 5)).then_inc(E["rows3_ld"], 16)
                    g.wait_ge(E["ln2_n"], after(l, "ln2_n", t + 1))
                    if t == 0:
                        g.wait_ge(E["rows3_ld"], after(l, "rows3_ld", 48))
                    if t + 2 < n:
                        fetch(t + 2)
                    link(g.tensor_tensor(x, x, lng, ALU.mult))
                    g.tensor_tensor(x, x, lnb, ALU.add).then_inc(E["xfin"], 1)
                    g.wait_ge(E["xfin"], after(l, "xfin", t + 1))
                    if l:
                        g.dma_start(out[0][t * P:(t + 1) * P, :], x).then_inc(S["outst"], 16)
                    elif t < LT:
                        g.dma_start(xsave[t * P:(t + 1) * P, :], x).then_inc(S["xsave_st"], 16)

            g.wait_ge(S["o_mm"], 48)
            g.wait_ge(S["o_ev"], 48)
            mixer_rows(0)
            dispatch(0)
            moe(0)
            mod_cols(1, 23)
            link(g.memset(wdn, 0.0))
            g.sem_inc(S["wz"], 1)
            for d in range(2):
                g.dma_start(wdn[:, :, 32 * d:32 * d + RANK], a["gla_wg_down"][0, d].rearrange("(p c) r -> p c r", c=KC)).then_inc(S["gw_ld"], 16)
                g.dma_start(wup[32 * d:32 * d + RANK, :], a["gla_wg_up"][0, d]).then_inc(S["gw_ld"], 16)
            for d in range(2):
                g.dma_start(bgc[:, 4 * d:4 * d + 4], a["gla_bg"][0, d].rearrange("(h p) -> p h", p=P), allow_slow_non_contiguous=True).then_inc(S["bg_ld"], 16)
            g.wait_ge(S["bg_ld"], 32)
            g.sem_inc(S["wz"], 1)
            for n in range(7 * GH):
                h, k = divmod(n, 7)
                l2 = 1 << k
                npair = SEQ // (2 * l2)
                lv, gb = LVB[n % 3], GB[h % 2]
                qq, kk, f, b = (x.rearrange("p (n s l) -> p n s l", s=2, l=l2)
                                for x in (lv[:, 0, :], lv[:, 1, :], gb[:, 0, 0:SEQ], gb[:, 1, 0:SEQ]))
                rf = f[:, :, 0, l2 - 1:l2].to_broadcast([P, npair, l2])
                rbk = b[:, :, 1, 0:1].to_broadcast([P, npair, l2])
                if k == 0:
                    g.wait_ge(S["ls_done"], 3 * h + 2)
                if n >= 3:
                    g.wait_ge(S["lv_mm"], 8 * ((n - 3) // 7) + (n - 3) % 7 + 2)
                g.tensor_tensor(qq[:, :, 1, :], f[:, :, 1, :], rf, ALU.subtract)
                g.tensor_tensor(qq[:, :, 0, :], b[:, :, 0, :], rbk, ALU.subtract)
                g.tensor_tensor(kk[:, :, 0, :], rf, f[:, :, 0, :], ALU.subtract)
                g.tensor_tensor(kk[:, :, 1, :], rbk, b[:, :, 1, :], ALU.subtract).then_inc(S["lv_arg"], 1)
            g.wait_ge(S["go_mm"], 16)
            g.wait_ge(S["go_ev"], 16)
            g.wait_ge(S["gss"], 16)
            mixer_rows(1)
            dispatch(1)
            moe(1)
            g.wait_ge(S["outst"], 16 * LT)


_INS = ["x", "c", "ctx", "c_ctx", "ada_w", "ada_b", "ln_g", "ln_b", "attn_w_qkv", "attn_w_o", "attn_lambda", "attn_subln_g",
        "gla_w_in", "gla_wg_down", "gla_wg_up", "gla_bg", "gla_norm_g", "gla_w_o", "router_w", "router_b",
        "moe_w_gate", "moe_w_up", "moe_w_down"]


def kernel(**inputs):
    from concourse import bacc
    from concourse.bass_utils import run_bass_kernel_spmd

    nc = bacc.Bacc("TRN2", target_bir_lowering=False, num_devices=1)
    arrays, aps = {}, {}
    for name in _INS:
        arr = np.ascontiguousarray(inputs[name])
        arrays[f"in_{name}"] = arr
        aps[name] = nc.dram_tensor(f"in_{name}", arr.shape, mybir.dt.from_np(arr.dtype), kind="ExternalInput").ap()
    table = constants()
    arrays["constants"] = table
    const_ap = nc.dram_tensor("constants", table.shape, F32, kind="ExternalInput").ap()
    out = nc.dram_tensor("out", (1, SEQ, D), F32, kind="ExternalOutput").ap()
    build(nc, aps, out, const_ap)
    r = run_bass_kernel_spmd(nc, [arrays], core_ids=[0])
    return r.results[0]["out"]
```

```python
from contextlib import ExitStack
import math

import numpy as np
import concourse.bass as bass
from concourse import mybir

ALU = mybir.AluOpType
ACT = mybir.ActivationFunctionType
F32 = mybir.dt.float32
I32 = mybir.dt.int32
AX = mybir.AxisListType

P = 128
D = 1024
KC = D // P
SEQ, CTX = 512, 256
TOK = SEQ + CTX
LT, CT = SEQ // P, CTX // P
NT = LT + CT
ALPHA = 4.0 ** 0.25
EPS = 1e-5
HEADS, HD = 8, 64
GRID_W, ROT = 64, HD // 4
GH, DK, DV = 4, 128, 256
RANK = 16
TAU = 16.0
NE, NG, EPG = 16, 4, 4
FE = D // 2
LAMBDA0 = 0.8 - 0.6 * math.exp(0.0)
SLOT = 4096
RING = 6
MAXB = [(TOK * 2 + NE * (P - 1)) // P, (SEQ * 2 + NE * (P - 1)) // P]
MINB = [TOK * 2 // P, SEQ * 2 // P]
NBMAX = TOK // P
TILES = [NT, LT]

STREAM = [("ada", 0, j) for j in range(4)]
STREAM += [("qkv", 0, 2 * part + hg) for hg in range(2) for part in range(3)]
STREAM += [("ada", 0, 4), ("ada", 0, 5)]
STREAM += [("wo", 0, 0), ("wo", 0, 1)]
STREAM += [("ada", 0, j) for j in range(6, 12)]
STREAM += [("ada", 1, j) for j in range(12)]
MOE0 = len(STREAM)
STREAM += [("moe", 0, i) for i in range(3 * NE)]
GLA0 = len(STREAM)
STREAM += [("gla", 1, j) for j in range(6)]
STREAM += [("gap", 1, 0), ("gap", 1, 1)]
STREAM += [("wo", 1, 0), ("wo", 1, 1)]
MOE1 = len(STREAM)
STREAM += [("moe", 1, i) for i in range(3 * NE)]
MOEBASE = [MOE0, MOE1]
ADA_ITEMS = [p for p, it in enumerate(STREAM) if it[0] == "ada"]
PLAIN = [p for p, it in enumerate(STREAM) if it[0] in ("ada", "qkv", "gla")]
ADA_AFTER = {("o", 0): (8, 9), ("o", 1): (10,), ("o", 2): (11,), ("o", 3): (12,), ("o", 4): (13,), ("o", 5): (14,),
             ("r", 3): (15,), ("r", 4): (16,)}
ADA_SUMMED = (10, 11, 12, 13, 14, 15)
CHUNKS_SUMMED = 7
EXPERT_SLOTS = [[0, 1, 4, 5, 2, 3], [2, 3, 0, 1, 4, 5]]


def slot_of(p):
    if p < MOE0:
        return p % RING if p < 4 + 6 + 6 else (4, 5, 2, 3)[(p - 16) % 4]
    if p < GLA0:
        return EXPERT_SLOTS[0][(p - MOE0) % RING]
    if p < MOE1:
        return EXPERT_SLOTS[0][(p - GLA0) % RING]
    return EXPERT_SLOTS[1][(p - MOE1) % RING]


SLOT_OF = [slot_of(p) for p in range(len(STREAM))]


def loads(p):
    return sum(SLOT_OF[q] == SLOT_OF[p] and STREAM[q][0] != "gap" for q in range(p + 1))


def before(p):
    return max(q for q in range(p) if SLOT_OF[q] == SLOT_OF[p])


LAYER0_COUNTS = {
    "on_rdy": 6,
    "turn_mm": 12,
    "turn_ev": 12,
    "turn_use": 12,
    "y_mm": 6,
    "z_done": 6,
    "bn": 6,
    "ln_sqrt": 6,
    "ln_r": 6,
    "ln_n": 6,
    "hf_rdy": 6,
    "aff": 1,
    "y_all": 1,
    "scat": 192,
    "slot_ld": 16,
    "mask": 1,
    "rank_mm": 1,
    "dest": 1,
    "xfin": 6,
    "z2_done": 6,
    "bn2": 6,
    "ln2_sqrt": 6,
    "ln2_r": 6,
    "ln2_n": 6,
    "ya_scaled": 6,
    "rows_ld": 16,
    "rows2_ld": 64,
    "rows3_ld": 64,
    "lgk": 64,
    "hf_st0": 48,
    "hf_st1": 48,
    "ya_ld0": 64,
    "ya_ld1": 64,
    "ya_ld2": 64,
}


def after(l, name, v):
    return v + (LAYER0_COUNTS[name] if l else 0)


def constants():
    ident = np.eye(P, dtype=np.float32)
    rot = np.zeros((P, P), np.float32)
    for d in range(P):
        half = (d // ROT) % 2
        if half == 0:
            rot[d + ROT, d] = -1.0
        else:
            rot[d - ROT, d] = 1.0
    tri = np.triu(np.ones((P, P), np.float32), 1)
    ones = np.ones((P, P), np.float32)
    pos = np.arange(SEQ)
    inv = 10000.0 ** (-np.arange(ROT, dtype=np.float32) / ROT)
    inv = inv.astype(np.float32)
    ang_r = (pos // GRID_W).astype(np.float32)[:, None] * inv
    ang_c = (pos % GRID_W).astype(np.float32)[:, None] * inv
    ang = np.concatenate([ang_r, ang_r, ang_c, ang_c], -1)
    ang = np.concatenate([ang, ang], -1).T
    cs = np.stack([np.cos(ang), np.sin(ang)], 1).astype(np.float32).reshape(P, 2 * SEQ)
    i = np.arange(P)
    masks = [2.0 * ident]
    for lv in range(7):
        masks.append((((i[:, None] ^ i[None, :]) >> lv) == 1).astype(np.float32))
    masks = np.stack(masks, 1).reshape(P, 8 * P).astype(np.float32)
    row = np.zeros((P, 64), np.float32)
    row[:, 0:NBMAX] = np.arange(NBMAX) * P
    row[:, 8:8 + 28] = np.arange(28)
    row[:, 40:56] = np.where(np.arange(16) % 2 == 0, 1.0, -1.0)
    row[:, 36:40] = [1.0, 0.0, 0.0, 1.0]
    row[:, 56:56 + NT] = np.arange(NT)[None, :] * P + i[:, None]
    return np.concatenate([ident, rot, tri, ones, row, cs, masks], 1).astype(np.float32)


OFF = [(0, 1), (2, 3), (0, 2), (0, 3), (1, 2), (1, 3), (1, 0), (3, 2), (2, 0), (2, 1), (3, 0), (3, 1)]
NCONST = 4 * P + 64 + 2 * SEQ + 8 * P


def build(nc, a, out, consts, dumps=None):
    dumps = dumps or {}
    stack = ExitStack()
    with stack:
        def sb(name, cols, dt=F32, parts=P):
            return stack.enter_context(nc.sbuf_tensor(name, [parts, cols], dt))

        def sem(name):
            return stack.enter_context(nc.semaphore(name))

        def dram(name, shape, dt=F32):
            return nc.dram_tensor(name, shape, dt, kind="Internal").ap()

        ring = sb("ring", RING * SLOT)
        A0, A1, A2, A3 = (sb(f"arena{i}", NT * D) for i in range(4))
        cst = sb("cst", 4 * P + 64)
        cs = sb("cos_sin_or_masks", 8 * P)
        U = sb("union_small", 1792)
        sm = sb("small", 372)
        idx32 = sb("idx32", 192, I32)
        bank = [stack.enter_context(nc.psum_tensor(f"bank{i}", [P, 512], F32)) for i in range(8)]

        ident, rot, tri, ones = (cst[:, i * P:(i + 1) * P] for i in range(4))
        rowc = cst[:, 4 * P:4 * P + 64]
        kmul, jrow, sgn, tidf = rowc[:, 0:NBMAX], rowc[:, 8:36], rowc[:, 40:56], rowc[:, 56:56 + NT]

        modd = dram("mod_rows", [2, 2, 6 * D])
        hfd = [dram(f"ffn_in{l}", [TILES[l] * P, D]) for l in range(2)]
        ypad = [dram(f"expert_out{l}", [(MAXB[l] + 2) * P, D]) for l in range(2)]
        tokd = [dram(f"slot_token{l}", [P * 28, 1], I32) for l in range(2)]
        xsave = dram("x_between_layers", [SEQ, D])

        cur = [0]

        def take(n):
            cur[0] += n
            return sm[:, cur[0] - n:cur[0]]

        c_raw, c_act = take(16), take(16)
        modc = [take(32) for _ in range(2)]
        st_a = [take(16) for _ in range(4)]
        lam4, nlam = take(4), take(1)
        ss = take(48)
        rstd = take(48)
        bst, mv, sd, nmu = take(12), take(2), take(2), take(2)
        W2 = take(12)
        bgc = take(8)
        epst = take(1)
        rb = take(16)
        bstot, etot = take(24), take(12)
        ctot = [8, 22]
        routed = [idx32[:, 0:12], idx32[:, 12:24]]
        destI, addrI = routed
        tidI = idx32[:, 24:30]
        idxcur = idx32[:, 30:31]
        zeroI = idx32[:, 31:32]
        slotI = idx32[:, 32:60]
        inclI = idx32[:, 60:76]
        peI = idx32[:, 76:160]
        countI = idx32[:, 188:190]
        zfill = idx32[:, 160:188]

        def slot(p):
            s = SLOT_OF[p]
            return ring[:, s * SLOT:(s + 1) * SLOT]

        ring_ld = [sem(f"ring_loaded{i}") for i in range(RING)]
        ring_used = sem("ring_used")
        const_ld, x_ld, silu_c = sem("const_loaded"), sem("x_loaded"), sem("silu_c_done")
        ada_row = sem("ada_row_ready")
        adab_ld = [sem(f"ada_bias_loaded{i}") for i in range(2)]
        ada_st = [sem(f"ada_row_stored{i}") for i in range(2)]
        modc_ld = sem("mod_cols_loaded")
        xt_mm = sem("x_transposed")
        ht_l = sem("h_latent_ready")
        ht_c = sem("h_context_ready")
        S = {}
        for n in ("proj_mm", "qraw", "rot_mm", "rope_cos", "rope_done", "ctx_ev", "v_mm", "v_ev",
                  "sc_mm", "sc_half", "maxed", "exped", "pmix", "at_mm", "at_ev_lo", "at_ev_hi", "o_mm", "o_ev",
                  "lam_ld", "lam_a", "lam_b", "rms_sqrt", "dve", "act", "pool",
                  "cs_ld", "xres_ld", "routerw_ld",
                  "gq_mm", "gq_ev", "gk_mm", "gk_ev", "gv_mm", "gv_ev", "gd_mm", "gd_ev",
                  "gw_ld", "gu_mm", "ls_exp", "ls_done", "lv_arg", "lv_exp", "lv_mul", "lv_mm", "lv_ev",
                  "tl_exp", "tl_done", "kc_exp", "kc_done", "kc_mm", "kc_ev", "st_mm", "st_ev", "off_mm", "off_ev", "go_mm", "go_ev",
                  "gss", "wz", "router_b_ld", "passed", "bg_ld", "xsave_st", "mask_ld", "init", "outst", "tok_zero", "ada_sum", "sp_passed"):
            S[n] = sem(n)
        L = [{n: sem(n) for n in LAYER0_COUNTS}]
        L.append(dict(L[0]))
        for l in range(2):
            L[l].update({n: sem(f"{n}{l}") for n in (
                "tbl", "idx", "gath",
                "xt", "xt_a", "xt_v", "g_mm", "u_mm", "silu", "gmul", "gt_mm", "gt_ev", "yd_mm", "y_a", "y_v", "y_st", "yfill")})
        block = stack.enter_context(nc.Block())

        hT = A0[:, :].rearrange("p (c t) -> p c t", c=KC)
        xst = A1[:, :].rearrange("p (t n) -> p t n", t=NT)
        X = [A2[:, :].rearrange("p (t n) -> p t n", t=NT), A1[:, :].rearrange("p (t n) -> p t n", t=NT)]
        qT = A2[:, 0:4 * TOK].rearrange("p (h t) -> p h t", h=4)
        kT = A2[:, 4 * TOK:8 * TOK].rearrange("p (h t) -> p h t", h=4)
        vA = A3[:, 0:NT * 512].rearrange("p (t n) -> p t n", t=NT)
        PR = [A3[:, NT * 512 + i * 2 * TOK:NT * 512 + (i + 1) * 2 * TOK].rearrange("p (m k) -> p m k", m=2) for i in range(2)]
        qraw = [A3[:, NT * 512 + i * 512:NT * 512 + (i + 1) * 512] for i in range(2)]
        rtmp = A3[:, NT * 512 + 1024:NT * 512 + 1536]
        aT = [U[:, i * TOK:(i + 1) * TOK].rearrange("p (k q) -> p k q", k=NT) for i in range(2)]
        squares = U[:, 2 * TOK:2 * TOK + P]
        oall = A1[:, :].rearrange("p (t n) -> p t n", t=NT)
        adat = [A3[0:2, 1024 + i * 512:1536 + i * 512] for i in range(4)]
        adab = [A3[0:2, 3072 + i * 512:3584 + i * 512] for i in range(4)]
        adat += [A3[0:2, 4096 + (i % 2) * 512:4608 + (i % 2) * 512] for i in range(20)]
        adab += [A3[0:2, 5120 + (i % 2) * 512:5632 + (i % 2) * 512] for i in range(20)]
        oT = [A0[:, i * D:(i + 1) * D].rearrange("p (c t) -> p c t", c=KC) for i in range(2)]
        HF = [A0[:, (2 + i) * D:(3 + i) * D] for i in range(2)]
        gmc = A0[:, 5 * D:6 * D]
        scf, shf = A0[:, 4 * D:5 * D], A0[:, 5 * D:6 * D]
        gm, lng, lnb, Z = (A3[:, i * D:(i + 1) * D] for i in range(4))
        acc = [x.rearrange("p (s n) -> p s n", s=2) for x in (U[:, 512:1536], cs[:, 0:1024])]
        pick = rowc[:, 36:40].rearrange("p (s m) -> p s m", s=2)
        lamv = A3[:, 0:4 * HD]
        RT = A1[:, 4096:6144]
        xrow = A0[:, 0:D]
        xT = A0[:, D:2 * D].rearrange("p (c t) -> p c t", c=KC)
        gsil, gate = A0[:, 2 * D:2 * D + FE], A0[:, 2 * D + FE:3 * D]
        gT = A0[:, 3 * D:3 * D + FE].rearrange("p (c t) -> p c t", c=4)
        ysb = A0[:, 4 * D:5 * D]
        gbank = [bank[2][:, 0:256], bank[7][:, 0:256]]
        gtbank = [bank[4][:, 0:256], bank[2][:, 256:512]]
        YB = [A1, A2]
        yab = [[YB[l][:, (2 * i + k) * D:(2 * i + k + 1) * D] for i in range(3) for k in range(2)] for l in range(2)]
        normg = [U[:, 256:256 + P], U[:, 256:256 + DV]]
        rwt = U[:, 0:128].rearrange("p (c n) -> p c n", c=KC)
        V1 = A1[:, :].rearrange("p (t n) -> p t n", t=NT)
        R1 = A2[:, 0:LT * D].rearrange("p (t n) -> p t n", t=LT)
        QK = A3[:, 0:4096].rearrange("p (h k t) -> p h k t", h=GH, k=2)
        KX = A3[:, 4096:5120].rearrange("p (h t) -> p h t", h=GH)
        ST = A3[:, 5120:5632].rearrange("p (d e) -> p d e", d=2)
        KXT = A3[:, 5632:6144].rearrange("p (d t e) -> p d t e", d=2, t=2)
        W0, W1 = slot(GLA0 + 6), slot(GLA0 + 7)
        GB = [W[:, 0:2 * TOK].rearrange("p (d t) -> p d t", d=2) for W in (W0, W1)]
        LS = W0[:, 1536:3072].rearrange("p (d t) -> p d t", d=2)
        LVB = [x.rearrange("p (k t) -> p k t", k=2) for x in (W0[:, 3072:4096], W1[:, 1536:2560], W1[:, 2560:3584])]
        SD = [x.rearrange("p (b t) -> p b t", b=4) for x in (W1[:, 3584:4096], U[:, TOK + 512:TOK + 1024])]
        SO = A0[:, 0:1536].rearrange("p (k t) -> p k t", k=12)
        VARO = A0[:, 1536:2048].rearrange("p (k t) -> p k t", k=4)
        VARD = [A0[:, 2048 + 768 * i:2816 + 768 * i].rearrange("p (k t) -> p k t", k=6) for i in range(2)]
        KXG = A0[:, 3584:4096].rearrange("p (d t) -> p d t", d=2)
        TL = [A2[:, 4096:6144].rearrange("p (k t) -> p k t", k=4), A0[:, 4096:6144].rearrange("p (k t) -> p k t", k=4)]
        gdT = U[:, 0:TOK]
        wup = U[:, TOK:TOK + 512]
        wdn = U[:, TOK + 512:TOK + 1024].rearrange("p (c r) -> p c r", c=KC)
        cosT, sinT = cs[:, 0:SEQ], cs[:, SEQ:2 * SEQ]
        maskv = cs[:, :].rearrange("p (k t) -> p k t", k=8)

        def bcast_row(ap_1d, n):
            return ap_1d.unsqueeze(0).to_broadcast([P, n])

        def src_of(p):
            kind, l, j = STREAM[p]
            if kind == "ada":
                return a["ada_w"][l].rearrange("(p c) n -> p c n", c=KC)[:, :, j * 512:(j + 1) * 512]
            if kind == "qkv":
                return a["attn_w_qkv"][0].rearrange("(p c) n -> p c n", c=KC)[:, :, j * 512:(j + 1) * 512]
            if kind == "gla":
                return a["gla_w_in"][0].rearrange("(p c) n -> p c n", c=KC)[:, :, j * 512:(j + 1) * 512]
            w = a["attn_w_o"][0] if l == 0 else a["gla_w_o"][0]
            return w.rearrange("(p c) n -> p c n", c=KC)[:, :, j * 512:(j + 1) * 512]

        def used_value(p):
            return PLAIN.index(p) + 1

        vr_tiles = [(j, t) for j, tiles in ((2, NT), (3, NT), (4, LT), (5, LT)) for t in range(tiles)]
        VR_CUT = [len(vr_tiles) * k // 8 for k in range(9)]

        def mod_cols(eng, l, n):
            for k in (n - 1, n):
                eng.wait_ge(ada_st[k % 2], 16 * (k // 2 + 1))
            mvv = modc[l].rearrange("p (v s c) -> p v s c", v=2, s=2)
            for s in range(2):
                eng.dma_start(mvv[:, :, s, :], modd[l][s, 0:2 * D].rearrange("(v p c) -> p v c", v=2, c=KC)).then_inc(modc_ld, 16)

        def attn_units():
            return [(hb, t) for hb in range(4) for t in (0, 1, 4, 2, 3, 5)]

        def turns(l):
            n, lag, q = TILES[l], 3 - l, []
            for t in range(n):
                q.append(("o", t))
                if t >= lag:
                    q.append(("r", t - lag))
            return q + [("r", t) for t in range(n - lag, n)]

        @block.sync
        def _(sp):
            sp.dma_start(cst[:, :], consts[:, 0:4 * P + 64]).then_inc(const_ld, 16)
            sp.dma_start(c_raw[:, 0:8], a["c"][0].rearrange("(p c) -> p c", c=KC)).then_inc(const_ld, 16)
            sp.dma_start(c_raw[:, 8:16], a["c_ctx"].rearrange("(p c) -> p c", c=KC)).then_inc(const_ld, 16)

            def load_bias(n):
                _, l, j = STREAM[ADA_ITEMS[n]]
                if n >= 6:
                    sp.wait_ge(ada_row, n - 1)
                sp.dma_start(adab[n], a["ada_b"][l][j * 512:(j + 1) * 512].unsqueeze(0).to_broadcast([2, 512])
                             ).then_inc(adab_ld[n % 2], 16)

            def store_row(n):
                _, l, j = STREAM[ADA_ITEMS[n]]
                sp.wait_ge(ada_row, n + 1)
                sp.dma_start(modd[l][:, j * 512:(j + 1) * 512], adat[n]).then_inc(ada_st[n % 2], 16)

            def free(p):
                q = before(p)
                kind, l, j = STREAM[q]
                if kind == "moe":
                    if j % 3 == 0:
                        v = sp.value_load(inclI[0:1, j // 3:j // 3 + 1], min_val=1, max_val=64)
                        sp.wait_ge(L[l]["yd_mm"], v)
                    sp.wait_ge(ring_ld[SLOT_OF[q]], 16 * loads(q))
                elif kind == "gap":
                    sp.wait_ge(S["go_mm"], 16)
                    sp.wait_ge(S["xres_ld"], 16 * (NT + LT))
                    sp.wait_ge(L[1]["rows2_ld"], after(1, "rows2_ld", 48))
                elif kind == "wo":
                    last = turns(l).index(("o", TILES[l] - 1))
                    sp.wait_ge(L[l]["turn_use"], after(l, "turn_use", last + 1))
                else:
                    sp.wait_ge(ring_used, used_value(q))
                if kind == "ada":
                    n = ADA_ITEMS.index(q)
                    if n >= 4:
                        store_row(n)
                        if n + 2 < len(ADA_ITEMS):
                            load_bias(n + 2)

            def issue(p):
                if p >= RING:
                    free(p)
                sp.dma_start(slot(p), src_of(p) if STREAM[p][0] != "moe" else None).then_inc(ring_ld[SLOT_OF[p]], 16)

            def issue_expert(l, e_static, e, items=(0, 1, 2)):
                p = MOEBASE[l] + 3 * e_static
                gw = a["moe_w_gate"][l].rearrange("e (p c) n -> p e (c n)", c=KC)
                uw = a["moe_w_up"][l].rearrange("e (p c) n -> p e (c n)", c=KC)
                dw = a["moe_w_down"][l].rearrange("e (c p) n -> p e c n", c=4)
                for i in items:
                    if i < 2:
                        src, dst = (uw, gw)[i][:, bass.ds(e, 1), :].rearrange("p e n -> p (e n)"), slot(p + i)
                    else:
                        src = dw[:, bass.ds(e, 1), :, :].rearrange("p e c n -> p (e c) n")
                        dst = slot(p + 2).rearrange("p (c n) -> p c n", c=4)
                    sp.dma_start(dst, src).then_inc(ring_ld[SLOT_OF[p + i]], 16)

            for n in range(4):
                load_bias(n)
            for p in range(4):
                issue(p)
            for t in range(NT):
                src = a["x"][0][t * P:(t + 1) * P, :] if t < LT else a["ctx"][0][(t - LT) * P:(t - LT + 1) * P, :]
                sp.dma_start(xst[:, t, :], src).then_inc(x_ld, 16)
            issue(4)
            for n in range(4):
                store_row(n)
            mod_cols(sp, 0, 3)
            sp.dma_start(cs[:, :], consts[:, 4 * P + 64:4 * P + 64 + 2 * SEQ]).then_inc(S["cs_ld"], 16)
            issue(5)
            for l in range(2):
                for p in range(RING if l == 0 else GLA0, MOEBASE[l]):
                    if p == GLA0 + 3:
                        sp.wait_ge(L[0]["z2_done"], NT)
                    if p == ADA_ITEMS[20]:
                        free(MOE0)
                        free(MOE0 + 1)
                        issue_expert(0, 0, 0, (0, 1))
                    if STREAM[p][0] != "gap":
                        issue(p)
                    if p == ADA_ITEMS[4] + RING - 1:
                        sp.wait_ge(S["o_ev"], 48)
                        load_bias(4)
                        load_bias(5)
                    if p == GLA0:
                        sp.wait_ge(S["rope_done"], 16)
                        for m in range(2):
                            sp.wait_ge(L[m]["yfill"], 16)
                        sp.dma_start(cs[:, :], consts[:, 4 * P + 64 + 2 * SEQ:NCONST]).then_inc(S["mask_ld"], 16)
                for e in range(2):
                    items = (2,) if l == 0 and e == 0 else (0, 1, 2)
                    for i in items:
                        free(MOEBASE[l] + 3 * e + i)
                    issue_expert(l, e, e, items)
                if l == 0:
                    mod_cols(sp, 1, 23)
                sp.wait_ge(L[l]["tbl"], 1)
                with sp.Fori(1, NE // 2) as m:
                    for par in range(2):
                        v = sp.value_load(inclI[0:1, bass.ds(2 * m - 2 + par, 1)], min_val=1, max_val=64)
                        sp.wait_ge(L[l]["yd_mm"], v)
                        sp.sem_inc(S["sp_passed"], 1)
                        for i in range(3):
                            q = MOEBASE[l] + 3 * par + i
                            sp.wait_ge(ring_ld[SLOT_OF[q]], 16 * m + 16 * (loads(q) - 1))
                            sp.sem_inc(S["sp_passed"], 1)
                        issue_expert(l, 2 + par, 2 * m + par)
            for q in range(len(STREAM) - RING, len(STREAM)):
                sp.wait_ge(ring_ld[SLOT_OF[q]], 16 * loads(q))

        @block.tensor
        def _(pe):
            def ring_wait(p):
                pe.wait_ge(ring_ld[SLOT_OF[p]], 16 * loads(p))

            def ada(n):
                p = ADA_ITEMS[n]
                w = slot(p).rearrange("p (c n) -> p c n", c=KC)
                ring_wait(p)
                if n == 0:
                    pe.wait_ge(silu_c, 1)
                else:
                    pe.wait_ge(ada_row, n)
                if n in ADA_SUMMED:
                    i = ADA_SUMMED.index(n)
                    pe.wait_ge(S["ada_sum"], i + 1)
                    for s in range(2):
                        pe.matmul(bank[7][0:2, :], pick[:, s, :], acc[i % 2][:, s, :], start=(s == 0), stop=False)
                first = CHUNKS_SUMMED if n in ADA_SUMMED else 0
                cw = c_act.rearrange("p (s c) -> p c s", s=2)
                for c in range(first, KC):
                    mm = pe.matmul(bank[7][0:2, :], cw[:, c, :], w[:, c, :], start=(c == 0), stop=(c == KC - 1))
                mm.then_inc(ring_used, 1)

            def transpose_x(l):
                nl = X[0] if l else xst
                for c in range(KC):
                    if c >= 3:
                        pe.wait_ge(ht_l, KC * l + c - 2)
                        pe.wait_ge(ht_c, KC * l + c - 2)
                    for t in range(NT):
                        b = bank[c % 3] if t < LT else bank[3 + c % 3]
                        o = (t % LT) * P
                        mm = pe.transpose(b[:, o:o + P], nl[:, t, :].rearrange("p (q c) -> p c q", c=KC)[:, c, :], ident)
                    mm.then_inc(xt_mm, 1)

            pe.wait_ge(const_ld, 48)
            for n in range(4):
                ada(n)
            pe.wait_ge(x_ld, 16 * NT)
            transpose_x(0)
            pe.wait_ge(ht_l, KC)
            pe.wait_ge(ht_c, KC)

            k_blk = 0
            for hg in range(2):
                base = 4 + 3 * hg
                if hg:
                    pe.wait_ge(S["o_ev"], NT * 4 * hg)

                def rotate(i):
                    pe.wait_ge(S["qraw"], i + 1)
                    if i >= 2:
                        pe.wait_ge(S["rope_done"], i - 1)
                    pe.matmul(bank[4 + i % 2][:, :], rot, qraw[i % 2], start=True, stop=True).then_inc(S["rot_mm"], 1)

                for part in range(2):
                    p = base + part
                    ring_wait(p)
                    w = slot(p).rearrange("p (c n) -> p c n", c=KC)
                    for hb in range(4):
                        i = 8 * hg + 4 * part + hb
                        if i >= 2:
                            pe.wait_ge(S["qraw"], i - 1)
                            pe.wait_ge(S["ctx_ev"], i - 1)
                        for c in range(KC):
                            pe.matmul(bank[i % 2][:, :], w[:, c, hb * P:(hb + 1) * P], hT[:, c, 0:SEQ],
                                      start=(c == 0), stop=(c == KC - 1))
                        for c in range(KC):
                            mm = pe.matmul(bank[2 + i % 2][:, 0:CTX], w[:, c, hb * P:(hb + 1) * P], hT[:, c, SEQ:TOK],
                                           start=(c == 0), stop=(c == KC - 1))
                        mm.then_inc(S["proj_mm"], 1)
                        if i % 8:
                            rotate(i - 1)
                    pe.wait_ge(S["proj_mm"], 8 * hg + 4 * part + 4)
                    pe.sem_inc(ring_used, 1)
                rotate(8 * hg + 7)
                p = base + 2
                ring_wait(p)
                w = slot(p).rearrange("p (c n) -> p c n", c=KC)
                for t in range(NT):
                    n = NT * hg + t
                    if t >= 2:
                        pe.wait_ge(S["v_ev"], n - 1)
                    for c in range(KC):
                        mm = pe.matmul(bank[6 + t % 2][:, :], hT[:, c, t * P:(t + 1) * P], w[:, c, :],
                                       start=(c == 0), stop=(c == KC - 1))
                    mm.then_inc(S["v_mm"], 1)
                pe.wait_ge(S["v_mm"], NT * (hg + 1))
                pe.sem_inc(ring_used, 1)

                units = attn_units()
                u0 = len(units) * hg
                pe.wait_ge(S["rope_done"], 8 * (hg + 1))
                pe.wait_ge(S["ctx_ev"], 8 * (hg + 1))
                pe.wait_ge(S["v_ev"], NT * (hg + 1))

                def scores(k):
                    hb, t = units[k]
                    u = u0 + k
                    b0, b1, b2 = (bank[3 * (k % 2) + j] for j in range(3))
                    if k >= 2:
                        pe.wait_ge(S["exped"], u - 1)
                    q = [qT[64 * m:64 * m + 64, hb, t * P:(t + 1) * P] for m in range(2)]
                    kl = [kT[64 * m:64 * m + 64, hb, 0:SEQ] for m in range(2)]
                    kc = [kT[64 * m:64 * m + 64, hb, SEQ:TOK] for m in range(2)]
                    if t < LT:
                        pe.matmul(b2[:, 0:CTX], q[0], kc[0], start=True, stop=True).then_inc(S["sc_half"], 1)
                        pe.matmul(b0[:, :], q[0], kl[0], start=True, stop=True)
                        pe.matmul(b1[:, :], q[1], kl[1], start=True, stop=True)
                        pe.wait_ge(S["sc_half"], LT * (u // NT) + t + 1)
                        mm = pe.matmul(b2[:, CTX:2 * CTX], q[1], kc[1], start=True, stop=True)
                    else:
                        pe.matmul(b0[:, 0:CTX], q[0], kc[0], start=True, stop=True)
                        mm = pe.matmul(b1[:, 0:CTX], q[1], kc[1], start=True, stop=True)
                    mm.then_inc(S["sc_mm"], 1)

                def turn_probs(k):
                    hb, t = units[k]
                    u = u0 + k
                    pe.wait_ge(S["pmix"], u + 1)
                    if t < LT:
                        if u >= 1:
                            pe.wait_ge(S["at_ev_lo"], u)
                        for kb in range(4):
                            mm = pe.transpose(bank[6][:, kb * P:(kb + 1) * P], PR[k % 2][:, 0, kb * P:(kb + 1) * P], ident)
                        mm.then_inc(S["at_mm"], 1)
                    else:
                        pe.sem_inc(S["at_mm"], 1)
                    if u >= 1:
                        pe.wait_ge(S["o_ev"], u)
                    for kb in (4, 5):
                        mm = pe.transpose(bank[7][:, (kb - 4) * P:(kb - 3) * P], PR[k % 2][:, 0, kb * P:(kb + 1) * P], ident)
                    mm.then_inc(S["at_mm"], 1)

                def av(k):
                    hb, t = units[k]
                    u = u0 + k
                    pe.wait_ge(S["at_ev_lo"], u + 1)
                    pe.wait_ge(S["at_ev_hi"], u + 1)
                    blocks = list(range(NT)) if t < LT else [4, 5]
                    for kb in blocks:
                        mm = pe.matmul(bank[7][:, 256:384], aT[k % 2][:, kb, :], vA[:, kb, hb * P:(hb + 1) * P],
                                       start=(kb == blocks[0]), stop=(kb == blocks[-1]))
                    mm.then_inc(S["o_mm"], 1)

                scores(0)
                scores(1)
                for k in range(len(units)):
                    turn_probs(k)
                    if k + 2 < len(units):
                        scores(k + 2)
                    av(k)

            def mixer_out(l):
                q = turns(l)
                n = TILES[l]
                w0 = [p for p, it in enumerate(STREAM) if it[0] == "wo" and it[1] == l]
                wv = [slot(p).rearrange("p (c n) -> p c n", c=KC) for p in w0]
                src = [oall, R1][l]

                def turn(k):
                    kind, t = q[k]
                    if k >= 1:
                        pe.wait_ge(L[l]["turn_ev"], after(l, "turn_ev", k))
                    if kind == "o":
                        pe.wait_ge(L[l]["on_rdy"], after(l, "on_rdy", t + 1))
                        s = src[:, t, :]
                    else:
                        pe.wait_ge(L[l]["hf_rdy"], after(l, "hf_rdy", t + 1))
                        s = HF[t % 2]
                    for c in range(KC):
                        mm = pe.transpose(bank[2 + c // 4][:, (c % 4) * P:(c % 4 + 1) * P],
                                          s.rearrange("p (q c) -> p c q", c=KC)[:, c, :], ident)
                    mm.then_inc(L[l]["turn_mm"], 1)

                def use(k):
                    kind, t = q[k]
                    pe.wait_ge(L[l]["turn_ev"], after(l, "turn_ev", k + 1))
                    if kind == "o":
                        if t == 0:
                            ring_wait(w0[0])
                            ring_wait(w0[1])
                        if t >= 2:
                            pe.wait_ge(L[l]["z_done"], after(l, "z_done", t - 1))
                        for h in range(2):
                            for c in range(KC):
                                mm = pe.matmul(bank[4 * (t % 2) + h][:, :], oT[k % 2][:, c, :], wv[h][:, c, :],
                                               start=(c == 0), stop=(c == KC - 1))
                        mm.then_inc(L[l]["y_mm"], 1)
                        pe.wait_ge(L[l]["y_mm"], after(l, "y_mm", t + 1))
                        pe.sem_inc(L[l]["turn_use"], 1)
                    else:
                        if t == 0:
                            pe.wait_ge(S["routerw_ld"], 16 * (l + 1))
                        for c in range(KC):
                            mm = pe.matmul(bank[6][:, t * 16:(t + 1) * 16], oT[k % 2][:, c, :], rwt[:, c, :],
                                           start=(c == 0), stop=(c == KC - 1), skip_group_check=True)
                        mm.then_inc(L[l]["turn_use"], 1)

                turn(0)
                for k in range(len(q)):
                    if k + 1 < len(q):
                        turn(k + 1)
                    use(k)
                    if l == 0:
                        for m in ADA_AFTER.get(q[k], ()):
                            ada(m)

            def ranks(l):
                n = TILES[l]
                Mv, PM = RT[:, 0:n * 16], RT[:, 96:96 + n * 16]
                tot = RT[:, 96 + n * 16:112 + n * 16]
                pe.wait_ge(L[l]["mask"], after(l, "mask", 1))
                pe.matmul(bank[6][:, 0:n * 16], tri, Mv, start=True, stop=False, skip_group_check=True)
                pe.matmul(bank[6][:, 0:n * 16], ones, PM, start=False, stop=True, skip_group_check=True)
                pe.matmul(bank[5][:, 0:16], ones, tot, start=True, stop=True).then_inc(L[l]["rank_mm"], 1)

            def moe(l):
                E = L[l]
                base = MOEBASE[l]

                def turn(j, first=False):
                    pe.wait_ge(E["gath"], 16 * (j + 1))
                    if not first:
                        pe.wait_ge(E["xt_a"], j)
                        pe.wait_ge(E["xt_v"], j)
                    for c in range(KC):
                        mm = pe.transpose(bank[c // 4][:, (c % 4) * P:(c % 4 + 1) * P],
                                          xrow.rearrange("p (q c) -> p c q", c=KC)[:, c, :], ident)
                    mm.then_inc(E["xt"], 1)

                pe.wait_ge(E["tbl"], 1)
                pe.sem_inc(E["yd_mm"], 1)
                nb = pe.value_load(inclI[0:1, NE - 1:NE], min_val=2, max_val=MAXB[l] + 1)
                turn(0, True)
                sl = EXPERT_SLOTS[l]
                uses = [loads(base + i) - 1 for i in range(3)]
                uses1 = [loads(base + 3 + i) - 1 for i in range(3)]
                with pe.Fori(0, MAXB[l]) as j:
                    with pe.If(j + 1 < nb):
                        par = pe.value_load(peI[0:1, bass.ds(3 * j, 1)], min_val=0, max_val=1)
                        h0 = pe.value_load(peI[0:1, bass.ds(3 * j + 1, 1)], min_val=0, max_val=16 * 17)
                        h1 = pe.value_load(peI[0:1, bass.ds(3 * j + 2, 1)], min_val=0, max_val=16 * 17)

                        def weights(i, cols):
                            step = (sl[i + 3] - sl[i]) * SLOT
                            pe.wait_ge(ring_ld[sl[i]], h0 + 16 * uses[i])
                            pe.wait_ge(ring_ld[sl[i + 3]], h1 + 16 * uses1[i])
                            return lambda c, o, n: ring[:, bass.ds(sl[i] * SLOT + par * step + c * cols + o, n)]

                        pe.wait_ge(E["xt_a"], j + 1)
                        pe.wait_ge(E["xt_v"], j + 1)
                        w = weights(0, FE)
                        for c in range(KC):
                            mm = pe.matmul(bank[3][:, :], xT[:, c, :], w(c, 0, FE), start=(c == 0), stop=(c == KC - 1))
                        mm.then_inc(E["u_mm"], 1)
                        w = weights(1, FE)
                        for h in range(2):
                            for c in range(KC):
                                mm = pe.matmul(gbank[h], xT[:, c, :], w(c, h * 256, 256), start=(c == 0), stop=(c == KC - 1))
                            mm.then_inc(E["g_mm"], 1)

                        def turn_gate(h):
                            pe.wait_ge(E["gmul"], 2 * j + h + 1)
                            for c in (2 * h, 2 * h + 1):
                                mm = pe.transpose(gtbank[h][:, (c % 2) * P:(c % 2 + 1) * P], gate[:, c * P:(c + 1) * P], ident)
                            mm.then_inc(E["gt_mm"], 1)

                        turn_gate(0)
                        turn(j + 1)
                        turn_gate(1)
                        w = weights(2, D)
                        pe.wait_ge(E["y_a"], j + 1)
                        pe.wait_ge(E["y_v"], j + 1)
                        for h in range(2):
                            pe.wait_ge(E["gt_ev"], 2 * j + h + 1)
                            for o in range(2):
                                for c in (2 * h, 2 * h + 1):
                                    mm = pe.matmul(bank[5 + o][:, :], gT[:, c, :], w(c, o * 512, 512), start=(c == 0), stop=(c == 3),
                                                   skip_group_check=True)
                        mm.then_inc(E["yd_mm"], 1)

            pe.wait_ge(S["o_ev"], 48)
            for n in range(4, 8):
                ada(n)
            mixer_out(0)
            for n in (17, 18):
                ada(n)
            ranks(0)
            for n in range(19, 24):
                ada(n)
            moe(0)

            pe.wait_ge(L[0]["xfin"], NT)
            transpose_x(1)
            pe.wait_ge(ht_l, 2 * KC)
            pe.wait_ge(ht_c, 2 * KC)
            for i in range(8):
                part, h = divmod(i, 4)
                p = GLA0 + part
                if h == 0:
                    ring_wait(p)
                w = slot(p).rearrange("p (c n) -> p c n", c=KC)
                if i >= 2:
                    pe.wait_ge(S["gq_ev"], i - 1)
                for c in range(KC):
                    mm = pe.matmul(bank[i % 2][:, :], w[:, c, h * P:(h + 1) * P], hT[:, c, 0:SEQ], start=(c == 0), stop=(c == KC - 1))
                mm.then_inc(S["gq_mm"], 1)
                if part:
                    if h >= 2:
                        pe.wait_ge(S["gk_ev"], h - 1)
                    for c in range(KC):
                        mm = pe.matmul(bank[2 + i % 2][:, 0:CTX], w[:, c, h * P:(h + 1) * P], hT[:, c, SEQ:TOK],
                                       start=(c == 0), stop=(c == KC - 1))
                    mm.then_inc(S["gk_mm"], 1)
                if h == 3:
                    pe.wait_ge(S["gq_mm"], i + 1)
                    if part:
                        pe.wait_ge(S["gk_mm"], 4)
                    pe.sem_inc(ring_used, 1)
            pe.wait_ge(S["gw_ld"], 64)
            pe.wait_ge(S["wz"], 2)
            pe.wait_ge(S["gq_ev"], 8)
            for c in range(KC):
                pe.matmul(bank[0][0:64, :], wdn[:, c, :], hT[:, c, 0:SEQ], start=(c == 0), stop=(c == KC - 1))
            for c in range(KC):
                mm = pe.matmul(bank[1][0:64, 0:CTX], wdn[:, c, :], hT[:, c, SEQ:TOK], start=(c == 0), stop=(c == KC - 1))
            mm.then_inc(S["gd_mm"], 1)
            pe.wait_ge(S["gd_ev"], 1)
            pe.wait_ge(S["gk_ev"], 4)

            def project(n):
                j, t = vr_tiles[n]
                p = GLA0 + j
                if t == 0:
                    ring_wait(p)
                w = slot(p).rearrange("p (c n) -> p c n", c=KC)
                if n >= 2:
                    pe.wait_ge(S["gv_ev"], n - 1)
                for c in range(KC):
                    mm = pe.matmul(bank[6 + n % 2][:, :], hT[:, c, t * P:(t + 1) * P], w[:, c, :], start=(c == 0), stop=(c == KC - 1))
                mm.then_inc(S["gv_mm"], 1)
                if n + 1 == len(vr_tiles) or vr_tiles[n + 1][0] != j:
                    pe.wait_ge(S["gv_mm"], n + 1)
                    pe.sem_inc(ring_used, 1)

            def gates(h):
                if h:
                    pe.wait_ge(S["ls_done"], 3 * h)
                for d in range(2):
                    b0, b1 = bank[2 * d], bank[2 * d + 1]
                    w = wup[32 * d:32 * d + RANK, h * P:(h + 1) * P]
                    g = gdT[32 * d:32 * d + RANK, :]
                    pe.matmul(b0[:, :], w, g[:, 0:SEQ], start=True, stop=True)
                    pe.matmul(b1[:, 0:CTX], w, g[:, SEQ:TOK], start=True, stop=True).then_inc(S["gu_mm"], 1)

            def level(h, k):
                lv = 8 * h + k
                if lv >= 2:
                    pe.wait_ge(S["lv_ev"], lv - 1)
                if k:
                    pe.wait_ge(S["lv_mul"], 7 * h + k)
                src = QK[:, h] if k == 0 else LVB[(7 * h + k - 1) % 3]
                for b in range(4):
                    mm = pe.matmul(bank[4 + lv % 2][:, b * P:(b + 1) * P], src[:, 1, b * P:(b + 1) * P],
                                   src[:, 0, b * P:(b + 1) * P], start=True, stop=True, skip_group_check=True)
                mm.then_inc(S["lv_mm"], 1)

            def off_diagonal(h, g):
                if g == 0:
                    pe.wait_ge(S["tl_done"], h + 1)
                    if h:
                        pe.wait_ge(S["go_ev"], 4 * h)
                        pe.wait_ge(S["gss"], 4 * h)
                if g == 2:
                    pe.wait_ge(S["off_ev"], 3 * h + 1)
                tl = TL[h % 2]
                for n in range(4 * g, 4 * g + 4):
                    s, t = OFF[n]
                    far = abs(s - t) > 1 or {s, t} == {1, 2}
                    if s < t:
                        kk = VARO[:, 0, :] if (s == 0 and far) else tl[:, 1, s * P:(s + 1) * P]
                        qq = VARO[:, 1, :] if (t == 3 and far) else tl[:, 0, t * P:(t + 1) * P]
                    else:
                        kk = VARO[:, 2, :] if (s == 3 and far) else tl[:, 3, s * P:(s + 1) * P]
                        qq = VARO[:, 3, :] if (t == 0 and far) else tl[:, 2, t * P:(t + 1) * P]
                    mm = pe.matmul(bank[6 + g % 2][:, (n % 4) * P:(n % 4 + 1) * P], kk, qq, start=True, stop=True, skip_group_check=True)
                mm.then_inc(S["off_mm"], 1)

            def context_keys(h):
                pe.wait_ge(S["kc_done"], h + 1)
                pe.wait_ge(S["off_ev"], 3 * h + 2)
                for d in range(2):
                    for t in range(CT):
                        mm = pe.transpose(bank[7][:, (2 * d + t) * P:(2 * d + t + 1) * P], KXG[:, d, t * P:(t + 1) * P], ident)
                mm.then_inc(S["kc_mm"], 1)

            def context_states(h):
                pe.wait_ge(S["kc_ev"], h + 1)
                pe.wait_ge(S["off_ev"], 3 * h + 3)
                for d in range(2):
                    for t in range(CT):
                        mm = pe.matmul(bank[6][:, d * DV:(d + 1) * DV], KXT[:, d, t, :], V1[:, LT + t, h * DV:(h + 1) * DV],
                                       start=(t == 0), stop=(t == CT - 1), skip_group_check=True)
                mm.then_inc(S["st_mm"], 1)

            def outputs(h, t):
                if t == 0:
                    pe.wait_ge(S["lv_ev"], 8 * h + 8)
                    pe.wait_ge(S["st_ev"], h + 1)
                if t >= 2:
                    pe.wait_ge(S["go_ev"], 4 * h + t - 1)
                    pe.wait_ge(S["gss"], 4 * h + t - 1)
                b = bank[6 + t % 2]
                for s in range(LT):
                    lhs = SD[h % 2][:, t, :] if s == t else SO[:, OFF.index((s, t)), :]
                    pe.matmul(b[:, 0:DV], lhs, V1[:, s, h * DV:(h + 1) * DV], start=(s == 0), stop=False)
                qf = TL[h % 2][:, 0, 0:P] if t == 0 else VARD[h % 2][:, t - 1, :]
                qb = TL[h % 2][:, 2, 3 * P:4 * P] if t == 3 else VARD[h % 2][:, 3 + t, :]
                pe.matmul(b[:, 0:DV], qf, ST[:, 0, :], start=False, stop=False)
                pe.matmul(b[:, 0:DV], qb, ST[:, 1, :], start=False, stop=True).then_inc(S["go_mm"], 1)

            gates(0)
            for h in range(GH):
                for k in range(8):
                    level(h, k)
                    if k == 0 and h + 1 < GH:
                        gates(h + 1)
                    if h == 0:
                        for n in range(VR_CUT[k], VR_CUT[k + 1]):
                            project(n)
                    elif k < 4:
                        outputs(h - 1, k)
                    elif k == 4:
                        off_diagonal(h, 0)
                        off_diagonal(h, 1)
                    elif k == 5:
                        off_diagonal(h, 2)
                        context_keys(h)
                    elif k == 6:
                        context_states(h)
                if h == 0:
                    pe.wait_ge(S["gv_ev"], len(vr_tiles))
                    for g in range(3):
                        off_diagonal(h, g)
                    context_keys(h)
                    context_states(h)
            for t in range(LT):
                outputs(GH - 1, t)
            mixer_out(1)
            ranks(1)
            moe(1)

        @block.scalar
        def _(act):
            cnt = [0]

            def link(ins):
                cnt[0] += 1
                ins.then_inc(S["act"], 1)
                act.wait_ge(S["act"], cnt[0])

            act.wait_ge(const_ld, 48)
            act.activation(c_act, c_raw, ACT.Silu).then_inc(silu_c, 1)

            def context_h(l):
                act.wait_ge(modc_ld, 16 * 2 * (l + 1))
                mvv = modc[l].rearrange("p (v s c) -> p v s c", v=2, s=2)
                for c in range(KC):
                    act.wait_ge(xt_mm, KC * l + c + 1)
                    act.activation(hT[:, c, SEQ:TOK], bank[3 + c % 3][:, 0:CTX], ACT.Identity,
                                   bias=mvv[:, 0, 1, c:c + 1], scale=mvv[:, 1, 1, c:c + 1]).then_inc(ht_c, 1)

            act.wait_ge(S["lam_a"], 1)
            act.activation(lam4[:, 2:4], lam4[:, 0:2], ACT.Exp).then_inc(S["lam_b"], 1)
            context_h(0)
            for hg in range(2):
                if hg:
                    act.wait_ge(S["o_mm"], NT * 4 * hg)
                for i in range(8 * hg, 8 * hg + 8):
                    hb, dst = i % 4, (qT, kT)[(i % 8) // 4]
                    act.wait_ge(S["proj_mm"], i + 1)
                    if i >= 2:
                        act.wait_ge(S["rot_mm"], i - 1)
                        act.wait_ge(S["rope_cos"], i - 1)
                    act.activation(qraw[i % 2], bank[i % 2][:, :], ACT.Copy).then_inc(S["qraw"], 1)
                    act.activation(dst[:, hb, SEQ:TOK], bank[2 + i % 2][:, 0:CTX], ACT.Copy).then_inc(S["ctx_ev"], 1)
                for t in range(NT):
                    act.wait_ge(S["v_mm"], NT * hg + t + 1)
                    act.activation(vA[:, t, :], bank[6 + t % 2][:, :], ACT.Copy).then_inc(S["v_ev"], 1)
                units = attn_units()
                scale = float(HD) ** -0.5

                def probs(k):
                    hb, t = units[k]
                    u = len(units) * hg + k
                    b0, b1, b2 = (bank[3 * (k % 2) + j] for j in range(3))
                    st = st_a[k % 4]
                    if u >= 2:
                        act.wait_ge(S["at_mm"], 2 * u - 2)
                    if k == 0:
                        act.wait_ge(S["rope_done"], 8 * hg + 8)
                    act.wait_ge(S["maxed"], u + 1)
                    if t < LT:
                        for m in range(2):
                            act.activation(PR[k % 2][:, m, 0:SEQ], (b0, b1)[m][:, :], ACT.Exp, bias=st[:, 4 + m:5 + m],
                                           scale=scale, accum_out=st[:, 6 + 2 * m:7 + 2 * m])
                    for m in range(2):
                        src = b2[:, m * CTX:(m + 1) * CTX] if t < LT else (b0, b1)[m][:, 0:CTX]
                        ins = act.activation(PR[k % 2][:, m, SEQ:TOK], src, ACT.Exp,
                                             bias=st[:, 4 + m:5 + m], scale=scale, accum_out=st[:, 7 + 2 * m:8 + 2 * m])
                    ins.then_inc(S["exped"], 1)

                def out(k):
                    hb, t = units[k]
                    u = len(units) * hg + k
                    h = 4 * hg + hb
                    act.wait_ge(S["at_mm"], 2 * u + 2)
                    if u >= 2:
                        act.wait_ge(S["o_mm"], u - 1)
                    act.activation(aT[k % 2][:, 4:6, :], bank[7][:, 0:2 * P].rearrange("p (k q) -> p k q", k=2), ACT.Copy
                                   ).then_inc(S["at_ev_hi"], 1)

                def fin(k):
                    hb, t = units[k]
                    u = len(units) * hg + k
                    h = 4 * hg + hb
                    st = st_a[k % 4]
                    act.wait_ge(S["o_mm"], u + 1)
                    act.activation(oall[:, t, h * P:(h + 1) * P], bank[7][:, 256:384], ACT.Copy, scale=st[:, 12:13]
                                   ).then_inc(S["o_ev"], 1)

                def square(k):
                    hb, t = units[k]
                    u = len(units) * hg + k
                    h = 4 * hg + hb
                    act.wait_ge(S["o_ev"], u + 1)
                    if cnt[0]:
                        act.wait_ge(S["act"], cnt[0])
                    act.activation(squares, oall[:, t, h * P:(h + 1) * P], ACT.Square,
                                   accum_out=ss[:, t * HEADS + h:t * HEADS + h + 1]).then_inc(S["act"], 1)
                    cnt[0] += 1

                probs(0)
                for k in range(len(units)):
                    out(k)
                    if k:
                        square(k - 1)
                    if k + 1 < len(units):
                        probs(k + 1)
                    fin(k)
                square(len(units) - 1)
            act.wait_ge(S["act"], cnt[0])
            act.wait_ge(S["init"], 1)
            act.activation(rstd, ss, ACT.Sqrt, bias=epst, scale=1.0 / P).then_inc(S["rms_sqrt"], 1)

            def mixer_out(l):
                q = turns(l)
                for k in range(len(q)):
                    act.wait_ge(L[l]["turn_mm"], after(l, "turn_mm", k + 1))
                    if k >= 2:
                        act.wait_ge(L[l]["turn_use"], after(l, "turn_use", k - 1))
                    act.activation(oT[k % 2][:, 0:4, :], bank[2][:, :].rearrange("p (c t) -> p c t", c=4), ACT.Copy)
                    act.activation(oT[k % 2][:, 4:8, :], bank[3][:, :].rearrange("p (c t) -> p c t", c=4), ACT.Copy
                                   ).then_inc(L[l]["turn_ev"], 1)
                    if k and q[k - 1][0] == "o":
                        t = q[k - 1][1]
                        act.wait_ge(L[l]["bn"], after(l, "bn", t + 1))
                        if t:
                            act.wait_ge(L[l]["ln_n"], after(l, "ln_n", t))
                        act.activation(sd[:, 0:1], mv[:, 1:2], ACT.Sqrt, bias=epst).then_inc(L[l]["ln_sqrt"], 1)
                        act.wait_ge(L[l]["ln_r"], after(l, "ln_r", t + 1))
                        x = X[l][:, t, :]
                        act.activation(x, x, ACT.Identity, bias=nmu[:, 0:1], scale=sd[:, 0:1]).then_inc(L[l]["ln_n"], 1)
                n = TILES[l]
                act.wait_ge(L[l]["turn_use"], after(l, "turn_use", len(turns(l))))
                act.activation(RT[:, 208:208 + n * 16], bank[6][:, 0:n * 16], ACT.Sigmoid).then_inc(L[l]["aff"], 1)

            def moe(l):
                E = L[l]
                act.wait_ge(E["tbl"], 1)
                nb = act.value_load(inclI[0:1, NE - 1:NE], min_val=2, max_val=MAXB[l] + 1)

                def turned(j):
                    act.wait_ge(E["xt"], j + 1)
                    act.activation(xT[:, 4:8, :], bank[1][:, :].rearrange("p (c t) -> p c t", c=4), ACT.Copy).then_inc(E["xt_a"], 1)

                act.sem_inc(E["y_a"], 1)
                act.wait_ge(E["yfill"], 16)
                act.dma_start(ypad[l][(MAXB[l] + 1) * P:, :], X[l][:, 0, :]).then_inc(E["y_st"], 16)
                turned(0)
                with act.Fori(0, MAXB[l]) as j:
                    with act.If(j + 1 < nb):
                        for h in range(2):
                            act.wait_ge(E["g_mm"], 2 * j + h + 1)
                            act.activation(gsil[:, h * 256:(h + 1) * 256], gbank[h], ACT.Silu).then_inc(E["silu"], 1)
                        turned(j + 1)
                        act.wait_ge(E["yd_mm"], j + 2)
                        act.wait_ge(E["y_st"], 16 * (j + 1))
                        act.activation(ysb[:, 0:512], bank[5][:, :], ACT.Copy).then_inc(E["y_a"], 1)
                        act.wait_ge(E["y_a"], j + 2)
                        act.wait_ge(E["y_v"], j + 2)
                        act.dma_start(ypad[l][bass.ds(j * P, P), :], ysb).then_inc(E["y_st"], 16)
                stores = act.value_load(countI[0:1, 0:1], min_val=16, max_val=16 * 28)
                act.wait_ge(E["y_st"], stores)
                act.sem_inc(E["y_all"], 1)
                n = TILES[l]

                def scale(t):
                    ya = yab[l][2 * (t % 3)]
                    name = f"ya_ld{t % 3}"
                    act.wait_ge(E[name], after(l, name, 32 * (t // 3 + 1)))
                    act.activation(ya, ya, ACT.Copy, scale=W2[:, t:t + 1]).then_inc(E["ya_scaled"], 1)

                scale(0)
                scale(1)
                for t in range(n):
                    act.wait_ge(E["bn2"], after(l, "bn2", t + 1))
                    if t:
                        act.wait_ge(E["ln2_n"], after(l, "ln2_n", t))
                    act.activation(sd[:, 1:2], mv[:, 1:2], ACT.Sqrt, bias=epst).then_inc(E["ln2_sqrt"], 1)
                    act.wait_ge(E["ln2_r"], after(l, "ln2_r", t + 1))
                    x = X[l][:, t, :]
                    act.activation(x, x, ACT.Identity, bias=nmu[:, 1:2], scale=sd[:, 1:2]).then_inc(E["ln2_n"], 1)
                    if t + 2 < n:
                        scale(t + 2)

            mixer_out(0)
            moe(0)
            context_h(1)
            for i in range(8):
                part, h = divmod(i, 4)
                act.wait_ge(S["gq_mm"], i + 1)
                act.activation(QK[:, h, part, :], bank[i % 2][:, :], ACT.Copy, scale=(DK ** -0.5 if part == 0 else 1.0)
                               ).then_inc(S["gq_ev"], 1)
                if part:
                    act.wait_ge(S["gk_mm"], h + 1)
                    act.activation(KX[:, h, :], bank[2 + i % 2][:, 0:CTX], ACT.Copy).then_inc(S["gk_ev"], 1)
            act.wait_ge(S["gd_mm"], 1)
            act.activation(gdT[0:64, 0:SEQ], bank[0][0:64, :], ACT.Copy)
            act.activation(gdT[0:64, SEQ:TOK], bank[1][0:64, 0:CTX], ACT.Copy).then_inc(S["gd_ev"], 1)
            inv = 1.0 / TAU

            def project(n):
                j, t = vr_tiles[n]
                if j == 4 and t == 0:
                    act.wait_ge(S["xsave_st"], 16 * LT)
                act.wait_ge(S["gv_mm"], n + 1)
                dst = (V1 if j < 4 else R1)[:, t, (j % 2) * 512:(j % 2 + 1) * 512]
                act.activation(dst, bank[6 + n % 2][:, :], ACT.Copy if j < 4 else ACT.Silu).then_inc(S["gv_ev"], 1)

            def log_sigmoid(h, part):
                if part == 0:
                    if h:
                        act.wait_ge(S["ls_done"], 3 * h)
                    for d in range(2):
                        act.wait_ge(S["gu_mm"], 2 * h + d + 1)
                        bg = bgc[:, 4 * d + h:4 * d + h + 1]
                        act.activation(LS[:, d, 0:SEQ], bank[2 * d][:, :], ACT.Abs, bias=bg)
                        link(act.activation(LS[:, d, SEQ:TOK], bank[2 * d + 1][:, 0:CTX], ACT.Abs, bias=bg))
                else:
                    link(act.activation(LS[:, :, :], LS[:, :, :], ACT.Exp, scale=-1.0))
                    act.activation(LS[:, :, :], LS[:, :, :], ACT.Ln, bias=1.0).then_inc(S["ls_exp"], 1)

            def level(h, k):
                n = 7 * h + k
                act.wait_ge(S["lv_arg"], n + 1)
                act.activation(LVB[n % 3], LVB[n % 3], ACT.Exp, scale=inv).then_inc(S["lv_exp"], 1)

            bias = lambda n: bstot[:, n:n + 1]

            def decay_context(h):
                bf, bb = GB[h % 2][:, 0, :], GB[h % 2][:, 1, :]
                act.wait_ge(S["ls_done"], 3 * h + 3)
                if h:
                    act.wait_ge(S["kc_mm"], h)
                act.activation(KXG[:, 0, :], bf[:, SEQ:TOK], ACT.Exp, scale=-inv, bias=bias(ctot[h % 2]))
                act.activation(KXG[:, 1, :], bb[:, SEQ:TOK], ACT.Exp, scale=-inv, bias=bias(ctot[h % 2] + 1)).then_inc(S["kc_exp"], 1)

            def decay_blocks(h):
                bf, bb = GB[h % 2][:, 0, :], GB[h % 2][:, 1, :]
                tl = TL[h % 2]
                act.wait_ge(S["ls_done"], 3 * h + 3)
                if h >= 2:
                    act.wait_ge(S["go_mm"], 4 * (h - 1))
                act.activation(tl[:, 0, :], bf[:, 0:SEQ], ACT.Exp, scale=inv)
                act.activation(tl[:, 2, :], bb[:, 0:SEQ], ACT.Exp, scale=inv)
                for b in range(4):
                    act.activation(tl[:, 1, b * P:(b + 1) * P], bf[:, b * P:(b + 1) * P], ACT.Exp, scale=-inv, bias=bias(b))
                    act.activation(tl[:, 3, b * P:(b + 1) * P], bb[:, b * P:(b + 1) * P], ACT.Exp, scale=-inv, bias=bias(4 + b))
                if h:
                    act.wait_ge(S["tl_done"], h)
                act.activation(etot[:, 0:10], bstot[:, 12:22], ACT.Exp).then_inc(S["tl_exp"], 1)

            def off_diagonal(h, g):
                act.wait_ge(S["off_mm"], 3 * h + g + 1)
                if g == 0 and h:
                    act.wait_ge(S["go_mm"], 4 * h)
                act.activation(SO[:, 4 * g:4 * g + 4, :], bank[6 + g % 2][:, :].rearrange("p (k t) -> p k t", k=4), ACT.Copy
                               ).then_inc(S["off_ev"], 1)

            def context_keys(h):
                act.wait_ge(S["kc_mm"], h + 1)
                act.activation(KXT[:, :, :, :], bank[7][:, :].rearrange("p (d t e) -> p d t e", d=2, t=2), ACT.Copy
                               ).then_inc(S["kc_ev"], 1)

            def context_states(h):
                act.wait_ge(S["st_mm"], h + 1)
                act.activation(ST[:, :, :], bank[6][:, :].rearrange("p (d e) -> p d e", d=2), ACT.Copy).then_inc(S["st_ev"], 1)

            def square(h, t):
                act.wait_ge(S["go_ev"], 4 * h + t + 1)
                act.activation(bank[6 + t % 2][:, DV:2 * DV], bank[6 + t % 2][:, 0:DV], ACT.Square,
                               accum_out=ss[:, t * GH + h:t * GH + h + 1]).then_inc(S["gss"], 1)

            log_sigmoid(0, 0)
            log_sigmoid(0, 1)
            for h in range(GH):
                for k in range(8):
                    if k < 7:
                        level(h, k)
                    if h == 0 and k == 1:
                        decay_blocks(0)
                    if h + 1 < GH:
                        if k == 1:
                            log_sigmoid(h + 1, 0)
                        if k == 2:
                            log_sigmoid(h + 1, 1)
                    if h == 0:
                        for n in range(VR_CUT[k], VR_CUT[k + 1]):
                            project(n)
                        if k == 7:
                            act.wait_ge(S["gv_mm"], len(vr_tiles))
                            decay_context(0)
                            for g in range(3):
                                off_diagonal(0, g)
                            context_keys(0)
                            context_states(0)
                    else:
                        if 1 <= k < 5:
                            square(h - 1, k - 1)
                        if k == 4:
                            off_diagonal(h, 0)
                            off_diagonal(h, 1)
                        if k == 5:
                            off_diagonal(h, 2)
                            context_keys(h)
                        if k == 6:
                            context_states(h)
                    if h + 1 < GH:
                        if k == (6 if h else 7):
                            decay_context(h + 1)
                        if k == 7:
                            decay_blocks(h + 1)
            for t in range(LT):
                square(GH - 1, t)
            act.wait_ge(S["gss"], 16)
            act.activation(rstd[:, 0:16], ss[:, 0:16], ACT.Sqrt, bias=epst, scale=1.0 / DV).then_inc(S["rms_sqrt"], 1)
            mixer_out(1)
            moe(1)

        @block.vector
        def _(v):
            cnt = [0]

            def link(ins):
                cnt[0] += 1
                ins.then_inc(S["dve"], 1)
                v.wait_ge(S["dve"], cnt[0])

            def ada(n):
                j = STREAM[ADA_ITEMS[n]][2]
                v.wait_ge(ring_used, used_value(ADA_ITEMS[n]))
                if n == 4:
                    v.wait_ge(S["o_mm"], 48)
                if n == 0:
                    for i in range(2):
                        v.wait_ge(adab_ld[i], 32)
                if n >= 4:
                    v.wait_ge(adab_ld[n % 2], 16 * (n // 2 + 1))
                if n >= 6:
                    v.wait_ge(ada_st[n % 2], 16 * (n // 2))
                one = 1.0 if j in (2, 3, 8, 9) else 0.0
                v.scalar_tensor_tensor(adat[n], bank[7][0:2, :], one, adab[n], ALU.add, ALU.add).then_inc(ada_row, 1)

            def ada_sum(n):
                p, i = ADA_ITEMS[n], ADA_SUMMED.index(n)
                w = slot(p).rearrange("p (c n) -> p c n", c=KC)
                v.wait_ge(ring_ld[SLOT_OF[p]], 16 * loads(p))
                if i >= 2:
                    v.wait_ge(ring_used, used_value(ADA_ITEMS[ADA_SUMMED[i - 2]]))
                for c in range(CHUNKS_SUMMED):
                    for s in range(2):
                        f = c_act[:, s * KC + c:s * KC + c + 1]
                        if c >= 1:
                            v.wait_ge(S["dve"], cnt[0] - 1)
                        if c == 0:
                            ins = v.tensor_scalar(acc[i % 2][:, s, :], w[:, c, :], f, None, ALU.mult)
                        else:
                            ins = v.scalar_tensor_tensor(acc[i % 2][:, s, :], w[:, c, :], f, acc[i % 2][:, s, :], ALU.mult, ALU.add)
                        ins.then_inc(S["dve"], 1)
                        cnt[0] += 1
                v.wait_ge(S["dve"], cnt[0])
                v.sem_inc(S["ada_sum"], 1)

            def latent_h(l):
                v.wait_ge(modc_ld, 16 * 2 * (l + 1))
                mvv = modc[l].rearrange("p (v s c) -> p v s c", v=2, s=2)
                for c in range(KC):
                    v.wait_ge(xt_mm, KC * l + c + 1)
                    v.tensor_scalar(hT[:, c, 0:SEQ], bank[c % 3][:, :], mvv[:, 1, 0, c:c + 1], mvv[:, 0, 0, c:c + 1],
                                    ALU.mult, ALU.add).then_inc(ht_l, 1)

            v.memset(epst, EPS).then_inc(S["init"], 1)
            for n in range(4):
                ada(n)
            v.wait_ge(S["lam_ld"], 16)
            v.wait_ge(ada_row, 4)
            lv4 = lamv.rearrange("p (k d) -> p k d", k=4)
            for i in range(2):
                ins = v.tensor_tensor_reduce(out=Z[:, i * HD:(i + 1) * HD], in0=lv4[:, 2 * i, :], in1=lv4[:, 2 * i + 1, :], scale=1.0, scalar=0.0,
                                             op0=ALU.mult, op1=ALU.add, accum_out=lam4[:, i:i + 1])
            ins.then_inc(S["lam_a"], 1)
            v.wait_ge(S["lam_b"], 1)
            link(v.tensor_tensor(nlam, lam4[:, 3:4], lam4[:, 2:3], ALU.subtract))
            link(v.tensor_scalar(nlam, nlam, -LAMBDA0, None, ALU.add))
            latent_h(0)
            v.wait_ge(S["cs_ld"], 16)
            for hg in range(2):
                for i in range(8 * hg, 8 * hg + 8):
                    hb, dst = i % 4, (qT, kT)[(i % 8) // 4]
                    v.wait_ge(S["rot_mm"], i + 1)
                    v.wait_ge(S["rope_cos"], i + 1)
                    if i:
                        v.wait_ge(S["rope_done"], i)
                    link(v.tensor_tensor(rtmp, bank[4 + i % 2][:, :], sinT, ALU.mult))
                    v.tensor_tensor(dst[:, hb, 0:SEQ], dst[:, hb, 0:SEQ], rtmp, ALU.add).then_inc(S["rope_done"], 1)
                units = attn_units()
                scale = float(HD) ** -0.5

                def maxes(k):
                    hb, t = units[k]
                    b = bank[3 * (k % 2):3 * (k % 2) + 3]
                    st = st_a[k % 4]
                    u = len(units) * hg + k
                    if k >= 4:
                        v.wait_ge(S["o_ev"], u - 3)
                    v.wait_ge(S["sc_mm"], u + 1)
                    w = SEQ if t < LT else CTX
                    v.tensor_reduce(st[:, 0:1], b[0][:, 0:w], AX.X, ALU.max)
                    ins = v.tensor_reduce(st[:, 1:2], b[1][:, 0:w], AX.X, ALU.max)
                    if t < LT:
                        ins = v.tensor_reduce(st[:, 2:4], b[2][:, :].rearrange("p (m k) -> p m k", m=2), AX.X, ALU.max)
                    link(ins)
                    if t < LT:
                        link(v.tensor_tensor(st[:, 2:4], st[:, 0:2], st[:, 2:4], ALU.max))
                    peak = st[:, 2:4] if t < LT else st[:, 0:2]
                    v.tensor_scalar(st[:, 4:6], peak, -scale, None, ALU.mult).then_inc(S["maxed"], 1)

                def mix(k):
                    hb, t = units[k]
                    st = st_a[k % 4]
                    u = len(units) * hg + k
                    v.wait_ge(S["exped"], u + 1)
                    r4 = st[:, 6:10].rearrange("p (m k) -> p m k", m=2)
                    if t < LT:
                        link(v.tensor_tensor(st[:, 10:12], r4[:, :, 0], r4[:, :, 1], ALU.add))
                    else:
                        link(v.tensor_copy(st[:, 10:12], r4[:, :, 1]))
                    link(v.reciprocal(st[:, 12:14], st[:, 10:12]))
                    link(v.scalar_tensor_tensor(st[:, 14:15], st[:, 10:11], st[:, 13:14], nlam, ALU.mult, ALU.mult))
                    lo = 0 if t < LT else SEQ
                    v.scalar_tensor_tensor(PR[k % 2][:, 0, lo:TOK], PR[k % 2][:, 1, lo:TOK], st[:, 14:15],
                                           PR[k % 2][:, 0, lo:TOK], ALU.mult, ALU.add).then_inc(S["pmix"], 1)

                def turned(k):
                    hb, t = units[k]
                    u = len(units) * hg + k
                    v.wait_ge(S["at_mm"], 2 * u + 1)
                    if u >= 2:
                        v.wait_ge(S["o_mm"], u - 1)
                    if t < LT:
                        v.tensor_copy(aT[k % 2][:, 0:4, :], bank[6][:, :].rearrange("p (k q) -> p k q", k=4)).then_inc(S["at_ev_lo"], 1)
                    else:
                        v.sem_inc(S["at_ev_lo"], 1)

                maxes(0)
                mix(0)
                maxes(1)
                for k in range(len(units)):
                    turned(k)
                    if k + 1 < len(units):
                        mix(k + 1)
                    if k + 2 < len(units):
                        maxes(k + 2)

            def rms_rows(l, between=()):
                nh, w = (HEADS, P) if l == 0 else (GH, DV)
                n = TILES[l]
                src = [oall, R1][l]
                v.wait_ge(S["rms_sqrt"], l + 1)
                link(v.reciprocal(rstd[:, 0:n * nh], rstd[:, 0:n * nh]))
                if l == 0:
                    link(v.tensor_scalar(rstd, rstd, 1.0 - LAMBDA0, None, ALU.mult))
                for t in range(n):
                    o = src[:, t, :].rearrange("p (h w) -> p h w", h=nh)
                    r = rstd[:, t * nh:(t + 1) * nh].unsqueeze(2).to_broadcast([P, nh, w])
                    link(v.tensor_tensor(o, o, r, ALU.mult))
                    g = normg[l].unsqueeze(1).to_broadcast([P, nh, w])
                    if t == 0:
                        v.wait_ge(L[l]["rows_ld"], after(l, "rows_ld", 16))
                    v.tensor_tensor(o, o, g, ALU.mult).then_inc(L[l]["on_rdy"], 1)
                    if between and t % 2:
                        ada(between[t // 2])

            def stats(l, t, x, name_bn, name_sqrt, name_r, col):
                link(v.bn_stats(bst[:, 0:6], x[:, 0:512]))
                link(v.bn_stats(bst[:, 6:12], x[:, 512:1024]))
                v.bn_aggr(mv, bst.rearrange("p (k s) -> p k s", k=2)).then_inc(L[l][name_bn], 1)
                v.wait_ge(L[l][name_bn], after(l, name_bn, t + 1))
                v.wait_ge(L[l][name_sqrt], after(l, name_sqrt, t + 1))
                link(v.reciprocal(sd[:, col:col + 1], sd[:, col:col + 1]))
                v.scalar_tensor_tensor(nmu[:, col:col + 1], mv[:, 0:1], -1.0, sd[:, col:col + 1], ALU.mult, ALU.mult
                                       ).then_inc(L[l][name_r], 1)

            def mixer_norm(l):
                for t in range(TILES[l]):
                    v.wait_ge(L[l]["y_mm"], after(l, "y_mm", t + 1))
                    if t == 0:
                        v.wait_ge(S["xres_ld"], 16 * (NT + (LT if l else 0)))
                    v.wait_ge(L[l]["rows2_ld"], after(l, "rows2_ld", 48 if t < LT else 64))
                    for h in range(2):
                        ins = v.tensor_tensor(Z[:, h * 512:(h + 1) * 512], bank[4 * (t % 2) + h][:, :], gm[:, h * 512:(h + 1) * 512], ALU.mult)
                    ins.then_inc(L[l]["z_done"], 1)
                    v.wait_ge(L[l]["z_done"], after(l, "z_done", t + 1))
                    x = X[l][:, t, :]
                    link(v.scalar_tensor_tensor(x, x, ALPHA, Z, ALU.mult, ALU.add))
                    stats(l, t, x, "bn", "ln_sqrt", "ln_r", 0)
                    if l == 0:
                        for n in ADA_AFTER.get(("o", t), ()):
                            ada(n)
                        ada_sum(ADA_SUMMED[t])

            def route(l, between=None):
                n = TILES[l]
                E = L[l]
                m = n * 16
                Mv, PM, aff = RT[:, 0:m], RT[:, 96:112 + m], RT[:, 208:208 + m]
                sel, rk, tmp = RT[:, 304:304 + m], RT[:, 400:400 + m], RT[:, 496:496 + m]
                gs, gk, gt = RT[:, 592:592 + 4 * n], RT[:, 616:616 + 4 * n], RT[:, 640:640 + 4 * n]
                AB = RT[:, 664:664 + 2 * m]
                t2 = RT[:, 856:856 + 2 * m]
                big = RT[:, 1048:1496]
                f1, f2, f3, f4 = (RT[:, 1496 + 12 * i:1496 + 12 * i + 2 * n] for i in range(4))
                nbk, incl, excl = RT[:, 1560:1576], RT[:, 1576:1592], RT[:, 1592:1608]
                E28, P28, pet = RT[:, 1608:1636], RT[:, 1636:1664], RT[:, 1664:1748]

                def rank4(s, r, t, groups):
                    s, r, t = (x.rearrange("p (g i) -> p g i", i=4) for x in (s, r, t))
                    link(v.memset(r, 0.0))
                    for d in range(1, 4):
                        link(v.tensor_tensor(t[:, :, 0:4 - d], s[:, :, 0:4 - d], s[:, :, d:4], ALU.is_ge))
                        link(v.tensor_tensor(r[:, :, d:4], r[:, :, d:4], t[:, :, 0:4 - d], ALU.add))
                        link(v.scalar_tensor_tensor(r[:, :, 0:4 - d], r[:, :, 0:4 - d], 1.0, t[:, :, 0:4 - d], ALU.add, ALU.subtract))

                v.wait_ge(E["aff"], after(l, "aff", 1))
                v.wait_ge(S["router_b_ld"], 16)
                a3 = aff.rearrange("p (t e) -> p t e", e=16)
                link(v.tensor_tensor(sel.rearrange("p (t e) -> p t e", e=16), a3, rb.unsqueeze(1).to_broadcast([P, n, 16]), ALU.add))
                rank4(sel, rk, tmp, 4 * n)
                link(v.scalar_tensor_tensor(tmp, rk, 2.0, sel, ALU.is_lt, ALU.mult))
                link(v.tensor_reduce(gs, tmp.rearrange("p (g i) -> p g i", i=4), AX.X, ALU.add))
                if between is not None:
                    ada(between)
                rank4(gs, gk, gt, n)
                link(v.tensor_scalar(gt, gk, 0.0, None, ALU.is_equal))
                g4 = gt.unsqueeze(2).to_broadcast([P, 4 * n, 4])
                r4 = rk.rearrange("p (g i) -> p g i", i=4)
                for k in range(2):
                    link(v.scalar_tensor_tensor(AB[:, k * m:(k + 1) * m].rearrange("p (g i) -> p g i", i=4), r4, float(k), g4,
                                                ALU.is_equal, ALU.mult))
                link(v.tensor_tensor(Mv, AB[:, 0:m], AB[:, m:2 * m], ALU.add))
                link(v.memset(PM[:, 0:16], 0.0))
                for t in range(n):
                    ins = v.tensor_tensor(PM[:, (t + 1) * 16:(t + 2) * 16], PM[:, t * 16:(t + 1) * 16], Mv[:, t * 16:(t + 1) * 16], ALU.add)
                    if t < n - 1:
                        link(ins)
                ins.then_inc(E["mask"], 1)
                ab3 = AB.rearrange("p (k e) -> p k e", k=2)
                t3 = t2.rearrange("p (k e) -> p k e", k=2)
                link(v.tensor_tensor(t3, ab3, aff.unsqueeze(1).to_broadcast([P, 2, m]), ALU.mult))
                w2 = W2[:, 0:2 * n]
                link(v.tensor_reduce(w2, t2.rearrange("p (k e) -> p k e", e=16), AX.X, ALU.add))
                link(v.tensor_tensor(f1[:, 0:n], w2[:, 0:n], w2[:, n:2 * n], ALU.add))
                link(v.reciprocal(f1[:, 0:n], f1[:, 0:n]))
                w3 = w2.rearrange("p (k t) -> p k t", k=2)
                link(v.tensor_tensor(w3, w3, f1[:, 0:n].unsqueeze(1).to_broadcast([P, 2, n]), ALU.mult))

            def route_2(l):
                n = TILES[l]
                E = L[l]
                m = n * 16
                AB, t2 = RT[:, 664:664 + 2 * m], RT[:, 856:856 + 2 * m]
                big = RT[:, 1048:1496]
                f1, f2, f3, f4 = (RT[:, 1496 + 12 * i:1496 + 12 * i + 2 * n] for i in range(4))
                nbk, incl, excl = RT[:, 1560:1576], RT[:, 1576:1592], RT[:, 1592:1608]
                E28, P28, pet = RT[:, 1608:1636], RT[:, 1636:1664], RT[:, 1664:1748]
                t3 = t2.rearrange("p (k t e) -> p k t e", k=2, e=16)
                ab4 = AB.rearrange("p (k t e) -> p k t e", k=2, e=16)
                v.wait_ge(E["rank_mm"], after(l, "rank_mm", 1))
                b6 = big[:, 0:96].rearrange("p (e k) -> p e k", k=6)
                link(v.tensor_tensor(b6, bank[5][:, 0:16].unsqueeze(2).to_broadcast([P, 16, 6]),
                                     kmul.unsqueeze(1).to_broadcast([P, 16, 6]), ALU.is_gt))
                link(v.tensor_reduce(nbk, b6, AX.X, ALU.add))
                link(v.tensor_tensor_scan(incl, ones[:, 0:16], nbk, 0.0, ALU.mult, ALU.add))
                link(v.tensor_tensor(excl, incl, nbk, ALU.subtract))
                rk3 = bank[6][:, 0:m].unsqueeze(1).to_broadcast([P, 2, m])
                link(v.tensor_tensor(t2.rearrange("p (k e) -> p k e", k=2), AB.rearrange("p (k e) -> p k e", k=2), rk3, ALU.mult))
                link(v.tensor_reduce(f1, t2.rearrange("p (k e) -> p k e", e=16), AX.X, ALU.add))
                link(v.tensor_tensor(t2.rearrange("p (k e) -> p k e", e=16), AB.rearrange("p (k e) -> p k e", e=16),
                                     excl.unsqueeze(1).to_broadcast([P, 2 * n, 16]), ALU.mult))
                link(v.tensor_reduce(f2, t2.rearrange("p (k e) -> p k e", e=16), AX.X, ALU.add))
                b5 = big[:, 0:10 * n].rearrange("p (t k) -> p t k", k=5)
                link(v.tensor_tensor(b5, f1.unsqueeze(2).to_broadcast([P, 2 * n, 5]),
                                     kmul[:, 1:6].unsqueeze(1).to_broadcast([P, 2 * n, 5]), ALU.is_ge))
                link(v.tensor_reduce(f3, b5, AX.X, ALU.add))
                link(v.tensor_tensor(f2, f2, f3, ALU.add))
                link(v.scalar_tensor_tensor(f1, f3, -float(P), f1, ALU.mult, ALU.add))
                link(v.scalar_tensor_tensor(f4, f2, float(P), f1, ALU.mult, ALU.add))
                link(v.scalar_tensor_tensor(f3, f1, 28.0, f2, ALU.mult, ALU.add))
                link(v.tensor_copy(destI[:, 0:2 * n], f4))
                link(v.tensor_copy(addrI[:, 0:2 * n], f3))
                link(v.tensor_copy(tidI, tidf))
                v.sem_inc(E["dest"], 1)
                b28 = big.rearrange("p (j e) -> p j e", e=16)
                link(v.tensor_tensor(b28, incl.unsqueeze(1).to_broadcast([P, 28, 16]), jrow.unsqueeze(2).to_broadcast([P, 28, 16]), ALU.is_le))
                link(v.tensor_reduce(E28, b28, AX.X, ALU.add))
                link(v.tensor_tensor(b28, b28, sgn.unsqueeze(1).to_broadcast([P, 28, 16]), ALU.mult))
                link(v.tensor_reduce(P28, b28, AX.X, ALU.add))
                p3 = pet.rearrange("p (j k) -> p j k", k=3)
                link(v.tensor_scalar(E28, E28, 8.0, None, ALU.mult))
                link(v.tensor_copy(p3[:, :, 0], P28))
                link(v.scalar_tensor_tensor(p3[:, :, 1], P28, -8.0, E28, ALU.mult, ALU.add))
                link(v.tensor_scalar(p3[:, :, 1], p3[:, :, 1], 16.0, None, ALU.add))
                link(v.scalar_tensor_tensor(p3[:, :, 2], P28, 8.0, E28, ALU.mult, ALU.add))
                link(v.tensor_copy(peI, pet))
                link(v.tensor_scalar(f1[:, 0:1], incl[:, NE - 1:NE], 16.0, 16.0, ALU.mult, ALU.add))
                link(v.tensor_scalar(f1[:, 1:2], incl[:, NE - 1:NE], -16.0, 16.0 * (MAXB[l] + 1), ALU.mult, ALU.add))
                link(v.tensor_copy(countI, f1[:, 0:2]))
                link(v.tensor_scalar(incl, incl, 1.0, None, ALU.add))
                v.tensor_copy(inclI, incl).then_inc(E["tbl"], 1)

            def moe(l):
                E = L[l]
                v.wait_ge(E["tbl"], 1)
                nb = v.value_load(inclI[0:1, NE - 1:NE], min_val=2, max_val=MAXB[l] + 1)

                def turned(j):
                    v.wait_ge(E["xt"], j + 1)
                    v.tensor_copy(xT[:, 0:4, :], bank[0][:, :].rearrange("p (c t) -> p c t", c=4)).then_inc(E["xt_v"], 1)

                v.sem_inc(E["y_v"], 1)
                turned(0)
                with v.Fori(0, MAXB[l]) as j:
                    with v.If(j + 1 < nb):
                        v.wait_ge(E["u_mm"], j + 1)
                        for h in range(2):
                            v.wait_ge(E["silu"], 2 * j + h + 1)
                            cols = slice(h * 256, (h + 1) * 256)
                            v.tensor_tensor(gate[:, cols], bank[3][:, cols], gsil[:, cols], ALU.mult).then_inc(E["gmul"], 1)
                        for h in range(2):
                            v.wait_ge(E["gt_mm"], 2 * j + h + 1)
                            v.tensor_copy(gT[:, 2 * h:2 * h + 2, :], gtbank[h].rearrange("p (c t) -> p c t", c=2)).then_inc(E["gt_ev"], 1)
                        turned(j + 1)
                        v.wait_ge(E["yd_mm"], j + 2)
                        v.wait_ge(E["y_st"], 16 * (j + 1))
                        v.tensor_copy(ysb[:, 512:1024], bank[6][:, :]).then_inc(E["y_v"], 1)
                n = TILES[l]
                for t in range(n):
                    x = X[l][:, t, :]
                    ya, yb = yab[l][2 * (t % 3)], yab[l][2 * (t % 3) + 1]
                    v.wait_ge(E["ya_scaled"], after(l, "ya_scaled", t + 1))
                    if t == 0:
                        v.wait_ge(E["rows3_ld"], after(l, "rows3_ld", 64 if l == 0 else 48))
                    link(v.scalar_tensor_tensor(ya, yb, W2[:, n + t:n + t + 1], ya, ALU.mult, ALU.add))
                    v.tensor_tensor(ya, ya, gm if t < LT else gmc, ALU.mult).then_inc(E["z2_done"], 1)
                    v.wait_ge(E["z2_done"], after(l, "z2_done", t + 1))
                    link(v.scalar_tensor_tensor(x, x, ALPHA, ya, ALU.mult, ALU.add))
                    stats(l, t, x, "bn2", "ln2_sqrt", "ln2_r", 1)

            ada(4)
            rms_rows(0, between=(5, 6, 7))
            mixer_norm(0)
            ada(15)
            ada(16)
            route(0, between=17)
            ada(18)
            route_2(0)
            for n in range(19, 24):
                ada(n)
            moe(0)
            latent_h(1)
            v.wait_ge(ht_l, 2 * KC)
            v.wait_ge(S["mask_ld"], 16)

            def log_sigmoid(h, d):
                gb = GB[h % 2]
                v.wait_ge(S["ls_exp"], h + 1)
                bg = bgc[:, 4 * d + h:4 * d + h + 1]
                v.tensor_scalar(gb[:, d, 0:SEQ], bank[2 * d][:, :], bg, 0.0, ALU.add, ALU.min)
                link(v.tensor_scalar(gb[:, d, SEQ:TOK], bank[2 * d + 1][:, 0:CTX], bg, 0.0, ALU.add, ALU.min))
                link(v.tensor_tensor(LS[:, d, :], gb[:, d, :], LS[:, d, :], ALU.subtract))
                for o, w in [(b * P, P) for b in range(4)] + [(SEQ, CTX)]:
                    src, dst = LS[:, d, o:o + w], gb[:, d, o:o + w]
                    if d:
                        src, dst = src[:, ::-1], dst[:, ::-1]
                    one = ones[:, 0:1].to_broadcast([P, w])
                    ins = v.tensor_tensor_scan(dst, one, src, 0.0, ALU.mult, ALU.add)
                ins.then_inc(S["ls_done"], 1)

            def totals(h):
                gb = GB[h % 2]
                v.wait_ge(S["ls_done"], 3 * h + 2)
                tf = gb[:, 0, 0:SEQ].rearrange("p (b t) -> p b t", b=4)[:, :, P - 1]
                tb = gb[:, 1, 0:SEQ].rearrange("p (b t) -> p b t", b=4)[:, :, 0]
                v.tensor_scalar(bstot[:, 0:4], tf, 1.0 / TAU, None, ALU.mult)
                v.tensor_scalar(bstot[:, 4:8], tb, 1.0 / TAU, None, ALU.mult)
                v.tensor_scalar(bstot[:, ctot[h % 2]:ctot[h % 2] + 1], gb[:, 0, TOK - 1:TOK], 1.0 / TAU, None, ALU.mult)
                link(v.tensor_scalar(bstot[:, ctot[h % 2] + 1:ctot[h % 2] + 2], gb[:, 1, SEQ:SEQ + 1], 1.0 / TAU, None, ALU.mult))
                v.tensor_copy(bstot[:, 12:14], bstot[:, 1:3])
                v.tensor_copy(bstot[:, 14:15], bstot[:, 6:7])
                v.tensor_copy(bstot[:, 15:16], bstot[:, 5:6])
                v.tensor_copy(bstot[:, 16:17], bstot[:, 0:1])
                v.tensor_tensor(bstot[:, 17:18], bstot[:, 0:1], bstot[:, 1:2], ALU.add)
                v.tensor_copy(bstot[:, 21:22], bstot[:, 7:8])
                link(v.tensor_tensor(bstot[:, 20:21], bstot[:, 7:8], bstot[:, 6:7], ALU.add))
                v.tensor_tensor(bstot[:, 18:19], bstot[:, 17:18], bstot[:, 2:3], ALU.add)
                v.tensor_tensor(bstot[:, 19:20], bstot[:, 20:21], bstot[:, 5:6], ALU.add).then_inc(S["ls_done"], 1)

            def level(h, k):
                n = 7 * h + k
                v.wait_ge(S["lv_exp"], n + 1)
                v.tensor_tensor(LVB[n % 3], LVB[n % 3], QK[:, h], ALU.mult).then_inc(S["lv_mul"], 1)

            def diag(h, k):
                i = 8 * h + k
                v.wait_ge(S["lv_mm"], i + 1)
                ps = bank[4 + i % 2][:, :].rearrange("p (b t) -> p b t", b=4)
                mk = maskv[:, k, :].unsqueeze(1).to_broadcast([P, 4, P])
                if k == 0:
                    if h >= 2:
                        v.wait_ge(S["go_mm"], 4 * (h - 1))
                    v.tensor_tensor(SD[h % 2], ps, mk, ALU.mult).then_inc(S["lv_ev"], 1)
                else:
                    v.wait_ge(S["lv_ev"], i)
                    v.copy_predicated(SD[h % 2], mk.bitcast(I32), ps).then_inc(S["lv_ev"], 1)

            def decay_context(h):
                v.wait_ge(S["kc_exp"], h + 1)
                for d in range(2):
                    ins = v.tensor_tensor(KXG[:, d, :], KXG[:, d, :], KX[:, h, :], ALU.mult)
                ins.then_inc(S["kc_done"], 1)

            def decay_blocks(h):
                tl = TL[h % 2]
                v.wait_ge(S["tl_exp"], h + 1)
                for k in range(4):
                    ins = v.tensor_tensor(tl[:, k, :], tl[:, k, :], QK[:, h, k % 2, :], ALU.mult)
                link(ins)
                if h:
                    v.wait_ge(S["off_mm"], 3 * h)
                qf, kf, qb, kb = (tl[:, k, :].rearrange("p (b t) -> p b t", b=4) for k in range(4))
                for n, src in enumerate((kf[:, 0, :], qf[:, 3, :], kb[:, 3, :], qb[:, 0, :],
                                         qf[:, 1, :], qf[:, 2, :], qf[:, 3, :], qb[:, 0, :], qb[:, 1, :], qb[:, 2, :])):
                    dst = VARO[:, n, :] if n < 4 else VARD[h % 2][:, n - 4, :]
                    ins = v.tensor_scalar(dst, src, etot[:, n:n + 1], None, ALU.mult)
                ins.then_inc(S["tl_done"], 1)

            def outputs(h, t):
                v.wait_ge(S["go_mm"], 4 * h + t + 1)
                r = R1[:, t, h * DV:(h + 1) * DV]
                v.tensor_tensor(r, r, bank[6 + t % 2][:, 0:DV], ALU.mult).then_inc(S["go_ev"], 1)

            for d in range(2):
                log_sigmoid(0, d)
            totals(0)
            for h in range(GH):
                for k in range(8):
                    if k < 7:
                        level(h, k)
                    diag(h, k)
                    if h and k < 4:
                        outputs(h - 1, k)
                    if h + 1 < GH:
                        if k in (3, 4):
                            log_sigmoid(h + 1, k - 3)
                        if k == 5:
                            totals(h + 1)
                if h == 0:
                    v.wait_ge(S["gv_mm"], len(vr_tiles))
                    decay_context(0)
                    decay_blocks(0)
                if h + 1 < GH:
                    decay_context(h + 1)
                    decay_blocks(h + 1)
            for t in range(LT):
                outputs(GH - 1, t)
            v.wait_ge(S["go_ev"], 16)
            rms_rows(1)
            mixer_norm(1)
            route(1)
            route_2(1)
            moe(1)

        @block.gpsimd
        def _(g):
            cnt = [0]

            def link(ins):
                cnt[0] += 1
                ins.then_inc(S["pool"], 1)
                g.wait_ge(S["pool"], cnt[0])

            g.dma_start(lamv, a["attn_lambda"][0].rearrange("k d -> (k d)").unsqueeze(0).to_broadcast([P, 4 * HD])).then_inc(S["lam_ld"], 16)
            link(g.memset(idx32[:, :], 0))
            for l in range(2):
                g.dma_start(tokd[l].rearrange("(p j) o -> p (j o)", j=28), zfill).then_inc(S["tok_zero"], 16)
            g.dma_start(rb, a["router_b"].unsqueeze(0).to_broadcast([P, 16])).then_inc(S["router_b_ld"], 16)

            g.wait_ge(S["cs_ld"], 16)
            for i in range(16):
                hb, dst = i % 4, (qT, kT)[(i % 8) // 4]
                g.wait_ge(S["qraw"], i + 1)
                if i == 8:
                    g.wait_ge(S["o_mm"], 24)
                g.tensor_tensor(dst[:, hb, 0:SEQ], qraw[i % 2], cosT, ALU.mult).then_inc(S["rope_cos"], 1)
                if i % 8 == 7:
                    l = i // 8
                    g.wait_ge(S["v_mm"], NT * (l + 1))
                    g.dma_start(ypad[l][MINB[l] * P:, :].rearrange("(b p) n -> p b n", p=P),
                                cs[:, :].unsqueeze(1).to_broadcast([P, MAXB[l] + 2 - MINB[l], D])).then_inc(L[l]["yfill"], 16)

            def row(l, s, vec):
                return bcast_row(modd[l][s, vec * D:(vec + 1) * D], D)

            def small_rows(l):
                w = (P, DV)[l]
                gsrc = (a["attn_subln_g"][0], a["gla_norm_g"][0])[l]
                g.dma_start(normg[l], gsrc.unsqueeze(0).to_broadcast([P, w])).then_inc(L[l]["rows_ld"], 16)
                g.dma_start(rwt, a["router_w"].rearrange("(p c) e -> p c e", c=KC)).then_inc(S["routerw_ld"], 16)

            def mixer_rows(l):
                E = L[l]
                if l == 0:
                    small_rows(0)
                for t in range(TILES[l]):
                    src = xsave[t * P:(t + 1) * P, :] if l else (
                        a["x"][0][t * P:(t + 1) * P, :] if t < LT else a["ctx"][0][(t - LT) * P:(t - LT + 1) * P, :])
                    g.dma_start(X[l][:, t, :], src).then_inc(S["xres_ld"], 16)
                if l == 0:
                    for k in (4, 5):
                        g.wait_ge(ada_st[k % 2], 16 * (k // 2 + 1))
                g.dma_start(gm, row(l, 0, 2)).then_inc(E["rows2_ld"], 16)
                g.dma_start(lng, bcast_row(a["ln_g"][l, 0], D)).then_inc(E["rows2_ld"], 16)
                g.dma_start(lnb, bcast_row(a["ln_b"][l, 0], D)).then_inc(E["rows2_ld"], 16)
                if l == 0:
                    for k in (8, 9):
                        g.wait_ge(ada_st[k % 2], 16 * (k // 2 + 1))
                g.dma_start(scf, row(l, 0, 4)).then_inc(E["lgk"], 16)
                g.dma_start(shf, row(l, 0, 3)).then_inc(E["lgk"], 16)
                for t in range(TILES[l]):
                    x = X[l][:, t, :]
                    hf = HF[t % 2]
                    if t >= 2:
                        g.wait_ge(E[f"hf_st{t % 2}"], after(l, f"hf_st{t % 2}", 16 * (t // 2)))
                        g.wait_ge(E["turn_mm"], after(l, "turn_mm", turns(l).index(("r", t - 2)) + 1))
                    if t in (0, LT):
                        if t == 0:
                            g.wait_ge(E["rows2_ld"], after(l, "rows2_ld", 48))
                        g.wait_ge(E["lgk"], after(l, "lgk", 32 if t == 0 else 64))
                        link(g.tensor_tensor(hf, lnb, scf, ALU.mult))
                        link(g.tensor_tensor(shf, shf, hf, ALU.add))
                        link(g.tensor_tensor(scf, scf, lng, ALU.mult))
                    g.wait_ge(E["ln_n"], after(l, "ln_n", t + 1))
                    link(g.tensor_tensor(hf, x, scf, ALU.mult))
                    g.tensor_tensor(hf, hf, shf, ALU.add).then_inc(E["hf_rdy"], 1)
                    g.wait_ge(E["hf_rdy"], after(l, "hf_rdy", t + 1))
                    g.dma_start(hfd[l][t * P:(t + 1) * P, :], hf).then_inc(E[f"hf_st{t % 2}"], 16)
                    if l == 0 and t == LT - 1:
                        g.wait_ge(E["z_done"], after(l, "z_done", LT))
                        g.dma_start(gm, row(l, 1, 2)).then_inc(E["rows2_ld"], 16)
                        g.dma_start(scf, row(l, 1, 4)).then_inc(E["lgk"], 16)
                        g.dma_start(shf, row(l, 1, 3)).then_inc(E["lgk"], 16)
                    link(g.tensor_tensor(x, x, lng, ALU.mult))
                    link(g.tensor_tensor(x, x, lnb, ALU.add))

            def dispatch(l):
                E = L[l]
                n = TILES[l]
                g.wait_ge(E["dest"], after(l, "dest", 1))
                g.wait_ge(S["tok_zero"], 32)
                for k in range(2 * n):
                    g.indirect_dma_start(out=tokd[l], out_offset=bass.IndirectOffsetOnAxis(ap=addrI[:, k:k + 1], axis=0),
                                         in_=tidI[:, k % n:k % n + 1], in_offset=None).then_inc(E["scat"], 16)
                g.wait_ge(E["scat"], after(l, "scat", 32 * n))
                g.dma_start(slotI, tokd[l].rearrange("(p j) o -> p (j o)", j=28)).then_inc(E["slot_ld"], 16)
                for b in range(2):
                    g.wait_ge(E[f"hf_st{b}"], after(l, f"hf_st{b}", 16 * (n // 2)))
                g.wait_ge(E["slot_ld"], after(l, "slot_ld", 16))

            def gate_weights():
                link(g.memset(wdn, 0.0))
                g.sem_inc(S["wz"], 1)
                for d in range(2):
                    g.dma_start(wdn[:, :, 32 * d:32 * d + RANK], a["gla_wg_down"][0, d].rearrange("(p c) r -> p c r", c=KC)).then_inc(S["gw_ld"], 16)
                    g.dma_start(wup[32 * d:32 * d + RANK, :], a["gla_wg_up"][0, d]).then_inc(S["gw_ld"], 16)
                for d in range(2):
                    g.dma_start(bgc[:, 4 * d:4 * d + 4], a["gla_bg"][0, d].rearrange("(h p) -> p h", p=P), allow_slow_non_contiguous=True).then_inc(S["bg_ld"], 16)
                g.wait_ge(S["bg_ld"], 32)
                g.sem_inc(S["wz"], 1)

            def moe(l):
                E = L[l]
                n = TILES[l]
                g.wait_ge(E["tbl"], 1)
                nb = g.value_load(inclI[0:1, NE - 1:NE], min_val=2, max_val=MAXB[l] + 1)

                def passed():
                    g.sem_inc(S["passed"], 1)

                def gather(j):
                    g.tensor_copy(idxcur, slotI[:, bass.ds(j, 1)]).then_inc(E["idx"], 1)
                    g.wait_ge(E["idx"], j + 1)
                    passed()
                    g.indirect_dma_start(out=xrow, out_offset=None, in_=hfd[l],
                                         in_offset=bass.IndirectOffsetOnAxis(ap=idxcur, axis=0)).then_inc(E["gath"], 16)

                g.tensor_copy(idxcur, slotI[:, 0:1]).then_inc(E["idx"], 1)
                g.wait_ge(E["idx"], 1)
                g.indirect_dma_start(out=xrow, out_offset=None, in_=hfd[l],
                                     in_offset=bass.IndirectOffsetOnAxis(ap=idxcur, axis=0)).then_inc(E["gath"], 16)
                if l == 0:
                    gate_weights()
                with g.Fori(0, MAXB[l]) as j:
                    with g.If(j + 1 < nb):
                        g.wait_ge(E["xt"], j + 1)
                        g.wait_ge(E["gath"], 16 * (j + 1))
                        gather(j + 1)
                g.wait_ge(E["gath"], 16 * nb)
                passed()
                if l == 0:
                    for k in (10, 11):
                        g.wait_ge(ada_st[k % 2], 16 * (k // 2 + 1))
                g.dma_start(gm, row(l, 0, 5)).then_inc(E["rows3_ld"], 16)
                if l == 0:
                    g.dma_start(gmc, row(l, 1, 5)).then_inc(E["rows3_ld"], 16)
                g.dma_start(lng, bcast_row(a["ln_g"][l, 1], D)).then_inc(E["rows3_ld"], 16)
                g.dma_start(lnb, bcast_row(a["ln_b"][l, 1], D)).then_inc(E["rows3_ld"], 16)
                g.wait_ge(E["y_all"], after(l, "y_all", 1))
                def fetch(t):
                    for k in range(2):
                        g.indirect_dma_start(out=yab[l][2 * (t % 3) + k], out_offset=None, in_=ypad[l],
                                             in_offset=bass.IndirectOffsetOnAxis(ap=destI[:, k * n + t:k * n + t + 1], axis=0)
                                             ).then_inc(E[f"ya_ld{t % 3}"], 16)

                fetch(0)
                fetch(1)
                fetch(2)
                for t in range(n):
                    x = X[l][:, t, :]
                    if t + 3 < n:
                        g.wait_ge(E["bn2"], after(l, "bn2", t + 1))
                        fetch(t + 3)
                    g.wait_ge(E["ln2_n"], after(l, "ln2_n", t + 1))
                    if t == 0:
                        g.wait_ge(E["rows3_ld"], after(l, "rows3_ld", 64 if l == 0 else 48))
                    link(g.tensor_tensor(x, x, lng, ALU.mult))
                    g.tensor_tensor(x, x, lnb, ALU.add).then_inc(E["xfin"], 1)
                    g.wait_ge(E["xfin"], after(l, "xfin", t + 1))
                    if l:
                        g.dma_start(out[0][t * P:(t + 1) * P, :], x).then_inc(S["outst"], 16)
                    elif t < LT:
                        g.dma_start(xsave[t * P:(t + 1) * P, :], x).then_inc(S["xsave_st"], 16)

            g.wait_ge(S["o_mm"], 48)
            g.wait_ge(S["o_ev"], 48)
            mixer_rows(0)
            dispatch(0)
            moe(0)
            for n in range(7 * GH):
                h, k = divmod(n, 7)
                l2 = 1 << k
                npair = SEQ // (2 * l2)
                lv, gb = LVB[n % 3], GB[h % 2]
                qq, kk, f, b = (x.rearrange("p (n s l) -> p n s l", s=2, l=l2)
                                for x in (lv[:, 0, :], lv[:, 1, :], gb[:, 0, 0:SEQ], gb[:, 1, 0:SEQ]))
                rf = f[:, :, 0, l2 - 1:l2].to_broadcast([P, npair, l2])
                rbk = b[:, :, 1, 0:1].to_broadcast([P, npair, l2])
                if k == 0:
                    g.wait_ge(S["ls_done"], 3 * h + 2)
                if n >= 3:
                    g.wait_ge(S["lv_mm"], 8 * ((n - 3) // 7) + (n - 3) % 7 + 2)
                g.tensor_tensor(qq[:, :, 1, :], f[:, :, 1, :], rf, ALU.subtract)
                g.tensor_tensor(qq[:, :, 0, :], b[:, :, 0, :], rbk, ALU.subtract)
                g.tensor_tensor(kk[:, :, 0, :], rf, f[:, :, 0, :], ALU.subtract)
                g.tensor_tensor(kk[:, :, 1, :], rbk, b[:, :, 1, :], ALU.subtract).then_inc(S["lv_arg"], 1)
            g.wait_ge(S["gu_mm"], 2 * GH)
            small_rows(1)
            g.wait_ge(S["go_mm"], 16)
            g.wait_ge(S["go_ev"], 16)
            g.wait_ge(S["gss"], 16)
            mixer_rows(1)
            dispatch(1)
            moe(1)
            g.wait_ge(S["outst"], 16 * LT)


_INS = ["x", "c", "ctx", "c_ctx", "ada_w", "ada_b", "ln_g", "ln_b", "attn_w_qkv", "attn_w_o", "attn_lambda", "attn_subln_g",
        "gla_w_in", "gla_wg_down", "gla_wg_up", "gla_bg", "gla_norm_g", "gla_w_o", "router_w", "router_b",
        "moe_w_gate", "moe_w_up", "moe_w_down"]


def kernel(**inputs):
    from concourse import bacc
    from concourse.bass_utils import run_bass_kernel_spmd

    nc = bacc.Bacc("TRN2", target_bir_lowering=False, num_devices=1)
    arrays, aps = {}, {}
    for name in _INS:
        arr = np.ascontiguousarray(inputs[name])
        arrays[f"in_{name}"] = arr
        aps[name] = nc.dram_tensor(f"in_{name}", arr.shape, mybir.dt.from_np(arr.dtype), kind="ExternalInput").ap()
    table = constants()
    arrays["constants"] = table
    const_ap = nc.dram_tensor("constants", table.shape, F32, kind="ExternalInput").ap()
    out = nc.dram_tensor("out", (1, SEQ, D), F32, kind="ExternalOutput").ap()
    build(nc, aps, out, const_ap)
    r = run_bass_kernel_spmd(nc, [arrays], core_ids=[0])
    return r.results[0]["out"]
```
